# Optimizing a Trainium2 kernel written in Bass

```python
import jax, jax.numpy as jnp
from jax import lax
import numpy as np

D_MODEL = 1024
BATCH = 1
SEQ = 1024
DEPTH = 1

CHUNK = 64
Q_BLOCK = 128
EPS = 1e-6
MAX_STREAM_OFFSET = 4096

D_RNN = D_MODEL
LRU_BLOCK_W = 256
LRU_BLOCKS = D_RNN // LRU_BLOCK_W
CONV_W = 4
LRU_C = 8.0

MLA_HEADS = 16
V_HEAD = D_MODEL // MLA_HEADS
QK_NOPE = 64
QK_ROPE = 32
QK_HEAD = QK_NOPE + QK_ROPE
Q_LORA = 768
KV_LORA = 256
ROPE_THETA = 10000.0

N_BRANCH = 2
IN_SPLITS = (D_RNN, D_RNN, Q_LORA, KV_LORA, QK_ROPE, N_BRANCH * D_MODEL)
D_IN = sum(IN_SPLITS)

N_GROUPS = 4
EXPERTS_PER_GROUP = 8
N_EXPERTS = N_GROUPS * EXPERTS_PER_GROUP
TOP_K = 2
D_EXPERT = 256
MOE_BLOCK = 128


def rms_norm(x, g):
    xf = x.astype(jnp.float32)
    y = xf * lax.rsqrt(jnp.mean(xf * xf, axis=-1, keepdims=True) + EPS)
    return (y * g.astype(jnp.float32)).astype(x.dtype)

def causal_conv(x, w, b):
    y = lax.conv_general_dilated(
        x, w[:, None, :].astype(x.dtype), window_strides=(1,),
        padding=[(CONV_W - 1, 0)], dimension_numbers=('NWC', 'WIO', 'NWC'),
        feature_group_count=x.shape[-1])
    return y + b.astype(x.dtype)

def rg_lru(x, wa, ba, wx, bx, lam):
    B, S, _ = x.shape
    xb = x.reshape(B, S, LRU_BLOCKS, LRU_BLOCK_W)
    r = jax.nn.sigmoid((jnp.einsum('bshi,hij->bshj', xb, wa).reshape(B, S, D_RNN) + ba).astype(jnp.float32))
    i = jax.nn.sigmoid((jnp.einsum('bshi,hij->bshj', xb, wx).reshape(B, S, D_RNN) + bx).astype(jnp.float32))
    log_a = -LRU_C * r * jax.nn.softplus(-lam.astype(jnp.float32))
    a = jnp.exp(log_a)
    mult = jnp.sqrt(-jnp.expm1(2.0 * log_a))
    b = mult * (i * x.astype(jnp.float32))

    def combine(left, right):
        a_l, b_l = left
        a_r, b_r = right
        return a_l * a_r, a_r * b_l + b_r

    _, h = lax.associative_scan(combine, (a, b), axis=1)
    return h.astype(x.dtype)

def rope(x, pos):
    half = QK_ROPE // 2
    freq = ROPE_THETA ** (-jnp.arange(half, dtype=jnp.float32) / half)
    ang = pos.astype(jnp.float32)[:, :, None, None] * freq
    cos, sin = jnp.cos(ang), jnp.sin(ang)
    x1 = x[..., :half].astype(jnp.float32)
    x2 = x[..., half:].astype(jnp.float32)
    return jnp.concatenate([x1 * cos - x2 * sin, x1 * sin + x2 * cos], axis=-1).astype(x.dtype)

def chunk_causal_attention(q, k, v):
    B, S, H, _ = q.shape
    scale = QK_HEAD ** -0.5
    outs = []
    for blk in range(S // Q_BLOCK):
        q0 = blk * Q_BLOCK
        k_end = q0 + Q_BLOCK
        qb = q[:, q0:k_end]
        s = jnp.einsum('bqhd,bkhd->bhqk', qb, k[:, :k_end]).astype(jnp.float32) * scale
        q_chunk = (q0 + jnp.arange(Q_BLOCK)) // CHUNK
        k_chunk = jnp.arange(k_end) // CHUNK
        mask = k_chunk[None, :] <= q_chunk[:, None]
        s = jnp.where(mask, s, -jnp.inf)
        p = jax.nn.softmax(s, axis=-1).astype(v.dtype)
        outs.append(jnp.einsum('bhqk,bkhd->bqhd', p, v[:, :k_end]))
    return jnp.concatenate(outs, axis=1).reshape(B, S, H * V_HEAD)

def mla(q_c, kv_c, k_pe, pos, q_a_g, w_uq, kv_a_g, w_ukv, q_norm_g, k_norm_g):
    B, S, _ = q_c.shape
    q = (rms_norm(q_c, q_a_g) @ w_uq).reshape(B, S, MLA_HEADS, QK_HEAD)
    kv = (rms_norm(kv_c, kv_a_g) @ w_ukv).reshape(B, S, MLA_HEADS, QK_NOPE + V_HEAD)
    k_nope, v = kv[..., :QK_NOPE], kv[..., QK_NOPE:]
    k_pe_h = jnp.broadcast_to(k_pe[:, :, None, :], (B, S, MLA_HEADS, QK_ROPE))
    k = jnp.concatenate([k_nope, k_pe_h], axis=-1)
    q = rms_norm(q, q_norm_g)
    k = rms_norm(k, k_norm_g)
    q = jnp.concatenate([q[..., :QK_NOPE], rope(q[..., QK_NOPE:], pos)], axis=-1)
    k = jnp.concatenate([k[..., :QK_NOPE], rope(k[..., QK_NOPE:], pos)], axis=-1)
    return chunk_causal_attention(q, k, v)

def hier_moe(x, wg, bg, we, be, w_gate, w_up, w_down):
    B, S, D = x.shape
    T = B * S
    xt = x.reshape(T, D)
    xf = xt.astype(jnp.float32)
    g_logits = xf @ wg.astype(jnp.float32) + bg.astype(jnp.float32)
    g_prob = jax.nn.softmax(g_logits, axis=-1)
    grp = jnp.argmax(g_logits, axis=-1)
    p_grp = jnp.take_along_axis(g_prob, grp[:, None], axis=1)
    e_logits = (xf @ we.astype(jnp.float32) + be.astype(jnp.float32)).reshape(T, N_GROUPS, EXPERTS_PER_GROUP)
    e_in = jnp.take_along_axis(e_logits, grp[:, None, None], axis=1)[:, 0]
    top_v, top_i = lax.top_k(e_in, TOP_K)
    combine = p_grp * jax.nn.softmax(top_v, axis=-1)
    expert = grp[:, None] * EXPERTS_PER_GROUP + top_i

    A = T * TOP_K
    e_flat = expert.reshape(A)
    tok_flat = jnp.arange(A, dtype=jnp.int32) // TOP_K
    c_flat = combine.reshape(A)
    order = jnp.argsort(e_flat)
    e_sorted = e_flat[order]
    counts = jnp.bincount(e_flat, length=N_EXPERTS)
    padded = (counts + MOE_BLOCK - 1) // MOE_BLOCK * MOE_BLOCK
    starts = jnp.cumsum(counts) - counts
    p_ends = jnp.cumsum(padded)
    p_starts = p_ends - padded
    dest = p_starts[e_sorted] + (jnp.arange(A) - starts[e_sorted])
    P = A + N_EXPERTS * MOE_BLOCK
    n_blk = P // MOE_BLOCK
    tok_pad = jnp.full((P,), T, jnp.int32).at[dest].set(tok_flat[order])
    c_pad = jnp.zeros((P,), jnp.float32).at[dest].set(c_flat[order])
    blk_expert = jnp.clip(jnp.searchsorted(p_ends, jnp.arange(n_blk) * MOE_BLOCK, side='right'), 0, N_EXPERTS - 1)
    x_pad = jnp.concatenate([xt, jnp.zeros((1, D), xt.dtype)], axis=0)[tok_pad].reshape(n_blk, MOE_BLOCK, D)

    def expert_block(args):
        xb, e = args
        hb = jax.nn.silu(xb @ w_gate[e]) * (xb @ w_up[e])
        return hb @ w_down[e]

    y = lax.map(expert_block, (x_pad, blk_expert)).reshape(P, D).astype(jnp.float32) * c_pad[:, None]
    out = jax.ops.segment_sum(y, tok_pad, num_segments=T + 1)[:T]
    return out.astype(x.dtype).reshape(B, S, D)

def first_inputs(seed: int = 0) -> dict:
    key = jax.random.key(seed)
    ks = jax.random.split(key, 28)
    L = DEPTH

    def nrm(k, shape, s):
        return jax.random.normal(k, shape, jnp.float32) * s

    def gain(k, n):
        return 1.0 + 0.05 * jax.random.normal(k, (L, n), jnp.float32)

    x = jax.random.normal(ks[0], (BATCH, SEQ, D_MODEL), jnp.float32)
    offset = jax.random.randint(ks[1], (BATCH, 1), 0, MAX_STREAM_OFFSET, dtype=jnp.int32)
    positions = offset + jnp.arange(SEQ, dtype=jnp.int32)[None, :]
    a0 = jax.random.uniform(ks[2], (L, D_RNN), jnp.float32, 0.9, 0.999)
    s0 = a0 ** (1.0 / LRU_C)
    lru_lambda = jnp.log(s0) - jnp.log1p(-s0)
    return {
        "x": x,
        "positions": positions,
        "norm_mix_g": gain(ks[3], D_MODEL),
        "w_in": nrm(ks[4], (L, D_MODEL, D_IN), D_MODEL ** -0.5),
        "conv_w": nrm(ks[5], (L, CONV_W, D_RNN), CONV_W ** -0.5),
        "conv_b": nrm(ks[6], (L, D_RNN), 0.02),
        "lru_wa": nrm(ks[7], (L, LRU_BLOCKS, LRU_BLOCK_W, LRU_BLOCK_W), LRU_BLOCK_W ** -0.5),
        "lru_ba": nrm(ks[8], (L, D_RNN), 0.02),
        "lru_wx": nrm(ks[9], (L, LRU_BLOCKS, LRU_BLOCK_W, LRU_BLOCK_W), LRU_BLOCK_W ** -0.5),
        "lru_bx": nrm(ks[10], (L, D_RNN), 0.02),
        "lru_lambda": lru_lambda,
        "q_a_g": gain(ks[11], Q_LORA),
        "w_uq": nrm(ks[12], (L, Q_LORA, MLA_HEADS * QK_HEAD), Q_LORA ** -0.5),
        "kv_a_g": gain(ks[13], KV_LORA),
        "w_ukv": nrm(ks[14], (L, KV_LORA, MLA_HEADS * (QK_NOPE + V_HEAD)), KV_LORA ** -0.5),
        "q_norm_g": gain(ks[15], QK_HEAD),
        "k_norm_g": gain(ks[16], QK_HEAD),
        "w_out": nrm(ks[17], (L, D_MODEL, D_MODEL), D_MODEL ** -0.5),
        "norm_ffn_g": gain(ks[18], D_MODEL),
        "router_group_w": nrm(ks[19], (L, D_MODEL, N_GROUPS), D_MODEL ** -0.5),
        "router_group_b": nrm(ks[20], (L, N_GROUPS), 0.01),
        "router_expert_w": nrm(ks[21], (L, D_MODEL, N_EXPERTS), D_MODEL ** -0.5),
        "router_expert_b": nrm(ks[22], (L, N_EXPERTS), 0.01),
        "w_gate": nrm(ks[23], (L, N_EXPERTS, D_MODEL, D_EXPERT), D_MODEL ** -0.5),
        "w_up": nrm(ks[24], (L, N_EXPERTS, D_MODEL, D_EXPERT), D_MODEL ** -0.5),
        "w_down": nrm(ks[25], (L, N_EXPERTS, D_EXPERT, D_MODEL), D_EXPERT ** -0.5),
    }

def first_block(x, positions, norm_mix_g, w_in, conv_w, conv_b, lru_wa, lru_ba, lru_wx, lru_bx,
              lru_lambda, q_a_g, w_uq, kv_a_g, w_ukv, q_norm_g, k_norm_g, w_out, norm_ffn_g,
              router_group_w, router_group_b, router_expert_w, router_expert_b,
              w_gate, w_up, w_down):
    B, S, _ = x.shape
    split_points = np.cumsum(IN_SPLITS)[:-1].tolist()
    h = x
    for l in range(DEPTH):
        u = rms_norm(h, norm_mix_g[l])
        proj = u @ w_in[l]
        x_rnn, g_rnn, q_c, kv_c, k_pe, gate_logits = jnp.split(proj, split_points, axis=-1)
        xa = causal_conv(x_rnn, conv_w[l], conv_b[l])
        ya = rg_lru(xa, lru_wa[l], lru_ba[l], lru_wx[l], lru_bx[l], lru_lambda[l]) * jax.nn.gelu(g_rnn)
        yb = mla(q_c, kv_c, k_pe, positions, q_a_g[l], w_uq[l], kv_a_g[l], w_ukv[l], q_norm_g[l], k_norm_g[l])
        gates = jax.nn.sigmoid(gate_logits.astype(jnp.float32)).reshape(B, S, N_BRANCH, D_MODEL)
        merged = gates[:, :, 0] * ya.astype(jnp.float32) + gates[:, :, 1] * yb.astype(jnp.float32)
        h = h + merged.astype(h.dtype) @ w_out[l]
        h = h + hier_moe(rms_norm(h, norm_ffn_g[l]), router_group_w[l], router_group_b[l],
                         router_expert_w[l], router_expert_b[l], w_gate[l], w_up[l], w_down[l])
    return h


D_MIX = D_MODEL
HG_WIDTH = D_MIX // 2
HG_HEADS = 4
HG_DK = HG_WIDTH // HG_HEADS
HG_DV = HG_WIDTH // HG_HEADS
HG_CHUNK = 64
POOL_WIDTH = D_MIX - HG_WIDTH
POOL_WINDOWS = (2, 4, 8, 16)
POOL_GROUPS = len(POOL_WINDOWS)
POOL_CG = POOL_WIDTH // POOL_GROUPS
IN_COLS = 4 * HG_WIDTH + POOL_WIDTH
N_EXPERTS_2 = 64
TOP_K_2 = 8
N_GROUP = 8
TOPK_GROUP = 4
ROUTED_SCALE = 2.5
LN_EPS = 1e-5
RMS_EPS = 1e-6
DEEPNORM_ALPHA = (2 * DEPTH) ** 0.25
DEEPNORM_BETA = (8 * DEPTH) ** -0.25


def layer_norm(x, g, b):
    xf = x.astype(jnp.float32)
    mu = xf.mean(-1, keepdims=True)
    var = jnp.square(xf - mu).mean(-1, keepdims=True)
    return ((xf - mu) * lax.rsqrt(var + LN_EPS) * g + b).astype(x.dtype)

def hgrn2_chunked(q, k, v, logf):
    B, S, H, DK = q.shape
    DV = v.shape[-1]
    NC = S // HG_CHUNK

    def to_chunks(t):
        return t.reshape(B, NC, HG_CHUNK, H, t.shape[-1]).transpose(1, 0, 3, 2, 4)

    qc, kc, vc, fc = (to_chunks(t) for t in (q, k, v, logf))
    causal = jnp.tril(jnp.ones((HG_CHUNK, HG_CHUNK), dtype=bool))[:, :, None]

    def step(state, inp):
        qb, kb, vb, fb = inp
        b = jnp.cumsum(fb, axis=2)
        o_inter = jnp.einsum('bhtk,bhkv->bhtv', qb * jnp.exp(b), state)
        diff = b[:, :, :, None, :] - b[:, :, None, :, :]
        decay = jnp.where(causal, jnp.exp(jnp.minimum(diff, 0.0)), 0.0)
        scores = jnp.einsum('bhtk,bhsk,bhtsk->bhts', qb, kb, decay)
        o_intra = jnp.einsum('bhts,bhsv->bhtv', scores, vb)
        b_last = b[:, :, -1:, :]
        k_dec = kb * jnp.exp(b_last - b)
        new_state = jnp.exp(b_last[:, :, 0, :])[..., None] * state + jnp.einsum('bhsk,bhsv->bhkv', k_dec, vb)
        return new_state, o_inter + o_intra

    s0 = jnp.zeros((B, H, DK, DV), jnp.float32)
    _, oc = lax.scan(step, s0, (qc, kc, vc, fc))
    return oc.transpose(1, 0, 3, 2, 4).reshape(B, S, H, DV)

def multiscale_pool(u, w_pool, pool_scale):
    B, S = u.shape[0], u.shape[1]
    uf = u.astype(jnp.float32)
    c = jnp.cumsum(uf, axis=1)
    pos = jnp.arange(1, S + 1, dtype=jnp.float32)
    outs = []
    for gi, w in enumerate(POOL_WINDOWS):
        cg = c[:, :, gi]
        prev = jnp.pad(cg, ((0, 0), (w, 0), (0, 0)))[:, :S]
        cnt = jnp.minimum(pos, float(w))[None, :, None]
        outs.append((cg - prev) / cnt - uf[:, :, gi])
    p = jnp.stack(outs, axis=2)
    p = jnp.einsum('bsgc,gcd->bsgd', p, w_pool.astype(jnp.float32))
    return (p.reshape(B, S, -1) * pool_scale).astype(u.dtype)

def hybrid_mixer(h, lb, w_in, hg_norm_g, w_pool, pool_scale, w_out):
    B, S, _ = h.shape
    proj = h @ w_in
    q, f_pre, i_v, g_out, u = jnp.split(proj, [HG_WIDTH, 2 * HG_WIDTH, 3 * HG_WIDTH, 4 * HG_WIDTH], axis=-1)
    f = lb + (1.0 - lb) * jax.nn.sigmoid(f_pre.astype(jnp.float32))
    k = 1.0 - f
    logf = jnp.log(f)
    qh = jax.nn.silu(q.astype(jnp.float32))
    shp = (B, S, HG_HEADS, HG_DK)
    o = hgrn2_chunked(qh.reshape(shp), k.reshape(shp), i_v.astype(jnp.float32).reshape(B, S, HG_HEADS, HG_DV), logf.reshape(shp))
    o = o * lax.rsqrt(jnp.mean(jnp.square(o), axis=-1, keepdims=True) + RMS_EPS)
    o = o.reshape(B, S, HG_WIDTH) * hg_norm_g * jax.nn.silu(g_out.astype(jnp.float32))
    p = multiscale_pool(u.reshape(B, S, POOL_GROUPS, POOL_CG), w_pool, pool_scale)
    mix = jnp.concatenate([o.astype(h.dtype), p], axis=-1)
    return mix @ w_out

def moe_ffn(h, w_router, router_bias, w_gate, w_up, w_down, ws_gate, ws_up, ws_down):
    B, S, D = h.shape
    T = B * S
    A = T * TOP_K_2
    NB = -(-(A + N_EXPERTS_2 * (MOE_BLOCK - 1)) // MOE_BLOCK)
    xt = h.reshape(T, D)
    scores = jax.nn.sigmoid((xt @ w_router).astype(jnp.float32))
    sel = scores + router_bias.astype(jnp.float32)
    grp = sel.reshape(T, N_GROUP, N_EXPERTS_2 // N_GROUP)
    grp_score = lax.top_k(grp, 2)[0].sum(-1)
    _, gidx = lax.top_k(grp_score, TOPK_GROUP)
    gmask = jax.nn.one_hot(gidx, N_GROUP, dtype=jnp.int32).sum(1) > 0
    emask = jnp.repeat(gmask, N_EXPERTS_2 // N_GROUP, axis=1)
    _, eidx = lax.top_k(jnp.where(emask, sel, -jnp.inf), TOP_K_2)
    wts = jnp.take_along_axis(scores, eidx, axis=-1)
    wts = wts / wts.sum(-1, keepdims=True) * ROUTED_SCALE
    flat_e = eidx.reshape(A).astype(jnp.int32)
    flat_tok = jnp.repeat(jnp.arange(T, dtype=jnp.int32), TOP_K_2)
    flat_w = wts.reshape(A)
    order = jnp.argsort(flat_e, stable=True)
    se, stok, sw = flat_e[order], flat_tok[order], flat_w[order]
    counts = jnp.bincount(flat_e, length=N_EXPERTS_2)
    padded = ((counts + MOE_BLOCK - 1) // MOE_BLOCK) * MOE_BLOCK
    start = jnp.cumsum(counts) - counts
    pend = jnp.cumsum(padded)
    pstart = pend - padded
    dest = pstart[se] + (jnp.arange(A, dtype=jnp.int32) - start[se])
    tok_of_slot = jnp.full((NB * MOE_BLOCK,), T, dtype=jnp.int32).at[dest].set(stok)
    xpad = jnp.concatenate([xt, jnp.zeros((1, D), xt.dtype)], axis=0)
    xin = xpad[tok_of_slot].reshape(NB, MOE_BLOCK, D)
    blk_e = jnp.clip(jnp.searchsorted(pend, jnp.arange(NB) * MOE_BLOCK, side='right'), 0, N_EXPERTS_2 - 1)

    def block_ffn(args):
        xb, e = args
        return (jax.nn.silu(xb @ w_gate[e]) * (xb @ w_up[e])) @ w_down[e]

    yb = lax.map(block_ffn, (xin, blk_e)).reshape(NB * MOE_BLOCK, D)
    y_assign = yb[dest] * sw[:, None].astype(yb.dtype)
    routed = jax.ops.segment_sum(y_assign, stok, num_segments=T)
    shared = (jax.nn.silu(xt @ ws_gate) * (xt @ ws_up)) @ ws_down
    return (routed + shared).reshape(B, S, D)

def second_inputs(seed: int = 0) -> dict:
    key = jax.random.key(seed)
    ks = jax.random.split(key, 20)
    n = jax.random.normal
    f32 = jnp.float32
    col_scale = jnp.concatenate([
        jnp.ones((2 * HG_WIDTH,), f32), jnp.full((HG_WIDTH,), DEEPNORM_BETA, f32),
        jnp.ones((HG_WIDTH,), f32), jnp.full((POOL_WIDTH,), DEEPNORM_BETA, f32)])
    return {
        "x": n(ks[0], (BATCH, SEQ, D_MODEL), f32),
        "w_in": n(ks[1], (DEPTH, D_MODEL, IN_COLS), f32) * D_MODEL ** -0.5 * col_scale,
        "hg_lb_logits": n(ks[2], (DEPTH + 1, HG_WIDTH), f32) * 0.5,
        "hg_norm_g": 1.0 + 0.02 * n(ks[3], (DEPTH, HG_WIDTH), f32),
        "w_pool": n(ks[4], (DEPTH, POOL_GROUPS, POOL_CG, POOL_CG), f32) * POOL_CG ** -0.5 * DEEPNORM_BETA,
        "pool_scale": 1.0 + 0.02 * n(ks[5], (DEPTH, POOL_WIDTH), f32),
        "w_out": n(ks[6], (DEPTH, D_MIX, D_MODEL), f32) * D_MIX ** -0.5 * DEEPNORM_BETA,
        "ln1_g": 1.0 + 0.02 * n(ks[7], (DEPTH, D_MODEL), f32),
        "ln1_b": 0.02 * n(ks[8], (DEPTH, D_MODEL), f32),
        "w_router": n(ks[9], (DEPTH, D_MODEL, N_EXPERTS_2), f32) * D_MODEL ** -0.5,
        "router_bias": 0.01 * n(ks[10], (DEPTH, N_EXPERTS_2), f32),
        "w_gate": n(ks[11], (DEPTH, N_EXPERTS_2, D_MODEL, D_EXPERT), f32) * D_MODEL ** -0.5 * DEEPNORM_BETA,
        "w_up": n(ks[12], (DEPTH, N_EXPERTS_2, D_MODEL, D_EXPERT), f32) * D_MODEL ** -0.5 * DEEPNORM_BETA,
        "w_down": n(ks[13], (DEPTH, N_EXPERTS_2, D_EXPERT, D_MODEL), f32) * D_EXPERT ** -0.5 * DEEPNORM_BETA,
        "ws_gate": n(ks[14], (DEPTH, D_MODEL, D_EXPERT), f32) * D_MODEL ** -0.5 * DEEPNORM_BETA,
        "ws_up": n(ks[15], (DEPTH, D_MODEL, D_EXPERT), f32) * D_MODEL ** -0.5 * DEEPNORM_BETA,
        "ws_down": n(ks[16], (DEPTH, D_EXPERT, D_MODEL), f32) * D_EXPERT ** -0.5 * DEEPNORM_BETA,
        "ln2_g": 1.0 + 0.02 * n(ks[17], (DEPTH, D_MODEL), f32),
        "ln2_b": 0.02 * n(ks[18], (DEPTH, D_MODEL), f32),
    }

def second_block(x, w_in, hg_lb_logits, hg_norm_g, w_pool, pool_scale, w_out, ln1_g, ln1_b,
              w_router, router_bias, w_gate, w_up, w_down, ws_gate, ws_up, ws_down, ln2_g, ln2_b):
    lower_bounds = jnp.cumsum(jax.nn.softmax(hg_lb_logits.astype(jnp.float32), axis=0), axis=0)
    h = x
    for layer in range(DEPTH):
        mix = hybrid_mixer(h, lower_bounds[layer], w_in[layer], hg_norm_g[layer], w_pool[layer],
                           pool_scale[layer], w_out[layer])
        h = layer_norm(DEEPNORM_ALPHA * h + mix, ln1_g[layer], ln1_b[layer])
        ffn = moe_ffn(h, w_router[layer], router_bias[layer], w_gate[layer], w_up[layer], w_down[layer],
                      ws_gate[layer], ws_up[layer], ws_down[layer])
        h = layer_norm(DEEPNORM_ALPHA * h + ffn, ln2_g[layer], ln2_b[layer])
    return h


_first_inputs = second_inputs


def second_inputs(seed=0):
    import zlib

    import numpy as np

    out = dict(_first_inputs(seed))
    spreads = {}
    factors = {'hg_lb_logits': 3.67,
     'hg_norm_g': 7.754,
     'pool_scale': 8.0,
     'ln2_g': 2.875,
     'ln2_b': 2.903}
    for name, (base, spread) in spreads.items():
        noise = np.random.default_rng([zlib.crc32(name.encode()), seed]).standard_normal(out[name].shape)
        drawn = base * np.exp(spread * noise) if base else spread * noise
        out[name] = __import__('jax').numpy.asarray(drawn.astype(out[name].dtype))
    for name, factor in factors.items():
        out[name] = (out[name] * factor).astype(out[name].dtype)
    return out


_narrow_inputs = second_inputs


def second_inputs(seed=0):

    out = dict(_narrow_inputs(seed))
    wider = {'hg_norm_g': 3.4, 'pool_scale': 5.06, 'ln2_g': 3.23, 'ln2_b': 3.23}
    for name, times in wider.items():
        mean = out[name].mean()
        out[name] = (mean + times * (out[name] - mean)).astype(out[name].dtype)
    return out


def setup_inputs(seed=0):
    out = dict(first_inputs(seed))
    for name, value in second_inputs(seed + 1).items():
        if name != "x":
            out[name + "_2"] = value
    return out


def reference(
    x, positions, norm_mix_g, w_in, conv_w, conv_b, lru_wa, lru_ba, lru_wx, lru_bx, lru_lambda,
    q_a_g, w_uq, kv_a_g, w_ukv, q_norm_g, k_norm_g, w_out, norm_ffn_g, router_group_w,
    router_group_b, router_expert_w, router_expert_b, w_gate, w_up, w_down, w_in_2,
    hg_lb_logits_2, hg_norm_g_2, w_pool_2, pool_scale_2, w_out_2, ln1_g_2, ln1_b_2, w_router_2,
    router_bias_2, w_gate_2, w_up_2, w_down_2, ws_gate_2, ws_up_2, ws_down_2, ln2_g_2, ln2_b_2,
):
    x = first_block(
        x, positions, norm_mix_g, w_in, conv_w, conv_b, lru_wa, lru_ba, lru_wx, lru_bx,
        lru_lambda, q_a_g, w_uq, kv_a_g, w_ukv, q_norm_g, k_norm_g, w_out, norm_ffn_g,
        router_group_w, router_group_b, router_expert_w, router_expert_b, w_gate, w_up, w_down,
    )
    return second_block(
        x, w_in_2, hg_lb_logits_2, hg_norm_g_2, w_pool_2, pool_scale_2, w_out_2, ln1_g_2,
        ln1_b_2, w_router_2, router_bias_2, w_gate_2, w_up_2, w_down_2, ws_gate_2, ws_up_2,
        ws_down_2, ln2_g_2, ln2_b_2,
    )


_drawn_inputs = setup_inputs


def setup_inputs(seed=0):
    import zlib

    import numpy as np

    out = dict(_drawn_inputs(seed))
    spreads = {}
    factors = {'lru_ba': 8.0,
     'lru_bx': 5.554,
     'q_a_g': 3.809,
     'q_norm_g': 7.464,
     'k_norm_g': 3.047,
     'router_group_b': 4.269,
     'router_expert_b': 3.017,
     'router_bias_2': 2.818}
    for name, (base, spread) in spreads.items():
        noise = np.random.default_rng([zlib.crc32(name.encode()), seed]).standard_normal(out[name].shape)
        drawn = base * np.exp(spread * noise) if base else spread * noise
        out[name] = __import__('jax').numpy.asarray(drawn.astype(out[name].dtype))
    for name, factor in factors.items():
        out[name] = (out[name] * factor).astype(out[name].dtype)
    return out
```

```python
from contextlib import ExitStack

import numpy as np

import concourse.bass as bass
from concourse import mybir

F32 = mybir.dt.float32
I32 = mybir.dt.int32
U32 = mybir.dt.uint32
ALU = mybir.AluOpType
ACT = mybir.ActivationFunctionType
AX = mybir.AxisListType.X

P = 128
S = 1024
D = 1024
T = S // P
C = D // P
BANK = 512
HALF = S // BANK
EPS = 1e-6
LN_EPS = 1e-5
NEG = -1.0e30

LRU_W = 256
HEADS, NOPE, ROPE, VH = 16, 64, 32, 64
QK = NOPE + ROPE
Q_LORA, KV_LORA = 768, 256
ROPE_THETA = 10000.0
E1, GROUPS1, K1 = 32, 4, 2
E2, GROUPS2, K2, TOPG2 = 64, 8, 8, 4
F_EXP = 256
NB1 = (S * K1 + E1 * (P - 1)) // P
NB2 = (S * K2 + E2 * (P - 1)) // P
HG_HEADS = 4
HG_W = 512
POOL_W = 512
ALPHA = 2.0 ** 0.25
ROUTED_SCALE = 2.5


class Names:
    pass


def start_at_one(eng, *sems):
    for sem in sems:
        eng.sem_inc(sem, 1)


class Steps:

    def __init__(self, eng, sem, base=0):
        self.eng, self.sem, self.base, self.n = eng, sem, base, 0

    def __call__(self, ins):
        ins.then_inc(self.sem, 1)
        self.n += 1
        return self.n

    def join(self, n=None):
        self.eng.wait_ge(self.sem, self.base + (self.n if n is None else n))


def phase(nc):
    ctx = ExitStack()
    ns = Names()
    ns.ctx = ctx
    allocated = []

    def sems(names):
        allocated.extend(nc.alloc_semaphore(f"{name}_{n}") for name in names.split())
        return allocated[-len(names.split()):]

    def clear():
        nc.clear_and_free_semaphores(allocated)
        nc.all_engine_barrier()

    ctx.callback(clear)
    ns.sems = sems
    ns.n = n = nc.next_id()
    ns.sb = lambda name, shape, dt=F32: ctx.enter_context(nc.sbuf_tensor(f"{name}_{n}", shape, dt))
    ns.ps = lambda name, shape: ctx.enter_context(nc.psum_tensor(f"{name}_{n}", shape, F32))
    return ns


VECTORS = ("norm_mix_g:8 conv_w:32 conv_b:8 lru_ba:8 lru_bx:8 lru_lambda:8 q_a_g:6 kv_a_g:2 "
           "norm_ffn_g:8 hg_lb_logits_2:8 pool_scale_2:4")
VROW = {}
for _item in VECTORS.split():
    _name, _rows = _item.split(":")
    VROW[_name] = (sum(n for _, n in VROW.values()), int(_rows))
VROWS = sum(n for _, n in VROW.values())


def setup(nc, A, G):
    ph = phase(nc)
    with ph.ctx:
        vrow = ph.sb("vrow", [VROWS, P])
        posi = ph.sb("posi", [P, T], I32)
        posf = ph.sb("posf", [P, T])
        freq = ph.sb("freq", [P, ROPE // 2])
        ang = ph.sb("ang", [P, T, ROPE // 2])
        red = ph.sb("red", [P, T, ROPE // 2])
        turns = ph.sb("turns", [P, T, ROPE // 2])
        t1 = ph.sb("t1", [P, C])
        t2 = ph.sb("t2", [P, C])
        t3 = ph.sb("t3", [P, C])
        t4 = ph.sb("t4", [P, C])
        vps = ph.ps("vps", [P, P])
        (loaded, zeroed, made, vec_t, vec_ready, dve, act) = ph.sems(
            "loaded zeroed made vec_t vec_ready dve act")
        block = ph.ctx.enter_context(nc.Block())

        rowvecs = [(G.qg, A["q_norm_g"]), (G.kg, A["k_norm_g"])]
        N_LOADS = 1 + len(VROW) + 1 + len(rowvecs)

        @block.sync
        def _(sp):
            sp.dma_start(G.h[:], A["x"].rearrange("b (t p) d -> p (b t) d", p=P)).then_inc(loaded, 16)
            for name, (first, n) in VROW.items():
                src = A[name]
                if name == "conv_w":
                    src = src.rearrange("l w (c p) -> (l w c) p", p=P)
                else:
                    src = src.rearrange("l (c p) -> (l c) p", p=P)
                sp.dma_start(vrow[first:first + n, :], src).then_inc(loaded, 16)
            with nc.allow_non_contiguous_dma("1024 positions, once"):
                sp.dma_start(posi[:], A["positions"].rearrange("b (t p) -> p (b t)", p=P)).then_inc(loaded, 16)
            for dst, src in rowvecs:
                sp.dma_start(dst[:], src.to_broadcast([P, src.shape[1]])).then_inc(loaded, 16)

        @block.gpsimd
        def _(pool):
            g = nc.gpsimd
            st = Steps(pool, zeroed)
            st(g.memset(G.ident[:], 0.0))
            st(g.memset(G.ones[:], 1.0))
            st(g.memset(G.tri[:], 1.0))
            st.join()
            g.affine_select(out=G.ident[:], in_=G.ident[:], compare_op=ALU.not_equal, fill=1.0,
                            base=0, pattern=[[-1, P]], channel_multiplier=1).then_inc(made, 1)
            g.affine_select(out=G.tri[:], in_=G.tri[:], compare_op=ALU.is_gt, fill=0.0,
                            base=0, pattern=[[1, P]], channel_multiplier=-1).then_inc(made, 1)
            g.iota(G.iota[:], [[1, P]], base=0, channel_multiplier=0,
                   allow_small_or_imprecise_dtypes=True).then_inc(made, 1)
            g.iota(G.tok[:], [[P, T]], base=0, channel_multiplier=1,
                   allow_small_or_imprecise_dtypes=True).then_inc(made, 1)
            pool.wait_ge(made, 4)

        @block.tensor
        def _(pe):
            pe.wait_ge(loaded, 16 * N_LOADS)
            pe.wait_ge(made, 4)
            nc.tensor.transpose(vps[:, 0:VROWS], vrow[:], G.ident[0:VROWS, 0:VROWS]).then_inc(vec_t, 1)

        @block.vector
        def _(v):
            d = nc.vector
            st = Steps(v, dve)
            for i in range(ROPE // 2):
                st(d.memset(freq[:, i:i + 1], float(np.float32(ROPE_THETA ** (-i / (ROPE // 2))))))
            v.wait_ge(loaded, 16 * N_LOADS)
            st(d.tensor_scalar(G.qg[:], G.qg[:], -float(QK) ** -0.5, None, ALU.mult))
            st(d.tensor_copy(posf[:], posi[:]))
            st.join()
            st(d.tensor_tensor(ang[:], posf[:, :, None].to_broadcast([P, T, ROPE // 2]),
                               freq[:, None, :].to_broadcast([P, T, ROPE // 2]), ALU.mult))
            st.join()
            MAGIC = 1.5 * 2.0 ** 23
            PI2 = 2.0 * np.pi
            A1 = 6.28125
            A2 = float(np.float32(np.round((PI2 - A1) * 2.0 ** 22) / 2.0 ** 22))
            A3 = float(np.float32(PI2 - A1 - A2))
            for out, quarter in ((G.sin, 0.0), (G.cos, 0.25)):
                st(d.tensor_scalar(turns[:], ang[:], float(np.float32(1.0 / PI2)), quarter, ALU.mult, ALU.add))
                st.join()
                st(d.tensor_scalar(turns[:], turns[:], MAGIC, None, ALU.add))
                st.join()
                st(d.tensor_scalar(turns[:], turns[:], MAGIC, None, ALU.subtract))
                st.join()
                st(d.scalar_tensor_tensor(out=red[:], in0=turns[:], scalar=-A1, in1=ang[:],
                                          op0=ALU.mult, op1=ALU.add))
                st.join()
                st(d.scalar_tensor_tensor(out=red[:], in0=turns[:], scalar=-A2, in1=red[:],
                                          op0=ALU.mult, op1=ALU.add))
                st.join()
                st(d.scalar_tensor_tensor(out=red[:], in0=turns[:], scalar=-A3, in1=red[:],
                                          op0=ALU.mult, op1=ALU.add))
                st.join()
                st(d.tensor_scalar(red[:], red[:], quarter * PI2, 3.1415925, ALU.add, ALU.min))
                st.join()
                st(d.tensor_scalar(out[:], red[:], -3.1415925, None, ALU.max))
                st.join()
            v.wait_ge(vec_t, 1)
            d.tensor_copy(G.vec[:], vps[:, 0:VROWS]).then_inc(vec_ready, 1)
            v.wait_ge(act, 3)
            y, z, z2, acc = t1, t2, t3, t4
            st(d.tensor_scalar(z[:], y[:], 2.0, None, ALU.add))
            st.join()
            st(d.reciprocal(z[:], z[:]))
            st.join()
            st(d.tensor_tensor(z[:], z[:], y[:], ALU.mult))
            st.join()
            st(d.tensor_tensor(z2[:], z[:], z[:], ALU.mult))
            st(d.memset(acc[:], 1.0 / 17.0))
            st.join()
            for k in range(15, 0, -2):
                st(d.tensor_tensor(acc[:], acc[:], z2[:], ALU.mult))
                st.join()
                st(d.tensor_scalar(acc[:], acc[:], 1.0 / k, None, ALU.add))
                st.join()
            st(d.tensor_tensor(acc[:], acc[:], z[:], ALU.mult))
            first, n = VROW["lru_lambda"]
            st(d.tensor_scalar(z2[:], G.vec[:, first:first + n], -1.0, 0.0, ALU.mult, ALU.max))
            st.join()
            st(d.scalar_tensor_tensor(out=acc[:], in0=acc[:], scalar=2.0, in1=z2[:], op0=ALU.mult, op1=ALU.add))
            st.join()
            st(d.tensor_scalar(G.decay[:], acc[:], -8.0, None, ALU.mult))

        @block.scalar
        def _(a):
            a.wait_ge(vec_ready, 1)
            first, n = VROW["lru_lambda"]
            nc.scalar.activation(t1[:], G.vec[:, first:first + n], ACT.Abs).then_inc(act, 1)
            a.wait_ge(act, 1)
            nc.scalar.activation(t1[:], t1[:], ACT.Exp, scale=-1.0).then_inc(act, 1)
            nc.scalar.activation(G.sin[:], G.sin[:], ACT.Sin)
            nc.scalar.activation(G.cos[:], G.cos[:], ACT.Sin).then_inc(act, 1)


def vec(G, name):
    first, n = VROW[name]
    return G.vec[:, first:first + n]


def rms_to_cols(nc, G, gain, dst):
    ph = phase(nc)
    with ph.ctx:
        junk = ph.sb("junk", [P, D])
        ssq = ph.sb("ssq", [P, T])
        rstd = ph.sb("rstd", [P, T])
        xn = ph.sb("xn", [P, 2, D])
        tp = ph.ps("tp", [P, 2, C, P])
        squared, rooted, scaled, turned, taken, dve = ph.sems("squared rooted scaled turned taken dve")
        block = ph.ctx.enter_context(nc.Block())

        @block.scalar
        def _(a):
            for t in range(T):
                if t:
                    a.wait_ge(squared, t)
                nc.scalar.activation(junk[:], G.h[:, t, :], ACT.Square,
                                     accum_out=ssq[:, t:t + 1]).then_inc(squared, 1)
            a.wait_ge(dve, 1)
            nc.scalar.activation(rstd[:], ssq[:], ACT.Sqrt).then_inc(rooted, 1)
            a.wait_ge(dve, 2)
            for t in range(T):
                if t >= 2:
                    a.wait_ge(turned, t - 1)
                nc.scalar.activation(xn[:, t % 2, :], G.h[:, t, :], ACT.Copy,
                                     scale=rstd[:, t:t + 1]).then_inc(scaled, 1)

        @block.tensor
        def _(pe):
            for t in range(T):
                pe.wait_ge(scaled, t + 1)
                if t >= 2:
                    pe.wait_ge(taken, t - 1)
                for c in range(C):
                    last = nc.tensor.transpose(tp[:, t % 2, c, :], xn[:, t % 2, c * P:(c + 1) * P], G.ident[:])
                last.then_inc(turned, 1)

        @block.vector
        def _(v):
            d = nc.vector
            v.wait_ge(squared, T)
            d.tensor_scalar(ssq[:], ssq[:], 1.0 / D, EPS, ALU.mult, ALU.add).then_inc(dve, 1)
            v.wait_ge(rooted, 1)
            d.reciprocal(rstd[:], rstd[:]).then_inc(dve, 1)
            for t in range(T):
                v.wait_ge(turned, t + 1)
                d.tensor_tensor(dst[:, :, t * P:(t + 1) * P], tp[:, t % 2, :, :],
                                gain[:, :, None].to_broadcast([P, C, P]), ALU.mult).then_inc(taken, 1)


def lru(nc, A, G, y_d):
    ph = phase(nc)
    B = LRU_W // P
    NBLK = D // LRU_W
    CONV = 4
    w_in = A["w_in"].rearrange("l (c p) n -> p (l c) n", p=P)
    wa_d = A["lru_wa"].rearrange("l b (c p) n -> (l b) p c n", p=P)
    wx_d = A["lru_wx"].rearrange("l b (c p) n -> (l b) p c n", p=P)
    with ph.ctx:
        wcol = ph.sb("wcol", [P, 3, C, LRU_W])
        wgate = ph.sb("wgate", [P, 2, B, LRU_W])
        xp = ph.sb("xp", [P, B, CONV - 1 + S])
        xa = ph.sb("xa", [P, B, S])
        rr = ph.sb("rr", [P, B, S])
        aa = ph.sb("aa", [P, B, S])
        pp = ph.sb("pp", [P, B, S])
        ii = ph.sb("ii", [P, B, S])
        hh = ph.sb("hh", [P, B, S])
        gelu = ph.sb("gelu", [P, B, S])
        gate = ph.sb("gate", [P, B, S])
        zero = ph.sb("zero", [P, D])
        ps = ph.ps("ps", [P, 2, B, S])
        (w0, w1, w2, wg_in, group_ready, group_taken, pad_ready, xa_ready, log_ready, p_ready,
         q_ready, root_ready, dve, act, block_done, cleared, zero_out) = ph.sems(
            "w0 w1 w2 wg_in group_ready group_taken pad_ready xa_ready log_ready p_ready "
            "q_ready root_ready dve act block_done cleared zero_out")
        w_in_sem = [w0, w1, w2]
        COL = [0, D, 2 * D + Q_LORA + KV_LORA + ROPE]
        GROUPS = 5
        block = ph.ctx.enter_context(nc.Block())

        @block.sync
        def _(sp):
            for k in range(3):
                sp.dma_start(wcol[:, k], w_in[:, :, COL[k]:COL[k] + LRU_W]).then_inc(w_in_sem[k], 16)
            sp.dma_start(wgate[:, 0], wa_d[0]).then_inc(wg_in, 16)
            sp.dma_start(wgate[:, 1], wx_d[0]).then_inc(wg_in, 16)
            with sp.Fori(0, NBLK - 1) as b:
                for k in range(3):
                    sp.wait_ge(group_ready, b * GROUPS + k + 1)
                    sp.dma_start(wcol[:, k], w_in[:, :, bass.ds((b + 1) * LRU_W + COL[k], LRU_W)]).then_inc(w_in_sem[k], 16)
                sp.wait_ge(group_ready, b * GROUPS + GROUPS)
                for k, src in enumerate((wa_d, wx_d)):
                    sp.dma_start(wgate[:, k], src[bass.ds(b + 1, 1)].rearrange("o p c n -> p (o c) n")).then_inc(wg_in, 16)

        @block.gpsimd
        def _(pool):
            nc.gpsimd.memset(zero[:], 0.0).then_inc(cleared, 1)
            pool.wait_ge(cleared, 1)
            spans = ((S * K1 // P, NB1), (S * K2 // P, NB2))
            for b0, b1 in spans:
                with pool.Fori(b0, b1) as b:
                    pool.dma_start(y_d[bass.ds(b * P, P), :], zero[:]).then_inc(zero_out, 16)
            pool.wait_ge(zero_out, 16 * sum(b1 - b0 for b0, b1 in spans))

        @block.tensor
        def _(pe):
            def in_group(b, m, k):
                slot = m % 2
                pe.wait_ge(w_in_sem[k], b * 16 + 16)
                for c in range(B):
                    for h in range(HALF):
                        for kc in range(C):
                            last = nc.tensor.matmul(ps[:, slot, c, h * BANK:(h + 1) * BANK],
                                                    wcol[:, k, kc, c * P:(c + 1) * P],
                                                    G.u[:, kc, h * BANK:(h + 1) * BANK],
                                                    start=kc == 0, stop=kc == C - 1)
                last.then_inc(group_ready, 1)

            def gate_group(b, m, k):
                slot = m % 2
                if k == 0:
                    pe.wait_ge(wg_in, b * 32 + 32)
                    pe.wait_ge(xa_ready, b + 1)
                for c in range(B):
                    for h in range(HALF):
                        for kc in range(B):
                            last = nc.tensor.matmul(ps[:, slot, c, h * BANK:(h + 1) * BANK],
                                                    wgate[:, k, kc, c * P:(c + 1) * P],
                                                    xa[:, kc, h * BANK:(h + 1) * BANK],
                                                    start=kc == 0, stop=kc == B - 1)
                last.then_inc(group_ready, 1)

            with pe.Fori(0, NBLK // 2) as j:
                for u in range(2):
                    b = j * 2 + u
                    for k in range(GROUPS):
                        m = u * GROUPS + k
                        pe.wait_ge(group_taken, 1 + j * (2 * GROUPS) + max(m - 1, 0))
                        if k < 3:
                            in_group(b, m, k)
                        else:
                            gate_group(b, m, k - 3)

        @block.scalar
        def _(a):
            s = nc.scalar
            start_at_one(a, group_taken)
            with a.Fori(0, NBLK // 2) as j:
                for u in range(2):
                    b = j * 2 + u
                    st = Steps(a, act, b * 3)
                    m = u * GROUPS
                    first = j * (2 * GROUPS) + m
                    a.wait_ge(group_ready, first + 1)
                    a.wait_ge(pad_ready, b + 1)
                    s.activation(xp[:, :, CONV - 1:], ps[:, m % 2], ACT.Copy).then_inc(group_taken, 1)
                    a.wait_ge(group_ready, first + 2)
                    a.wait_ge(block_done, 1 + b)
                    s.activation(gelu[:], ps[:, (m + 1) % 2], ACT.Gelu_apprx_tanh).then_inc(group_taken, 1)
                    a.wait_ge(group_ready, first + 3)
                    s.activation(gate[:], ps[:, (m + 2) % 2], ACT.Sigmoid).then_inc(group_taken, 1)
                    for k, (out, bias) in enumerate(((rr, vec(G, "lru_ba")), (ii, vec(G, "lru_bx")))):
                        a.wait_ge(group_ready, first + 4 + k)
                        for c in range(B):
                            last = s.activation(out[:, c, :], ps[:, (m + 3 + k) % 2, c, :], ACT.Sigmoid,
                                                bias=bias[:, bass.ds(b * B + c, 1)])
                            if c == B - 1:
                                last.then_inc(group_taken, 1)
                            else:
                                last.then_inc(act, 1)
                    a.wait_ge(log_ready, b + 1)
                    s.activation(pp[:], rr[:], ACT.Tanh, scale=-1.0).then_inc(p_ready, 1)
                    s.activation(aa[:], rr[:], ACT.Exp).then_inc(act, 1)
                    a.wait_ge(q_ready, b + 1)
                    s.activation(pp[:], pp[:], ACT.Sqrt).then_inc(root_ready, 1)

        @block.vector
        def _(v):
            d = nc.vector
            start_at_one(v, block_done)
            d.memset(xp[:, :, 0:CONV - 1], 0.0).then_inc(pad_ready, 1)
            N_STEPS = B * CONV - 1 + 1 + 1 + 2 + B + 1
            with v.Fori(0, NBLK) as b:
                st = Steps(v, dve, b * N_STEPS)
                v.wait_ge(group_taken, 1 + b * GROUPS + 1)
                v.wait_ge(pad_ready, b + 1)
                for k in range(CONV):
                    for c in range(B):
                        wk = vec(G, "conv_w")[:, bass.ds(b * B + (k * C + c), 1)]
                        if k == 0:
                            ins = d.tensor_scalar(xa[:, c, :], xp[:, c, 0:S], wk,
                                                  vec(G, "conv_b")[:, bass.ds(b * B + c, 1)], ALU.mult, ALU.add)
                        else:
                            st.join(st.n - 1)
                            ins = d.scalar_tensor_tensor(out=xa[:, c, :], in0=xp[:, c, k:k + S], scalar=wk,
                                                         in1=xa[:, c, :], op0=ALU.mult, op1=ALU.add)
                        if k == CONV - 1 and c == B - 1:
                            ins.then_inc(xa_ready, 1)
                        else:
                            st(ins)
                v.wait_ge(xa_ready, b + 1)
                d.memset(xp[:, :, 0:CONV - 1], 0.0).then_inc(pad_ready, 1)
                v.wait_ge(group_taken, 1 + b * GROUPS + 4)
                v.wait_ge(act, b * 3 + 1)
                st(d.tensor_scalar(rr[:, 0, :], rr[:, 0, :], G.decay[:, bass.ds(b * B, 1)], None, ALU.mult))
                d.tensor_scalar(rr[:, 1, :], rr[:, 1, :], G.decay[:, bass.ds(b * B + 1, 1)], None,
                                ALU.mult).then_inc(log_ready, 1)
                v.wait_ge(act, b * 3 + 3)
                st(d.tensor_tensor(hh[:], aa[:], aa[:], ALU.mult))
                st.join()
                v.wait_ge(p_ready, b + 1)
                d.scalar_tensor_tensor(out=pp[:], in0=hh[:], scalar=1.0, in1=pp[:], op0=ALU.add,
                                       op1=ALU.mult).then_inc(q_ready, 1)
                v.wait_ge(group_taken, 1 + b * GROUPS + 5)
                st(d.tensor_tensor(ii[:], ii[:], xa[:], ALU.mult))
                st.join()
                v.wait_ge(root_ready, b + 1)
                st(d.tensor_tensor(ii[:], ii[:], pp[:], ALU.mult))
                st.join()
                for c in range(B):
                    st(d.tensor_tensor_scan(hh[:, c, :], aa[:, c, :], ii[:, c, :], 0.0, ALU.mult, ALU.add))
                st.join()
                st(d.tensor_tensor(hh[:], hh[:], gelu[:], ALU.mult))
                st.join()
                d.tensor_tensor(G.ya[:, bass.ds(b * B, B), :], hh[:], gate[:], ALU.mult).then_inc(block_done, 1)
                assert st.n == N_STEPS, st.n


def persistent(nc, ctx):
    G = Names()
    sb = lambda name, shape, dt=F32: ctx.enter_context(nc.sbuf_tensor(name, shape, dt))
    G.h = sb("h", [P, T, D])
    G.vec = sb("vec", [P, VROWS])
    G.ident = sb("ident", [P, P])
    G.ones = sb("ones", [P, P])
    G.tri = sb("tri", [P, P])
    G.iota = sb("iota", [P, P])
    G.tok = sb("tok", [P, T])
    G.qg = sb("qg", [P, QK])
    G.kg = sb("kg", [P, QK])
    G.sin = sb("sin", [P, T, ROPE // 2])
    G.cos = sb("cos", [P, T, ROPE // 2])
    G.decay = sb("decay", [P, C])
    return G


def mla_project(nc, A, G, qk_d, v_d):
    ph = phase(nc)
    QC = Q_LORA // P
    KC = KV_LORA // P
    IN_W = Q_LORA + KV_LORA + ROPE
    HALF_Q = Q_LORA // 2
    KV_W = KV_LORA + ROPE
    H2 = ROPE // 2
    GROUP_HEADS = BANK // (NOPE + VH)
    NQ, NKV = HEADS * QK // BANK, HEADS * (NOPE + VH) // BANK
    TURN = 4
    with ph.ctx:
        w_low = ph.sb("w_low", [P, C, IN_W])
        w_uq = ph.sb("w_uq", [P, QC, HEADS * QK])
        w_ukv = ph.sb("w_ukv", [P, KC, HEADS * (NOPE + VH)])
        low = ph.sb("low", [P, Q_LORA + KV_LORA])
        kpe = ph.sb("kpe", [P, 2, ROPE])
        low_t = ph.sb("low_t", [P, QC + KC, P])
        gains = ph.sb("gains", [P, QC + KC])
        qk = ph.sb("qk", [P, 2, HEADS, QK])
        sq = ph.sb("sq", [P, 2, HEADS, QK])
        vv = ph.sb("vv", [P, HEADS, VH])
        stage = ph.sb("stage", [QK, 2, 2 * TURN, P])
        ss = ph.sb("ss", [P, 2])
        hs = ph.sb("hs", [P, 2, HEADS])
        qk_flat = qk[:].rearrange("p s h d -> p (s h d)")
        sq_low = ph.sb("sq_low", [P, Q_LORA + KV_LORA])
        rot = [sq[:].rearrange("p s h d -> p (s h d)")[:, i * 2 * HEADS * H2:(i + 1) * 2 * HEADS * H2]
               .rearrange("p (n d) -> p n d", d=H2) for i in range(4)]
        acc = ph.ps("acc", [P, 4, BANK])
        tr = ph.ps("tr", [P, QC + KC, P])
        ht = ph.ps("ht", [P, 2, TURN, P])
        (w_in0, w_in1, w_in2, acc_ready, acc_taken, row_sq, row_ms, row_rt, row_ok, tr_ready,
         tr_taken, qk_sq, qk_ms, qk_rt, qk_ok, ht_ready, ht_taken, v_out, st_out0,
         st_out1, dve, act) = ph.sems(
            "w_in0 w_in1 w_in2 acc_ready acc_taken row_sq row_ms row_rt row_ok tr_ready tr_taken "
            "qk_sq qk_ms qk_rt qk_ok ht_ready ht_taken v_out st_out0 st_out1 dve act")
        st_out = [st_out0, st_out1]
        block = ph.ctx.enter_context(nc.Block())
        PER = 3 + NQ + NKV
        TURNS = 2 * HEADS // TURN

        order = [("low", 0, k) for k in range(3)]
        for t in range(T):
            if t + 1 < T:
                order += [("low", t + 1, k) for k in range(3)]
            order += [("up", t, k) for k in range(NQ + NKV)]
        number = {key: n for n, key in enumerate(order)}

        @block.sync
        def _(sp):
            w = A["w_in"].rearrange("l (c p) n -> p (l c) n", p=P)
            sp.dma_start(w_low[:], w[:, :, 2 * D:2 * D + IN_W]).then_inc(w_in0, 16)
            sp.dma_start(w_uq[:], A["w_uq"].rearrange("l (c p) n -> p (l c) n", p=P)).then_inc(w_in1, 16)
            sp.dma_start(w_ukv[:], A["w_ukv"].rearrange("l (c p) n -> p (l c) n", p=P)).then_inc(w_in2, 16)
            for t in range(T):
                sp.wait_ge(acc_taken, number["up", t, NQ + NKV - 1] + 1)
                sp.dma_start(v_d[t * P:(t + 1) * P, :], vv[:].rearrange("p h d -> p (h d)")).then_inc(v_out, 16)
                for n in range(TURNS // 2):
                    sp.wait_ge(ht_taken, t * TURNS + 2 * n + 2)
                    s, first = divmod(n * 2 * TURN, HEADS)
                    sp.dma_start(qk_d[s, first:first + 2 * TURN, :, t * P:(t + 1) * P].rearrange("h p t -> p h t"),
                                 stage[:, n % 2]).then_inc(st_out[n % 2], 16)
            sp.wait_ge(v_out, 16 * T)
            for q in st_out:
                sp.wait_ge(q, 16 * T * TURNS // 4)

        @block.tensor
        def _(pe):
            def low_groups(t):
                if t == 0:
                    pe.wait_ge(w_in0, 16)
                for k in range(3):
                    n = number["low", t, k]
                    if n >= 4:
                        pe.wait_ge(acc_taken, n - 3)
                    c0 = k * HALF_Q
                    width = HALF_Q if k < 2 else KV_W
                    for kc in range(C):
                        last = nc.tensor.matmul(acc[:, n % 4, 0:width], G.u[:, kc, t * P:(t + 1) * P],
                                                w_low[:, kc, c0:c0 + width], start=kc == 0, stop=kc == C - 1)
                    last.then_inc(acc_ready, 1)

            def turn_low(t):
                pe.wait_ge(row_ok, t + 1)
                if t:
                    pe.wait_ge(tr_taken, t)
                for c in range(QC + KC):
                    last = nc.tensor.transpose(tr[:, c, :], low[:, c * P:(c + 1) * P], G.ident[:])
                last.then_inc(tr_ready, 1)

            def up_groups(t):
                if t == 0:
                    pe.wait_ge(w_in1, 16)
                    pe.wait_ge(w_in2, 16)
                pe.wait_ge(tr_taken, t + 1)
                for k in range(NQ + NKV):
                    n = number["up", t, k]
                    pe.wait_ge(acc_taken, n - 3)
                    chunks = range(QC) if k < NQ else range(QC, QC + KC)
                    for kc in chunks:
                        rhs = (w_uq[:, kc, k * BANK:(k + 1) * BANK] if k < NQ else
                               w_ukv[:, kc - QC, (k - NQ) * BANK:(k - NQ + 1) * BANK])
                        last = nc.tensor.matmul(acc[:, n % 4, :], low_t[:, kc, :], rhs,
                                                start=kc == chunks[0], stop=kc == chunks[-1])
                    last.then_inc(acc_ready, 1)

            def turn_heads(t):
                pe.wait_ge(qk_ok, t + 1)
                for n in range(TURNS):
                    m = t * TURNS + n
                    if m >= 2:
                        pe.wait_ge(ht_taken, m - 1)
                    for i in range(TURN):
                        s, head = divmod(n * TURN + i, HEADS)
                        last = nc.tensor.transpose(ht[0:QK, n % 2, i, :], qk[:, s, head, :], G.ident[:])
                    last.then_inc(ht_ready, 1)

            low_groups(0)
            for t in range(T):
                turn_low(t)
                if t + 1 < T:
                    low_groups(t + 1)
                if t:
                    turn_heads(t - 1)
                up_groups(t)
            turn_heads(T - 1)

        @block.scalar
        def _(a):
            s = nc.scalar
            st = Steps(a, act)

            def take_low(t):
                if t:
                    a.wait_ge(tr_ready, t)
                for k in range(3):
                    n = number["low", t, k]
                    a.wait_ge(acc_ready, n + 1)
                    c0 = k * HALF_Q
                    if k == 2:
                        if t >= 2:
                            a.wait_ge(qk_sq, t - 1)
                        st(s.activation(kpe[:, t % 2, :], acc[:, n % 4, KV_LORA:KV_W], ACT.Copy))
                    width = HALF_Q if k < 2 else KV_LORA
                    s.activation(low[:, c0:c0 + width], acc[:, n % 4, 0:width], ACT.Copy).then_inc(acc_taken, 1)
                a.wait_ge(acc_taken, number["low", t, 2] + 1)
                st(s.activation(sq_low[:, 0:Q_LORA], low[:, 0:Q_LORA], ACT.Square, accum_out=ss[:, 0:1]))
                s.activation(sq_low[:, Q_LORA:], low[:, Q_LORA:], ACT.Square,
                             accum_out=ss[:, 1:2]).then_inc(row_sq, 1)
                a.wait_ge(row_ms, t + 1)
                s.activation(ss[:], ss[:], ACT.Sqrt).then_inc(row_rt, 1)

            def take_up(t):
                if t:
                    a.wait_ge(ht_ready, t * TURNS)
                    a.wait_ge(v_out, 16 * t)
                for k in range(NQ + NKV):
                    n = number["up", t, k]
                    a.wait_ge(acc_ready, n + 1)
                    if k < NQ:
                        s.activation(qk_flat[:, k * BANK:(k + 1) * BANK], acc[:, n % 4, :],
                                     ACT.Copy).then_inc(acc_taken, 1)
                        continue
                    head = (k - NQ) * GROUP_HEADS
                    src = acc[:, n % 4, :].rearrange("p (h d) -> p h d", d=NOPE + VH)
                    st(s.activation(qk[:, 1, head:head + GROUP_HEADS, 0:NOPE], src[:, :, 0:NOPE], ACT.Copy))
                    s.activation(vv[:, head:head + GROUP_HEADS, :], src[:, :, NOPE:],
                                 ACT.Copy).then_inc(acc_taken, 1)
                st(s.activation(qk[:, 1, :, NOPE:], kpe[:, t % 2, None, :].to_broadcast([P, HEADS, ROPE]), ACT.Copy))
                a.wait_ge(acc_taken, number["up", t, NQ + NKV - 1] + 1)
                st.join()
                s.activation(sq[:], qk[:], ACT.Square).then_inc(qk_sq, 1)

            def take_heads(t):
                for n in range(TURNS):
                    m = t * TURNS + n
                    a.wait_ge(ht_ready, m + 1)
                    d = (m // 2)
                    if n % 2 == 0 and d >= 2:
                        a.wait_ge(st_out[(n // 2) % 2], 16 * (d // 2))
                    s.activation(stage[:, (n // 2) % 2, (n % 2) * TURN:(n % 2 + 1) * TURN, :],
                                 ht[0:QK, n % 2], ACT.Copy).then_inc(ht_taken, 1)

            def root_heads(t):
                a.wait_ge(qk_ms, t + 1)
                s.activation(hs[:], hs[:], ACT.Sqrt).then_inc(qk_rt, 1)

            take_low(0)
            for t in range(T):
                if t:
                    root_heads(t - 1)
                if t + 1 < T:
                    take_low(t + 1)
                if t:
                    take_heads(t - 1)
                take_up(t)
            root_heads(T - 1)
            take_heads(T - 1)

        @block.vector
        def _(v):
            d = nc.vector
            st = Steps(v, dve)
            st(d.tensor_copy(gains[:, 0:QC], vec(G, "q_a_g")))
            st(d.tensor_copy(gains[:, QC:], vec(G, "kv_a_g")))
            st.join()

            def scale_rows(t):
                v.wait_ge(row_sq, t + 1)
                st(d.tensor_scalar(ss[:, 0:1], ss[:, 0:1], 1.0 / Q_LORA, EPS, ALU.mult, ALU.add))
                d.tensor_scalar(ss[:, 1:2], ss[:, 1:2], 1.0 / KV_LORA, EPS, ALU.mult, ALU.add).then_inc(row_ms, 1)
                v.wait_ge(row_rt, t + 1)
                st(d.reciprocal(ss[:], ss[:]))
                st.join()
                st(d.tensor_scalar(low[:, 0:Q_LORA], low[:, 0:Q_LORA], ss[:, 0:1], None, ALU.mult))
                d.tensor_scalar(low[:, Q_LORA:], low[:, Q_LORA:], ss[:, 1:2], None, ALU.mult).then_inc(row_ok, 1)

            def take_turned(t):
                v.wait_ge(tr_ready, t + 1)
                if t:
                    v.wait_ge(acc_ready, number["up", t - 1, NQ + NKV - 1] + 1)
                d.tensor_tensor(low_t[:], tr[:], gains[:, :, None].to_broadcast([P, QC + KC, P]),
                                ALU.mult).then_inc(tr_taken, 1)

            def norm_heads(t):
                v.wait_ge(qk_sq, t + 1)
                st(d.tensor_reduce(hs[:], sq[:], AX, ALU.add))
                st.join()
                d.tensor_scalar(hs[:], hs[:], 1.0 / QK, EPS, ALU.mult, ALU.add).then_inc(qk_ms, 1)
                v.wait_ge(qk_rt, t + 1)
                st(d.reciprocal(hs[:], hs[:]))
                st.join()
                st(d.tensor_tensor(qk[:], qk[:], hs[:, :, :, None].to_broadcast([P, 2, HEADS, QK]), ALU.mult))
                st.join()
                for s, g in ((0, G.qg), (1, G.kg)):
                    st(d.tensor_tensor(qk[:, s], qk[:, s], g[:, None, :].to_broadcast([P, HEADS, QK]), ALU.mult))
                st.join()
                both = "p s h d -> p (s h) d"
                x1 = qk[:, :, :, NOPE:NOPE + H2].rearrange(both)
                x2 = qk[:, :, :, NOPE + H2:].rearrange(both)
                cos = G.cos[:, t, None, :].to_broadcast([P, 2 * HEADS, H2])
                sin = G.sin[:, t, None, :].to_broadcast([P, 2 * HEADS, H2])
                st(d.tensor_tensor(rot[0], x1, cos, ALU.mult))
                st(d.tensor_tensor(rot[1], x2, sin, ALU.mult))
                st(d.tensor_tensor(rot[2], x1, sin, ALU.mult))
                st(d.tensor_tensor(rot[3], x2, cos, ALU.mult))
                st.join()
                st(d.tensor_tensor(x1, rot[0], rot[1], ALU.subtract))
                d.tensor_tensor(x2, rot[2], rot[3], ALU.add).then_inc(qk_ok, 1)

            scale_rows(0)
            for t in range(T):
                take_turned(t)
                if t:
                    norm_heads(t - 1)
                if t + 1 < T:
                    scale_rows(t + 1)
            norm_heads(T - 1)


def attention(nc, A, G, qk_d, v_d):
    ph = phase(nc)
    ROUND = 4
    ROUNDS = HEADS // ROUND
    CHUNK = 64
    ORDER = [7, 0, 6, 1, 5, 2, 4, 3]
    N = ROUND * T
    turns = []
    for i in range(N):
        turns.append(("probs", i))
        if i >= 2 * T and (i - 1) % (2 * T) == 0:
            turns.append(("out", (i - 1) // (2 * T) - 1))
    turns.append(("out", ROUND // 2 - 1))
    a_turns = [x for x in turns if x[0] == "out" or x[1] % 2 == 0]
    a_no = {x: n for n, x in enumerate(a_turns)}
    b_no = {x: n for n, x in enumerate(turns)}
    A_ALL, B_ALL = len(a_turns), len(turns)
    with ph.ctx:
        qk = ph.sb("qk", [QK, 2, 2, S])
        vv = ph.sb("vv", [P, 2, T, VH])
        prob = ph.sb("prob", [P, 2, S])
        prob_t = ph.sb("prob_t", [P, 2, T, P])
        o_rows = ph.sb("o_rows", [P, T, 2 * VH])
        shift = ph.sb("shift", [P, 4])
        total = ph.sb("total", [P, 16])
        inv = ph.sb("inv", [P, T])
        early = ph.sb("early", [1, P])
        hide = ph.sb("hide", [1, CHUNK])
        wide = ph.ps("wide", [P, 2, S])
        narrow = ph.ps("narrow", [P, BANK])
        turn_a = ph.ps("turn_a", [P, 4, P])
        turn_b = ph.ps("turn_b", [P, 4, P])
        o_ps = ph.ps("o_ps", [P, T, VH])
        (qk_in0, qk_in1, v_in0, v_in1, sc_ready, max_ready, exp_done, a_ready, a_taken, b_ready,
         b_taken, o_ready, o_taken, inv_ready, cleared) = ph.sems(
            "qk_in0 qk_in1 v_in0 v_in1 sc_ready max_ready exp_done a_ready a_taken b_ready b_taken "
            "o_ready o_taken inv_ready cleared")
        qk_in, v_in = [qk_in0, qk_in1], [v_in0, v_in1]
        block = ph.ctx.enter_context(nc.Block())
        v_rows = v_d.rearrange("(t p) (h d) -> h p t d", p=P, d=VH)
        qk_h = qk_d.rearrange("s h p t -> h p s t")

        def scores_of(s):
            n = (ORDER[s % T] + 1) * P
            return wide[:, s // 2 % 2, 0:n] if s % 2 == 0 else narrow[:, 0:n]

        def total_of(s):
            c = s // T % 2 * T + ORDER[s % T]
            return total[:, c:c + 1]

        @block.sync
        def _(sp):
            def load(head, u):
                sp.dma_start(qk[:, u], qk_h[bass.ds(head, 1)].rearrange("o p s t -> p (o s) t")).then_inc(qk_in[u], 16)

            def load_values(head, u):
                sp.dma_start(vv[:, u], v_rows[bass.ds(head, 1)].rearrange("o p t d -> p (o t) d")).then_inc(v_in[u], 16)

            def reload(j, u):
                sp.wait_ge(sc_ready, j * N + (u + 1) * T)
                load(j * ROUND + (u + 2), u % 2)
                sp.wait_ge(o_ready, j * N + (u + 1) * T)
                load_values(j * ROUND + (u + 2), u % 2)

            for u in range(2):
                load(u, u)
                load_values(u, u)
            with sp.Fori(0, ROUNDS - 1) as j:
                for u in range(ROUND):
                    reload(j, u)
            for u in range(ROUND - 2):
                reload(ROUNDS - 1, u)

        @block.gpsimd
        def _(pool):
            nc.gpsimd.memset(early[:, 0:CHUNK], 1.0).then_inc(cleared, 1)
            nc.gpsimd.memset(early[:, CHUNK:], 0.0).then_inc(cleared, 1)
            nc.gpsimd.memset(hide[:], -NEG).then_inc(cleared, 1)

        @block.tensor
        def _(pe):
            pe.wait_ge(cleared, 3)
            with pe.Fori(0, ROUNDS) as j:
                def scores(s):
                    u, t = s // T, ORDER[s % T]
                    if s % T == 0:
                        pe.wait_ge(qk_in[u % 2], j * (ROUND // 2 * 16) + (u // 2 * 16 + 16))
                    out, n = scores_of(s), (t + 1) * P
                    for c0 in range(0, n, BANK):
                        w = min(BANK, n - c0)
                        nc.tensor.matmul(out[:, c0:c0 + w], qk[:, u % 2, 0, t * P:(t + 1) * P],
                                         qk[:, u % 2, 1, c0:c0 + w], start=True, stop=c0 + w < n)
                    nc.tensor.matmul(out[:, n - CHUNK:n], early[:], hide[:], start=False, stop=True
                                     ).then_inc(sc_ready, 1)

                def turn_probs(s):
                    t, what = ORDER[s % T], ("probs", s)
                    pe.wait_ge(exp_done, j * N + (s + 1))
                    blocks = [prob[:, s % 2, b * P:(b + 1) * P] for b in range(t + 1)]
                    if s % 2 == 0:
                        pe.wait_ge(a_taken, 1 + j * A_ALL + a_no[what])
                        for b in range(4):
                            last = nc.tensor.transpose(turn_a[:, b, :], blocks[b], G.ident[:])
                        last.then_inc(a_ready, 1)
                        blocks = blocks[4:]
                    pe.wait_ge(b_taken, 1 + j * B_ALL + b_no[what])
                    for b, src in enumerate(blocks):
                        last = nc.tensor.transpose(turn_b[:, b, :], src, G.ident[:])
                    last.then_inc(b_ready, 1)

                def values(s):
                    u, t, what = s // T, ORDER[s % T], ("probs", s)
                    if s % T == 0:
                        pe.wait_ge(v_in[u % 2], j * (ROUND // 2 * 16) + (u // 2 * 16 + 16))
                    if s % T == 0:
                        pe.wait_ge(o_taken, 1 + j * ROUND + u)
                    if s % 2 == 0:
                        pe.wait_ge(a_taken, 1 + j * A_ALL + (a_no[what] + 1))
                    pe.wait_ge(b_taken, 1 + j * B_ALL + (b_no[what] + 1))
                    for b in range(t + 1):
                        last = nc.tensor.matmul(o_ps[:, t, :], prob_t[:, s % 2, b, :],
                                                vv[:, u % 2, b, :], start=b == 0, stop=b == t)
                    last.then_inc(o_ready, 1)

                def turn_out(p):
                    what = ("out", p)
                    pe.wait_ge(o_taken, 1 + j * ROUND + (p + 1) * 2)
                    pe.wait_ge(a_taken, 1 + j * A_ALL + a_no[what])
                    for b in range(4):
                        last = nc.tensor.transpose(turn_a[:, b, :], o_rows[:, b, :], G.ident[:])
                    last.then_inc(a_ready, 1)
                    pe.wait_ge(b_taken, 1 + j * B_ALL + b_no[what])
                    for b in range(4):
                        last = nc.tensor.transpose(turn_b[:, b, :], o_rows[:, 4 + b, :], G.ident[:])
                    last.then_inc(b_ready, 1)

                scores(0)
                scores(1)
                for i in range(N):
                    turn_probs(i)
                    if i + 2 < N:
                        scores(i + 2)
                    if i:
                        values(i - 1)
                    for kind, p in turns[b_no["probs", i] + 1:][:1]:
                        if kind == "out" and i + 1 < N:
                            turn_out(p)
                values(N - 1)
                turn_out(ROUND // 2 - 1)

        @block.scalar
        def _(a):
            start_at_one(a, a_taken)
            with a.Fori(0, ROUNDS) as j:
                def exps(s):
                    n = (ORDER[s % T] + 1) * P
                    a.wait_ge(max_ready, j * N + (s + 1))
                    nc.scalar.activation(prob[:, s % 2, 0:n], scores_of(s), ACT.Exp, bias=shift[:, s % 4:s % 4 + 1],
                                         scale=-1.0, accum_out=total_of(s)).then_inc(exp_done, 1)

                exps(0)
                exps(1)
                for kind, n in turns:
                    if (kind, n) in a_no:
                        a.wait_ge(a_ready, j * A_ALL + (a_no[kind, n] + 1))
                    if kind == "out":
                        nc.scalar.activation(
                            G.yb[:, bass.ds(j * (ROUND // 2) + n, 1), 0:4 * P].rearrange("p o (b t) -> p (o b) t", t=P),
                            turn_a[:], ACT.Copy).then_inc(a_taken, 1)
                        continue
                    if n % 2 == 0:
                        if n >= 2:
                            a.wait_ge(o_ready, j * N + (n - 1))
                        nc.scalar.activation(prob_t[:, n % 2, 0:4, :], turn_a[:], ACT.Copy).then_inc(a_taken, 1)
                    if n + 2 < N:
                        a.wait_ge(b_ready, j * B_ALL + (b_no[kind, n] + 1))
                        exps(n + 2)

        @block.vector
        def _(v):
            d = nc.vector
            start_at_one(v, b_taken, o_taken)
            with v.Fori(0, ROUNDS) as j:
                def tops(s):
                    v.wait_ge(sc_ready, j * N + (s + 1))
                    d.tensor_reduce(shift[:, s % 4:s % 4 + 1], scores_of(s), AX, ALU.min).then_inc(max_ready, 1)

                def scale_out(u):
                    v.wait_ge(o_ready, j * N + (u + 1) * T)
                    d.reciprocal(inv[:], total[:, u % 2 * T:(u % 2 + 1) * T]).then_inc(inv_ready, 1)
                    v.wait_ge(inv_ready, j * ROUND + (u + 1))
                    d.tensor_tensor(o_rows[:, :, u % 2 * VH:(u % 2 + 1) * VH], o_ps[:],
                                    inv[:, :, None].to_broadcast([P, T, VH]), ALU.mult).then_inc(o_taken, 1)

                tops(0)
                tops(1)
                for kind, n in turns[:-1]:
                    if kind == "probs" and n > T and n % T == 1:
                        scale_out(n // T - 1)
                    v.wait_ge(b_ready, j * B_ALL + (b_no[kind, n] + 1))
                    if kind == "out":
                        d.tensor_copy(G.yb[:, bass.ds(j * (ROUND // 2) + n, 1), 4 * P:]
                                      .rearrange("p o (b t) -> p (o b) t", t=P), turn_b[:]).then_inc(b_taken, 1)
                        continue
                    t = ORDER[n % T]
                    if n >= 2:
                        v.wait_ge(o_ready, j * N + (n - 1))
                    if n % 2 == 0:
                        d.tensor_copy(prob_t[:, n % 2, 4:t + 1, :], turn_b[:, 0:t - 3, :]).then_inc(b_taken, 1)
                    else:
                        d.tensor_copy(prob_t[:, n % 2, 0:t + 1, :], turn_b[:, 0:t + 1, :]).then_inc(b_taken, 1)
                    if n + 2 < N:
                        tops(n + 2)
                scale_out(ROUND - 1)
                v.wait_ge(b_ready, j * B_ALL + B_ALL)
                d.tensor_copy(G.yb[:, bass.ds(j * (ROUND // 2) + (ROUND // 2 - 1), 1), 4 * P:]
                              .rearrange("p o (b t) -> p (o b) t", t=P), turn_b[:]).then_inc(b_taken, 1)


def merge(nc, A, G):
    ph = phase(nc)
    COL = 2 * D + Q_LORA + KV_LORA + ROPE + D
    HC = C // 2
    with ph.ctx:
        w_gate = ph.sb("w_gate", [P, 2, C, D // 4])
        w_out = ph.sb("w_out", [P, C, D])
        gate = ph.sb("gate", [P, 2, S])
        ps = ph.ps("ps", [P, 2, S])
        ps_o = ph.ps("ps_o", [P, 2, D])
        (wg0, wg1, wo_in, x_in, g_ready, g_taken, m_ready, o_ready, o_taken, dve) = ph.sems(
            "wg0 wg1 wo_in x_in g_ready g_taken m_ready o_ready o_taken dve")
        wg = [wg0, wg1]
        block = ph.ctx.enter_context(nc.Block())
        Q = 4
        PERQ = C // Q

        @block.sync
        def _(sp):
            w = A["w_in"].rearrange("l (c p) n -> p (l c) n", p=P)
            for q in range(Q):
                if q >= 2:
                    sp.wait_ge(g_ready, (q - 1) * PERQ)
                c0 = COL + q * (D // Q)
                sp.dma_start(w_gate[:, q % 2], w[:, :, c0:c0 + D // Q]).then_inc(wg[q % 2], 16)
                if q == 1:
                    sp.dma_start(w_out[:], A["w_out"].rearrange("l (c p) n -> p (l c) n", p=P)).then_inc(wo_in, 16)
            sp.wait_ge(g_ready, C)
            sp.dma_start(G.x2, A["x"].rearrange("b (t p) d -> p (b t) d", p=P)).then_inc(x_in, 16)

        @block.tensor
        def _(pe):
            for c in range(C):
                q, i = divmod(c, PERQ)
                if i == 0:
                    pe.wait_ge(wg[q % 2], 16 * (q // 2 + 1))
                if c >= 2:
                    pe.wait_ge(g_taken, c - 1)
                for h in range(HALF):
                    for kc in range(C):
                        last = nc.tensor.matmul(ps[:, c % 2, h * BANK:(h + 1) * BANK],
                                                w_gate[:, q % 2, kc, i * P:(i + 1) * P],
                                                G.u[:, kc, h * BANK:(h + 1) * BANK],
                                                start=kc == 0, stop=kc == C - 1)
                last.then_inc(g_ready, 1)
            pe.wait_ge(wo_in, 16)
            pe.wait_ge(m_ready, C)
            for t in range(T):
                if t >= 2:
                    pe.wait_ge(o_taken, t - 1)
                for h in range(HALF):
                    for kc in range(C):
                        last = nc.tensor.matmul(ps_o[:, t % 2, h * BANK:(h + 1) * BANK],
                                                G.ya[:, kc, t * P:(t + 1) * P],
                                                w_out[:, kc, h * BANK:(h + 1) * BANK],
                                                start=kc == 0, stop=kc == C - 1)
                last.then_inc(o_ready, 1)

        @block.scalar
        def _(a):
            for c in range(C):
                a.wait_ge(g_ready, c + 1)
                if c >= 2:
                    a.wait_ge(m_ready, c - 1)
                nc.scalar.activation(gate[:, c % 2, :], ps[:, c % 2, :], ACT.Sigmoid).then_inc(g_taken, 1)

        @block.vector
        def _(v):
            d = nc.vector
            st = Steps(v, dve)
            for c in range(C):
                v.wait_ge(g_taken, c + 1)
                st(d.tensor_tensor(G.yb[:, c, :], G.yb[:, c, :], gate[:, c % 2, :], ALU.mult))
                st.join()
                d.tensor_tensor(G.ya[:, c, :], G.ya[:, c, :], G.yb[:, c, :], ALU.add).then_inc(m_ready, 1)
            v.wait_ge(x_in, 16)
            for t in range(T):
                v.wait_ge(o_ready, t + 1)
                d.tensor_tensor(G.x2[:, t, :], G.x2[:, t, :], ps_o[:, t % 2, :], ALU.add).then_inc(o_taken, 1)


def norm_rows(nc, A, G, rows, rows_d):
    ph = phase(nc)
    with ph.ctx:
        gain = ph.sb("gain", [P, D])
        junk = ph.sb("junk", [P, D])
        ssq = ph.sb("ssq", [P, T])
        rstd = ph.sb("rstd", [P, T])
        gain_in, squared, mean, rooted, dve, stored = ph.sems("gain_in squared mean rooted dve stored")
        block = ph.ctx.enter_context(nc.Block())

        @block.sync
        def _(sp):
            sp.dma_start(gain[:], A["norm_ffn_g"].to_broadcast([P, D])).then_inc(gain_in, 16)
            for t in range(T):
                sp.wait_ge(dve, t + 2)
                sp.dma_start(rows_d[t * P:(t + 1) * P, :], rows[:, t, :]).then_inc(stored, 16)
            sp.wait_ge(stored, 16 * T)

        @block.scalar
        def _(a):
            for t in range(T):
                if t:
                    a.wait_ge(squared, t)
                nc.scalar.activation(junk[:], G.h[:, t, :], ACT.Square,
                                     accum_out=ssq[:, t:t + 1]).then_inc(squared, 1)
            a.wait_ge(mean, 1)
            nc.scalar.activation(rstd[:], ssq[:], ACT.Sqrt).then_inc(rooted, 1)

        @block.vector
        def _(v):
            d = nc.vector
            st = Steps(v, dve)
            v.wait_ge(squared, T)
            d.tensor_scalar(ssq[:], ssq[:], 1.0 / D, EPS, ALU.mult, ALU.add).then_inc(mean, 1)
            v.wait_ge(rooted, 1)
            st(d.reciprocal(rstd[:], rstd[:]))
            st.join()
            v.wait_ge(gain_in, 16)
            for t in range(T):
                st(d.scalar_tensor_tensor(out=rows[:, t, :], in0=G.h[:, t, :], scalar=rstd[:, t:t + 1],
                                          in1=gain[:], op0=ALU.mult, op1=ALU.mult))


def rows_to_cols(nc, G, rows, cols, logits=None, weights=()):
    ph = phase(nc)
    width = sum(n for _, n in weights)
    with ph.ctx:
        wr = ph.sb("wr", [P, C, max(width, 1)])
        tp = ph.ps("tp", [P, 2, C, P])
        w_in, turned, taken, lg = ph.sems("w_in turned taken lg")
        lps = ph.ps("lps", [P, T, max(width, 1)])
        block = ph.ctx.enter_context(nc.Block())

        @block.sync
        def _(sp):
            c0 = 0
            for src, n in weights:
                with nc.allow_non_contiguous_dma("small router matrices"):
                    sp.dma_start(wr[:, :, c0:c0 + n], src.rearrange("l (c p) n -> p (l c) n", p=P)).then_inc(w_in, 16)
                c0 += n

        @block.tensor
        def _(pe):
            def route(t):
                pe.wait_ge(taken, t + 1)
                for kc in range(C):
                    last = nc.tensor.matmul(lps[:, t, :], cols[:, kc, t * P:(t + 1) * P], wr[:, kc, :],
                                            start=kc == 0, stop=kc == C - 1)
                last.then_inc(lg, 1)

            if weights:
                pe.wait_ge(w_in, 16 * len(weights))
            for t in range(T):
                if t >= 2:
                    pe.wait_ge(taken, t - 1)
                for c in range(C):
                    last = nc.tensor.transpose(tp[:, t % 2, c, :], rows[:, t, c * P:(c + 1) * P], G.ident[:])
                last.then_inc(turned, 1)
                if weights and t:
                    route(t - 1)
            if weights:
                route(T - 1)

        @block.vector
        def _(v):
            for t in range(T):
                v.wait_ge(turned, t + 1)
                nc.vector.tensor_copy(cols[:, :, t * P:(t + 1) * P], tp[:, t % 2]).then_inc(taken, 1)
            if weights:
                v.wait_ge(lg, T)
                nc.vector.tensor_copy(logits, lps[:])


def route1(nc, A, G, lg):
    ph = phase(nc)
    PER = E1 // GROUPS1
    with ph.ctx:
        bias = ph.sb("bias", [P, GROUPS1 + E1])
        pad = ph.sb("pad", [P, T, 8])
        gtop = ph.sb("gtop", [P, T, 8])
        gidx = ph.sb("gidx", [P, T, 8], U32)
        gnum = ph.sb("gnum", [P, T, 1])
        pen = ph.sb("pen", [P, T, GROUPS1])
        ex = ph.sb("ex", [P, T, GROUPS1])
        pgrp = ph.sb("pgrp", [P, T])
        em = ph.sb("em", [P, T, GROUPS1, PER])
        etop = ph.sb("etop", [P, T, 8])
        eidx = ph.sb("eidx", [P, T, 8], U32)
        gap = ph.sb("gap", [P, T])
        loaded, dve, to_exp, exped, to_sig, siged = ph.sems("loaded dve to_exp exped to_sig siged")
        block = ph.ctx.enter_context(nc.Block())

        @block.sync
        def _(sp):
            sp.dma_start(bias[:, 0:GROUPS1], A["router_group_b"].to_broadcast([P, GROUPS1])).then_inc(loaded, 16)
            sp.dma_start(bias[:, GROUPS1:], A["router_expert_b"].to_broadcast([P, E1])).then_inc(loaded, 16)

        @block.scalar
        def _(a):
            a.wait_ge(to_exp, 1)
            nc.scalar.activation(ex[:], ex[:], ACT.Exp).then_inc(exped, 1)
            a.wait_ge(to_sig, 1)
            nc.scalar.activation(G.w[:, :, 0], gap[:], ACT.Sigmoid).then_inc(siged, 1)
            nc.scalar.activation(G.w[:, :, 1], gap[:], ACT.Sigmoid, scale=-1.0).then_inc(siged, 1)

        @block.vector
        def _(v):
            d = nc.vector
            st = Steps(v, dve)
            W = GROUPS1 + E1
            v.wait_ge(loaded, 32)
            st(d.tensor_tensor(lg, lg, bias[:, None, :].to_broadcast([P, T, W]), ALU.add))
            st(d.memset(pad[:], NEG))
            st.join()
            st(d.tensor_copy(pad[:, :, 0:GROUPS1], lg[:, :, 0:GROUPS1]))
            st.join()
            for t in range(T):
                st(d.max(gtop[:, t, :], pad[:, t, :]))
            st.join()
            for t in range(T):
                st(d.max_index(gidx[:, t, :], gtop[:, t, :], pad[:, t, :]))
            d.tensor_tensor(ex[:], lg[:, :, 0:GROUPS1], gtop[:, :, 0:1].to_broadcast([P, T, GROUPS1]),
                            ALU.subtract).then_inc(to_exp, 1)
            st.join()
            st(d.tensor_copy(gnum[:], gidx[:, :, 0:1]))
            st.join()
            st(d.tensor_tensor(pen[:], G.iota[:, None, 0:GROUPS1].to_broadcast([P, T, GROUPS1]),
                               gnum[:].to_broadcast([P, T, GROUPS1]), ALU.is_equal))
            st.join()
            st(d.tensor_scalar(pen[:], pen[:], -1.0, -NEG, ALU.add, ALU.mult))
            st.join()
            st(d.tensor_tensor(em[:], lg[:, :, GROUPS1:].rearrange("p t (g e) -> p t g e", g=GROUPS1),
                               pen[:, :, :, None].to_broadcast([P, T, GROUPS1, PER]), ALU.add))
            st.join()
            for t in range(T):
                st(d.max(etop[:, t, :], em[:, t]))
            st.join()
            for t in range(T):
                st(d.max_index(eidx[:, t, :], etop[:, t, :], em[:, t].rearrange("p g e -> p (g e)")))
            st(d.tensor_tensor(gap[:], etop[:, :, 0], etop[:, :, 1], ALU.subtract))
            st.join()
            d.tensor_copy(G.e, eidx[:, :, 0:K1]).then_inc(to_sig, 1)
            v.wait_ge(exped, 1)
            st(d.tensor_reduce(pgrp[:], ex[:], AX, ALU.add))
            st.join()
            st(d.reciprocal(pgrp[:], pgrp[:]))
            st.join()
            v.wait_ge(siged, 2)
            st(d.tensor_tensor(G.w, G.w, pgrp[:, :, None].to_broadcast([P, T, K1]), ALU.mult))


def dispatch(nc, G, K, E, NB, scores=None):
    ph = phase(nc)
    with ph.ctx:
        oh = ph.sb("oh", [P, T, K, E])
        prod = ph.sb("prod", [P, T, K, E])
        m = ph.sb("m", [P, T, E])
        before = ph.sb("before", [P, T + 1, E])
        cnt = ph.sb("cnt", [P, E])
        cnt_i = ph.sb("cnt_i", [P, E], I32)
        last_b = ph.sb("last_b", [P, E])
        first_b = ph.sb("first_b", [P, E])
        dest = ph.sb("dest", [P, T, E])
        destk = ph.sb("destk", [P, T, K])
        half_i = ph.sb("half_i", [P, 2, T, K], I32)
        half_f = ph.sb("half_f", [P, 2, T, K])
        lo = ph.sb("lo", [P, 2, K, P])
        hi = ph.sb("hi", [P, 2, K, P])
        cmp = ph.sb("cmp", [P, E])
        be = ph.sb("be", [P, 1])
        wsum = ph.sb("wsum", [P, T])
        rank = ph.ps("rank", [P, BANK])[:, 0:T * E].rearrange("p (t e) -> p t e", e=E)
        cps = ph.ps("cps", [P, BANK])[:, 0:E]
        tok_ps = ph.ps("tok_ps", [P, BANK])[:, 0:P]
        row_ps = ph.ps("row_ps", [1, BANK])[:, 0:P]
        (dve, sums_ready, ranked, be_ready, be_row, hot, scaled, used, toks) = ph.sems(
            "dve sums_ready ranked be_ready be_row hot scaled used toks")
        block = ph.ctx.enter_context(nc.Block())

        @block.tensor
        def _(pe):
            pe.wait_ge(sums_ready, 1)
            for t in range(T):
                nc.tensor.matmul(rank[:, t, :], G.tri[:], m[:, t, :], start=True, stop=False)
                nc.tensor.matmul(rank[:, t, :], G.ones[:], before[:, t, :], start=False, stop=True)
            nc.tensor.matmul(cps, G.ones[:], before[:, T, :], start=True, stop=True).then_inc(ranked, 1)
            pe.wait_ge(be_ready, 1)
            nc.tensor.matmul(row_ps, be[:], G.ident[:], start=True, stop=True).then_inc(be_row, 1)
            for t in range(T):
                pe.wait_ge(hot, t + 1)
                pe.wait_ge(scaled, t + 1)
                for k in range(K):
                    last = nc.tensor.matmul(tok_ps, lo[:, t % 2, k, :], hi[:, t % 2, k, :],
                                            start=t == 0 and k == 0, stop=t == T - 1 and k == K - 1)
                last.then_inc(used, 1)

        @block.scalar
        def _(a):
            for t in range(T):
                a.wait_ge(hot, t + 1)
                nc.scalar.activation(hi[:, t % 2], hi[:, t % 2], ACT.Copy, scale=G.tok[:, t:t + 1]).then_inc(scaled, 1)

        @block.vector
        def _(v):
            d = nc.vector
            st = Steps(v, dve)
            iota_e = G.iota[:, 0:E]
            for t in range(T):
                st(d.tensor_tensor(oh[:, t], G.e[:, t, :, None].to_broadcast([P, K, E]),
                                   iota_e[:, None, :].to_broadcast([P, K, E]), ALU.is_equal))
            st(d.memset(before[:, 0, :], 0.0))
            st.join()
            st(d.tensor_reduce(m[:], oh[:].rearrange("p t k e -> p t e k"), AX, ALU.add))
            st.join()
            for t in range(T):
                ins = d.tensor_tensor(before[:, t + 1, :], before[:, t, :], m[:, t, :], ALU.add)
                if t + 1 < T:
                    st(ins)
                    st.join()
                else:
                    ins.then_inc(sums_ready, 1)
            v.wait_ge(ranked, 1)
            st(d.tensor_scalar(cnt[:], cps, float(P - 1), None, ALU.add))
            st.join()
            st(d.tensor_copy(cnt_i[:], cnt[:]))
            st.join()
            st(d.tensor_scalar(cnt_i[:], cnt_i[:], 7, None, ALU.logical_shift_right))
            st.join()
            st(d.tensor_copy(cnt[:], cnt_i[:]))
            st.join()
            st(d.tensor_tensor_scan(last_b[:], G.ones[:, 0:E], cnt[:], 0.0, ALU.mult, ALU.add))
            st.join()
            st(d.tensor_tensor(first_b[:], last_b[:], cnt[:], ALU.subtract))
            st(d.tensor_copy(G.used, last_b[0:1, E - 1:E]))
            st(d.tensor_scalar(cmp[:], last_b[:], G.tok[:, 0:1], None, ALU.is_le))
            st.join()
            st(d.tensor_copy(G.first, first_b[0:1, :]))
            st(d.tensor_reduce(be[:], cmp[:], AX, ALU.add))
            st.join()
            d.tensor_scalar(be[:], be[:], float(E - 1), None, ALU.min).then_inc(be_ready, 1)
            st(d.scalar_tensor_tensor(out=dest[:], in0=first_b[:, None, :].to_broadcast([P, T, E]),
                                      scalar=float(P), in1=rank, op0=ALU.mult, op1=ALU.add))
            st.join()
            for t in range(T):
                st(d.tensor_tensor(prod[:, t], oh[:, t], dest[:, t, None, :].to_broadcast([P, K, E]), ALU.mult))
            st.join()
            st(d.tensor_reduce(destk[:], prod[:], AX, ALU.add))
            st.join()
            st(d.tensor_copy(G.slot, destk[:]))
            st.join()
            st(d.tensor_scalar(half_i[:, 0], G.slot, 7, None, ALU.logical_shift_right))
            st(d.tensor_scalar(half_i[:, 1], G.slot, P - 1, None, ALU.bitwise_and))
            st.join()
            st(d.tensor_copy(half_f[:], half_i[:]))
            st.join()
            iota_b = G.iota[:, None, :].to_broadcast([P, K, P])
            for t in range(T):
                if t >= 2:
                    v.wait_ge(used, t - 1)
                st(d.tensor_tensor(lo[:, t % 2], half_f[:, 1, t, :, None].to_broadcast([P, K, P]), iota_b, ALU.is_equal))
                d.tensor_tensor(hi[:, t % 2], half_f[:, 0, t, :, None].to_broadcast([P, K, P]), iota_b,
                                ALU.is_equal).then_inc(hot, 1)
            v.wait_ge(be_row, 1)
            st(d.tensor_copy(G.blk_e[:, 0:P], row_ps))
            st(d.memset(G.blk_e[:, P:], E - 1))
            if scores is not None:
                for t in range(T):
                    st(d.tensor_tensor(prod[:, t], oh[:, t], scores[:, t, None, :].to_broadcast([P, K, E]), ALU.mult))
                st.join()
                st(d.tensor_reduce(G.w, prod[:], AX, ALU.add))
                st.join()
                st(d.tensor_reduce(wsum[:], G.w, AX, ALU.add))
                st.join()
                st(d.reciprocal(wsum[:], wsum[:]))
                st.join()
                st(d.tensor_scalar(wsum[:], wsum[:], ROUTED_SCALE, None, ALU.mult))
                st.join()
                st(d.tensor_tensor(G.w, G.w, wsum[:, :, None].to_broadcast([P, T, K]), ALU.mult))
            st(d.memset(G.slot_tok, 0))
            v.wait_ge(used, T)
            st.join()
            st(d.tensor_copy(G.slot_tok[:, 0:P], tok_ps))


def experts(nc, G, E, NB, rows_d, wg_d, wu_d, wd_d, y_d):
    ph = phase(nc)
    W = 4
    FC = F_EXP // P
    with ph.ctx:
        w_gu = ph.sb("w_gu", [P, W, 2, C, F_EXP])
        w_dn = ph.sb("w_dn", [P, W, FC, D])
        idx = ph.sb("idx", [P, 2], I32)
        mark = ph.sb("mark", [P, 2])
        xb = ph.sb("xb", [P, 2, D])
        x_t = ph.sb("x_t", [P, 2, C, P])
        act_g = ph.sb("act_g", [P, 2, F_EXP])
        hid = ph.sb("hid", [P, 2, F_EXP])
        hid_t = ph.sb("hid_t", [P, 2, FC, P])
        y = ph.sb("y", [P, 2, D])
        x_ps = ph.ps("x_ps", [P, C, P])
        gu_ps = ph.ps("gu_ps", [P, 2, 2, F_EXP])
        h_ps = ph.ps("h_ps", [P, BANK // P, P])[:, 0:FC, :]
        y_ps = ph.ps("y_ps", [P, D])
        (w_in0, w_in1, w_in2, w_in3, w_ready, idx_ready, x_in0, x_in1, x_turned, x_ready, gu_ready,
         silu_done, hid_ready, h_turned, h_ready, y_ready, y_taken, y_out0, y_out1) = ph.sems(
            "w_in0 w_in1 w_in2 w_in3 w_ready idx_ready x_in0 x_in1 x_turned x_ready gu_ready "
            "silu_done hid_ready h_turned h_ready y_ready y_taken y_out0 y_out1")
        w_in, x_in, y_out = [w_in0, w_in1, w_in2, w_in3], [x_in0, x_in1], [y_out0, y_out1]
        wg_v = wg_d.rearrange("l e (p c) n -> (l e) p (c n)", c=C)
        wu_v = wu_d.rearrange("l e (p c) n -> (l e) p (c n)", c=C)
        wd_v = wd_d.rearrange("l e (p c) n -> (l e) p (c n)", c=FC)
        PAIRS = (NB + 1) // 2
        FAR = W - 2
        block = ph.ctx.enter_context(nc.Block())

        def steps(eng, step):
            n = eng.value_load(G.used, min_val=0, max_val=NB)
            for i in range(3):
                step(i, i % 2, 0)
            with eng.Fori(1, PAIRS) as j:
                for u in range(2):
                    i = j * 2 + (1 + u)
                    with eng.If(i <= n):
                        step(i, (1 + u) % 2, j * 16)
            return n

        @block.sync
        def _(sp):
            def load(e, slot):
                for dst, src in ((w_gu[:, slot, 0].rearrange("p c n -> p (c n)"), wg_v),
                                 (w_gu[:, slot, 1].rearrange("p c n -> p (c n)"), wu_v),
                                 (w_dn[:, slot].rearrange("p c n -> p (c n)"), wd_v)):
                    sp.dma_start(dst, src[bass.ds(e, 1)].rearrange("o p n -> p (o n)")).then_inc(w_in[slot], 16)

            for e in range(W):
                load(e, e)
            for e in range(W - 1):
                sp.wait_ge(w_in[e], 48)
                sp.sem_inc(w_ready, 1)
            with sp.Fori(0, E // W - 1) as j:
                for u in range(W):
                    e = j * W + (W + u)
                    done = sp.value_load(G.first[0:1, bass.ds(j * W + (u + 1), 1)], min_val=0, max_val=NB)
                    sp.wait_ge(y_ready, 1 + done)
                    load(e, u)
                    sp.wait_ge(w_in[(u - 1) % W], j * 48 + (48 if u == 0 else 96))
                    sp.sem_inc(w_ready, 1)
            sp.wait_ge(w_in[W - 1], (E // W) * 48)
            sp.sem_inc(w_ready, 1)

        @block.gpsimd
        def _(pool):
            g = nc.gpsimd

            def gather(b, slot, landed):
                if landed is not None:
                    pool.wait_ge(x_in[slot], landed)
                g.tensor_copy(idx[:, slot:slot + 1], G.slot_tok[:, bass.ds(b, 1)]).then_inc(idx_ready, 1)
                pool.wait_ge(idx_ready, 2 * b + 1)
                g.tensor_tensor(mark[:, slot:slot + 1], G.tok[:, 0:1], G.tok[:, 0:1], ALU.add).then_inc(idx_ready, 1)
                g.indirect_dma_start(xb[:, slot, :], None, rows_d, bass.IndirectOffsetOnAxis(
                    ap=idx[:, slot:slot + 1], axis=0)).then_inc(x_in[slot], 16)

            gather(0, 0, None)
            gather(1, 1, None)
            n = pool.value_load(G.used, min_val=0, max_val=NB)
            with pool.Fori(0, PAIRS) as j:
                for u in range(2):
                    i = j * 2 + (1 + u)
                    with pool.If(i <= n):
                        pool.wait_ge(x_turned, i)
                        gather(i + 1, u, j * 16 + 16)
            pool.wait_ge(y_out[0], (n + 1) // 2 * 16)
            pool.wait_ge(y_out[1], n // 2 * 16)

        @block.tensor
        def _(pe):
            def turn_rows(b, slot, landed):
                pe.wait_ge(x_in[slot], landed)
                for c in range(C):
                    last = nc.tensor.transpose(x_ps[:, c, :], xb[:, slot, c::C], G.ident[:])
                last.then_inc(x_turned, 1)

            def step(i, slot, rounds):
                first = isinstance(i, int) and i == 0
                e = pe.value_load(G.blk_e[0:1, bass.ds(i, 1)], min_val=0, max_val=E - 1)
                if not first:
                    e_before = pe.value_load(G.blk_e[0:1, bass.ds(i - 1, 1)], min_val=0, max_val=E - 1)
                    with pe.If(e > e_before + FAR):
                        finish(i, 1 - slot, e_before)
                pe.wait_ge(w_ready, e + 1)
                pe.wait_ge(x_ready, i + 1)
                ws = e % W
                for c in range(C):
                    last = nc.tensor.matmul(gu_ps[:, slot], x_t[:, slot, c, :],
                                            w_gu[:, bass.ds(ws, 1), :, c, :].rearrange("p o g n -> p (o g) n"),
                                            start=c == 0, stop=c == C - 1)
                last.then_inc(gu_ready, 1)
                turn_rows(i + 1, 1 - slot, 16 if first else rounds + 32)
                if not first:
                    with pe.If(e <= e_before + FAR):
                        finish(i, 1 - slot, e_before)
                pe.wait_ge(hid_ready, i + 1)
                for c in range(FC):
                    last = nc.tensor.transpose(h_ps[:, c, :], hid[:, slot, c::FC], G.ident[:])
                last.then_inc(h_turned, 1)

            def finish(i, slot, e):
                pe.wait_ge(h_ready, i)
                pe.wait_ge(y_taken, 1 + i - 1)
                ws = e % W
                for h in range(D // BANK):
                    for c in range(FC):
                        last = nc.tensor.matmul(y_ps[:, h * BANK:(h + 1) * BANK], hid_t[:, slot, c, :],
                                                w_dn[:, bass.ds(ws, 1), c, h * BANK:(h + 1) * BANK]
                                                .rearrange("p o n -> p (o n)"),
                                                start=c == 0, stop=c == FC - 1)
                last.then_inc(y_ready, 1)

            start_at_one(pe, y_ready)
            turn_rows(0, 0, 16)
            steps(pe, step)

        @block.scalar
        def _(a):
            s = nc.scalar

            def step(i, slot, rounds):
                a.wait_ge(gu_ready, i + 1)
                s.activation(act_g[:, slot, :], gu_ps[:, slot, 0, :], ACT.Silu).then_inc(silu_done, 1)
                if not (isinstance(i, int) and i == 0):
                    a.wait_ge(y_ready, 1 + i)
                    if not (isinstance(i, int) and i <= 2):
                        a.wait_ge(y_out[1 - slot], rounds)
                    s.activation(y[:, 1 - slot, :], y_ps[:], ACT.Copy).then_inc(y_taken, 1)
                    a.wait_ge(y_taken, 1 + i)
                    a.dma_start(y_d[bass.ds((i - 1) * P, P), :], y[:, 1 - slot, :]).then_inc(y_out[1 - slot], 16)

            start_at_one(a, y_taken)
            steps(a, step)

        @block.vector
        def _(v):
            d = nc.vector

            def step(i, slot, rounds):
                v.wait_ge(silu_done, i + 1)
                d.tensor_tensor(hid[:, slot, :], act_g[:, slot, :], gu_ps[:, slot, 1, :], ALU.mult).then_inc(hid_ready, 1)
                v.wait_ge(x_turned, i + 2)
                d.tensor_copy(x_t[:, 1 - slot], x_ps[:]).then_inc(x_ready, 1)
                v.wait_ge(h_turned, i + 1)
                d.tensor_copy(hid_t[:, slot], h_ps).then_inc(h_ready, 1)

            v.wait_ge(x_turned, 1)
            d.tensor_copy(x_t[:, 0], x_ps[:]).then_inc(x_ready, 1)
            steps(v, step)


def combine(nc, G, K, y_d):
    ph = phase(nc)
    R = 4
    with ph.ctx:
        idx = ph.sb("idx", [P, T * K], I32)
        yr = ph.sb("yr", [P, R, D])
        idx_ready, added = ph.sems("idx_ready added")
        y_in = ph.sems(" ".join(f"y_in{r}" for r in range(R)))
        block = ph.ctx.enter_context(nc.Block())

        @block.gpsimd
        def _(pool):
            nc.gpsimd.tensor_copy(idx[:], G.slot.rearrange("p t k -> p (t k)")).then_inc(idx_ready, 1)
            pool.wait_ge(idx_ready, 1)
            for n in range(T * K):
                if n >= R:
                    pool.wait_ge(added, n - R + 1)
                nc.gpsimd.indirect_dma_start(yr[:, n % R, :], None, y_d, bass.IndirectOffsetOnAxis(
                    ap=idx[:, n:n + 1], axis=0)).then_inc(y_in[n % R], 16)

        @block.vector
        def _(v):
            for n in range(T * K):
                v.wait_ge(y_in[n % R], 16 * (n // R + 1))
                if n % K:
                    v.wait_ge(added, n)
                h = G.h[:, n // K, :]
                nc.vector.scalar_tensor_tensor(out=h, in0=yr[:, n % R, :], scalar=G.w2[:, n:n + 1], in1=h,
                                               op0=ALU.mult, op1=ALU.add).then_inc(added, 1)


def moe_state(nc, ctx, G, K, E):
    sb = lambda name, shape, dt=F32: ctx.enter_context(nc.sbuf_tensor(name, shape, dt))
    G.e = sb(f"moe_e{E}", [P, T, K])[:]
    w = sb(f"moe_w{E}", [P, T * K])
    G.w2 = w[:]
    G.w = w[:].rearrange("p (t k) -> p t k", k=K)
    G.slot = sb(f"moe_slot{E}", [P, T, K], I32)[:]
    G.slot_tok = sb(f"moe_slot_tok{E}", [P, P + 2], I32)[:]
    G.blk_e = sb(f"moe_blk_e{E}", [1, P + 1], I32)[:]
    G.first = sb(f"moe_first{E}", [1, E], I32)[:]
    G.used = sb(f"moe_used{E}", [1, 1], I32)[:]


def hgrn(nc, A, G):
    ph = phase(nc)
    LEVELS = P.bit_length() - 1
    N = LEVELS + 1
    MASKED = 4 + 3 * LEVELS
    N_STEPS = 7 + 3 * LEVELS
    w_in = A["w_in_2"].rearrange("l (c p) (k h n) -> (l h) p c k n", p=P, h=HG_HEADS, n=P)
    with ph.ctx:
        w = ph.sb("w", [P, 4, C, P])
        lb_col = ph.sb("lb_col", [P, HG_HEADS])
        lb1_col = ph.sb("lb1_col", [P, HG_HEADS])
        gain = ph.sb("gain", [P, HG_W])
        mask = ph.sb("mask", [P, N, P])
        keep = ph.sb("keep", [P, S])
        q = ph.sb("q", [P, S])
        k = ph.sb("k", [P, S])
        b = ph.sb("b", [P, S])
        e = ph.sb("e", [P, S])
        qk = ph.sb("qk", [P, LEVELS, S])
        qb = ph.sb("qb", [P, S])
        kd = ph.sb("kd", [P, S])
        eb = ph.sb("eb", [P, T])
        val = ph.sb("val", [P, T, P])
        gate = ph.sb("gate", [P, T, P])
        osq = e[:].rearrange("p (t n) -> p t n", n=P)
        kd_t = ph.sb("kd_t", [P, 2, P])
        sm = ph.sb("sm", [P, N, P])
        sc = ph.sb("sc", [P, 2, P])
        state = ph.sb("state", [P, P])
        o = ph.sb("o", [P, T, P])
        rs = ph.sb("rs", [P, T])
        big = ph.ps("big", [P, 2, S])
        kt_ps = ph.ps("kt_ps", [P, BANK])[:, 0:P]
        o_ps = ph.ps("o_ps", [P, BANK])[:, 0:P]
        u_ps = ph.ps("u_ps", [P, BANK])[:, 0:P]
        (w_in_sem, gain_in, masked, proj, proj_taken, dve, act, to_exp, exped, lev_ready, sc_ps, sc_taken,
         sc_ready, kt_ready, kt_taken, o_ready, o_taken, u_ready, st_ready, root_in, rooted, o_done,
         turned, head_done, lb_ready) = ph.sems(
            "w_in_sem gain_in masked proj proj_taken dve act to_exp exped lev_ready sc_ps sc_taken "
            "sc_ready kt_ready kt_taken o_ready o_taken u_ready st_ready root_in rooted o_done "
            "turned head_done lb_ready")
        block = ph.ctx.enter_context(nc.Block())
        H = HG_HEADS

        @block.sync
        def _(sp):
            sp.dma_start(gain[:], A["hg_norm_g_2"].to_broadcast([P, HG_W])).then_inc(gain_in, 16)
            for i in range(4):
                sp.dma_start(w[:, i], w_in[0, :, :, i, :]).then_inc(w_in_sem, 16)
            with sp.Fori(0, H - 1) as h:
                sp.wait_ge(proj, h * 4 + 4)
                for i in range(4):
                    sp.dma_start(w[:, i], w_in[bass.ds(h + 1, 1), :, :, i, :].rearrange("o p c n -> p (o c) n")
                                 ).then_inc(w_in_sem, 16)

        @block.gpsimd
        def _(pool):
            g = nc.gpsimd
            st = Steps(pool, masked)
            st(g.memset(mask[:], 1.0))
            st(g.memset(keep[:], 1.0))
            st.join()
            st(g.memset(keep[:, 0::P], 0.0))
            for lev in range(LEVELS):
                half = 1 << lev
                pieces = P // (2 * half)
                m = mask[:, lev, :].rearrange("s (n r) -> s n r", r=2 * half)
                st(g.affine_select(out=m, in_=m, compare_op=ALU.is_ge, fill=0.0, base=0,
                                   pattern=[[-2 * half, pieces], [0, 2 * half]], channel_multiplier=1))
                st.join()
                st(g.affine_select(out=m, in_=m, compare_op=ALU.is_gt, fill=0.0, base=half,
                                   pattern=[[2 * half, pieces], [0, 2 * half]], channel_multiplier=-1))
                st.join()
                st(g.memset(m[:, :, 0:half], 0.0))
            st(g.affine_select(out=mask[:, LEVELS, :], in_=mask[:, LEVELS, :], compare_op=ALU.is_equal, fill=0.0,
                               base=0, pattern=[[-1, P]], channel_multiplier=1))
            assert st.n == MASKED, st.n

        @block.tensor
        def _(pe):
            with pe.Fori(0, H) as h:
                def project(i, by_channel):
                    pe.wait_ge(proj_taken, 1 + h * 4 + max(i - 1, 0))
                    slot = i % 2
                    if by_channel:
                        for half in range(HALF):
                            for kc in range(C):
                                last = nc.tensor.matmul(big[:, slot, half * BANK:(half + 1) * BANK], w[:, i, kc, :],
                                                        G.u[:, kc, half * BANK:(half + 1) * BANK],
                                                        start=kc == 0, stop=kc == C - 1)
                    else:
                        for t in range(T):
                            for kc in range(C):
                                last = nc.tensor.matmul(big[:, slot, t * P:(t + 1) * P],
                                                        G.u[:, kc, t * P:(t + 1) * P], w[:, i, kc, :],
                                                        start=kc == 0, stop=kc == C - 1)
                    last.then_inc(proj, 1)

                pe.wait_ge(w_in_sem, h * 64 + 64)
                for i in range(4):
                    project(i, i < 2)
                pe.wait_ge(lev_ready, h + 1)
                pe.wait_ge(proj_taken, 1 + h * 4 + 4)

                def scores(t):
                    cs = slice(t * P, (t + 1) * P)
                    pe.wait_ge(sc_taken, 1 + h * T + max(t - 1, 0))
                    for lev in range(N):
                        kk, qq = (qk[:, lev, cs], qk[:, lev, cs]) if lev < LEVELS else (k[:, cs], q[:, cs])
                        last = nc.tensor.matmul(big[:, t % 2, lev * P:(lev + 1) * P], kk, qq, start=True, stop=True)
                    last.then_inc(sc_ps, 1)
                    if t:
                        pe.wait_ge(kt_taken, h * T + t)
                    nc.tensor.transpose(kt_ps, kd[:, cs], G.ident[:]).then_inc(kt_ready, 1)

                scores(0)
                for t in range(T):
                    if t + 1 < T:
                        scores(t + 1)
                    pe.wait_ge(sc_ready, h * T + t + 1)
                    pe.wait_ge(st_ready, h * (T + 1) + t + 1)
                    pe.wait_ge(o_taken, 1 + h * T + t)
                    nc.tensor.matmul(o_ps, sc[:, t % 2, :], val[:, t, :], start=True, stop=False)
                    nc.tensor.matmul(o_ps, qb[:, t * P:(t + 1) * P], state[:], start=False, stop=True
                                     ).then_inc(o_ready, 1)
                    pe.wait_ge(kt_taken, h * T + t + 1)
                    nc.tensor.matmul(u_ps, kd_t[:, t % 2, :], val[:, t, :], start=True, stop=True).then_inc(u_ready, 1)
                pe.wait_ge(o_done, h + 1)
                for t in range(T):
                    last = nc.tensor.transpose(big[:, 0, t * P:(t + 1) * P], o[:, t, :], G.ident[:])
                last.then_inc(turned, 1)
                pe.wait_ge(head_done, 1 + h + 1)

        @block.scalar
        def _(a):
            s = nc.scalar
            start_at_one(a, proj_taken, o_taken)
            a.wait_ge(lb_ready, 1)
            s.activation(lb_col[:], lb_col[:], ACT.Sigmoid).then_inc(act, 1)
            with a.Fori(0, H) as h:
                a.wait_ge(head_done, 1 + h)
                a.wait_ge(proj, h * 4 + 1)
                s.activation(q[:], big[:, 0], ACT.Silu).then_inc(proj_taken, 1)
                a.wait_ge(proj, h * 4 + 2)
                s.activation(k[:], big[:, 1], ACT.Sigmoid).then_inc(proj_taken, 1)
                a.wait_ge(proj, h * 4 + 3)
                s.activation(val[:].rearrange("p t n -> p (t n)"), big[:, 0], ACT.Copy).then_inc(proj_taken, 1)
                a.wait_ge(proj, h * 4 + 4)
                s.activation(gate[:].rearrange("p t n -> p (t n)"), big[:, 1], ACT.Silu).then_inc(proj_taken, 1)
                a.wait_ge(to_exp, h * (LEVELS + 2) + 1)
                s.activation(b[:], e[:], ACT.Ln).then_inc(exped, 1)
                for lev in range(LEVELS):
                    a.wait_ge(to_exp, h * (LEVELS + 2) + lev + 2)
                    s.activation(qk[:, lev, :], qk[:, lev, :], ACT.Exp).then_inc(exped, 1)
                a.wait_ge(to_exp, h * (LEVELS + 2) + LEVELS + 2)
                s.activation(kd[:], kd[:], ACT.Exp).then_inc(exped, 1)
                s.activation(eb[:], e[:, P - 1::P], ACT.Exp).then_inc(exped, 1)
                s.activation(qb[:], e[:], ACT.Exp).then_inc(exped, 1)
                for t in range(T):
                    a.wait_ge(kt_ready, h * T + t + 1)
                    if t >= 2:
                        a.wait_ge(u_ready, h * T + t - 1)
                    s.activation(kd_t[:, t % 2, :], kt_ps, ACT.Copy).then_inc(kt_taken, 1)
                    a.wait_ge(o_ready, h * T + t + 1)
                    s.activation(o[:, t, :], o_ps, ACT.Copy).then_inc(o_taken, 1)
                a.wait_ge(o_taken, 1 + h * T + T)
                s.activation(osq, o[:], ACT.Square).then_inc(act, 1)
                a.wait_ge(root_in, h + 1)
                s.activation(rs[:], rs[:], ACT.Sqrt).then_inc(rooted, 1)

        @block.vector
        def _(v):
            d = nc.vector
            start_at_one(v, sc_taken, head_done)
            first, _ = VROW["hg_lb_logits_2"]
            d.tensor_tensor(lb_col[:], G.vec[:, first:first + H], G.vec[:, first + H:first + 2 * H],
                            ALU.subtract).then_inc(lb_ready, 1)
            v.wait_ge(act, 1)
            d.tensor_scalar(lb1_col[:], lb_col[:], -1.0, 1.0, ALU.mult, ALU.add).then_inc(lb_ready, 1)
            v.wait_ge(lb_ready, 2)
            v.wait_ge(masked, MASKED)
            v.wait_ge(gain_in, 16)
            with v.Fori(0, H) as h:
                st = Steps(v, dve, h * N_STEPS)
                EX = h * (LEVELS + 2)
                EXD = h * (LEVELS + 4)
                v.wait_ge(proj_taken, 1 + h * 4 + 2)
                d.tensor_scalar(e[:], k[:], lb1_col[:, bass.ds(h, 1)], lb_col[:, bass.ds(h, 1)], ALU.mult,
                                ALU.add).then_inc(to_exp, 1)
                v.wait_ge(to_exp, EX + 1)
                st(d.tensor_scalar(k[:], e[:], -1.0, 1.0, ALU.mult, ALU.add))
                v.wait_ge(exped, EXD + 1)
                st.join()
                st(d.tensor_tensor_scan(e[:], keep[:], b[:], 0.0, ALU.mult, ALU.add))
                st.join()
                piece = "p (n r) -> p n r"
                for lev in range(LEVELS):
                    half = 1 << lev
                    bb = e[:].rearrange(piece, r=2 * half)
                    out = qk[:, lev, :].rearrange(piece, r=2 * half)
                    mid = bb[:, :, half - 1:half].to_broadcast([P, S // (2 * half), half])
                    st(d.tensor_tensor(out[:, :, 0:half], mid, bb[:, :, 0:half], ALU.subtract))
                    d.tensor_tensor(out[:, :, half:], bb[:, :, half:], mid, ALU.subtract).then_inc(to_exp, 1)
                bb = e[:].rearrange(piece, r=P)
                d.tensor_tensor(kd[:].rearrange(piece, r=P), bb[:, :, P - 1:P].to_broadcast([P, T, P]),
                                bb, ALU.subtract).then_inc(to_exp, 1)
                for lev in range(LEVELS):
                    half = 1 << lev
                    out = qk[:, lev, :].rearrange(piece, r=2 * half)
                    v.wait_ge(exped, EXD + 2 + lev)
                    for by, sl in ((k, slice(0, half)), (q, slice(half, 2 * half))):
                        st(d.tensor_tensor(out[:, :, sl], out[:, :, sl],
                                           by[:].rearrange(piece, r=2 * half)[:, :, sl], ALU.mult))
                v.wait_ge(exped, EXD + LEVELS + 4)
                st(d.tensor_tensor(kd[:], kd[:], k[:], ALU.mult))
                d.tensor_tensor(qb[:], qb[:], q[:], ALU.mult).then_inc(lev_ready, 1)
                d.memset(state[:], 0.0).then_inc(st_ready, 1)
                for t in range(T):
                    v.wait_ge(sc_ps, h * T + t + 1)
                    d.tensor_tensor(sm[:].rearrange("p n t -> p (n t)"), big[:, t % 2],
                                    mask[:].rearrange("p n t -> p (n t)"), ALU.mult).then_inc(sc_taken, 1)
                    v.wait_ge(sc_taken, 1 + h * T + t + 1)
                    if t >= 2:
                        v.wait_ge(o_ready, h * T + t - 1)
                    if t == 0:
                        v.wait_ge(st_ready, h * (T + 1) + 1)
                    d.tensor_reduce(sc[:, t % 2, :], sm[:].rearrange("p n t -> p t n"), AX, ALU.add).then_inc(sc_ready, 1)
                    v.wait_ge(u_ready, h * T + t + 1)
                    d.scalar_tensor_tensor(out=state[:], in0=state[:], scalar=eb[:, t:t + 1], in1=u_ps,
                                           op0=ALU.mult, op1=ALU.add).then_inc(st_ready, 1)
                    v.wait_ge(st_ready, h * (T + 1) + t + 2)
                v.wait_ge(act, h + 2)
                st(d.tensor_reduce(rs[:], osq[:], AX, ALU.add))
                st.join()
                d.tensor_scalar(rs[:], rs[:], 1.0 / P, EPS, ALU.mult, ALU.add).then_inc(root_in, 1)
                v.wait_ge(rooted, h + 1)
                st(d.reciprocal(rs[:], rs[:]))
                st.join()
                v.wait_ge(proj_taken, 1 + h * 4 + 4)
                st(d.tensor_tensor(gate[:], gate[:], gain[:, bass.ds(h * P, P)].unsqueeze(1).to_broadcast([P, T, P]), ALU.mult))
                st(d.tensor_tensor(o[:], o[:], rs[:, :, None].to_broadcast([P, T, P]), ALU.mult))
                st.join()
                d.tensor_tensor(o[:], o[:], gate[:], ALU.mult).then_inc(o_done, 1)
                v.wait_ge(turned, h + 1)
                d.tensor_copy(G.mix[:, bass.ds(h, 1), :].rearrange("p o t -> p (o t)"), big[:, 0]
                              ).then_inc(head_done, 1)
                assert st.n == N_STEPS, st.n


def pooling(nc, A, G):
    ph = phase(nc)
    GR = POOL_W // P
    PAD = 1 << GR
    scale = vec(G, "pool_scale_2")
    with ph.ctx:
        w = ph.sb("w", [P, C, POOL_W])
        w_pool = ph.sb("w_pool", [P, GR, P])
        sums = ph.sb("sums", [P, 2, PAD + S])
        u = ph.sb("u", [P, S])
        inv = ph.sb("inv", [P, GR, PAD])
        pos = ph.sb("pos", [P, PAD])
        mean = ph.sb("mean", [P, 2, S])
        u_ps = ph.ps("u_ps", [P, 2, S])
        p_ps = ph.ps("p_ps", [P, 2, S])
        w_in, wp_in, u_ready, u_taken, m_ready, p_ready, p_taken, dve = ph.sems(
            "w_in wp_in u_ready u_taken m_ready p_ready p_taken dve")
        block = ph.ctx.enter_context(nc.Block())

        @block.sync
        def _(sp):
            sp.dma_start(w[:], A["w_in_2"].rearrange("l (c p) n -> p (l c) n", p=P)[:, :, 4 * HG_W:]).then_inc(w_in, 16)
            sp.dma_start(w_pool[:], A["w_pool_2"].rearrange("l g c d -> c (l g) d")).then_inc(wp_in, 16)

        @block.tensor
        def _(pe):
            def mix(g):
                pe.wait_ge(m_ready, g + 1)
                if g >= 2:
                    pe.wait_ge(p_taken, g - 1)
                for half in range(HALF):
                    hs = slice(half * BANK, (half + 1) * BANK)
                    last = nc.tensor.matmul(p_ps[:, g % 2, hs], w_pool[:, g, :], mean[:, g % 2, hs], start=True, stop=True)
                last.then_inc(p_ready, 1)

            pe.wait_ge(w_in, 16)
            pe.wait_ge(wp_in, 16)
            for g in range(GR):
                if g >= 2:
                    pe.wait_ge(u_taken, g - 1)
                for half in range(HALF):
                    hs = slice(half * BANK, (half + 1) * BANK)
                    for kc in range(C):
                        last = nc.tensor.matmul(u_ps[:, g % 2, hs], w[:, kc, g * P:(g + 1) * P], G.u[:, kc, hs],
                                                start=kc == 0, stop=kc == C - 1)
                last.then_inc(u_ready, 1)
                if g:
                    mix(g - 1)
            mix(GR - 1)

        @block.scalar
        def _(a):
            for g in range(GR):
                a.wait_ge(p_ready, g + 1)
                nc.scalar.activation(G.mix[:, HG_HEADS + g, :], p_ps[:, g % 2, :], ACT.Copy,
                                     scale=scale[:, g:g + 1]).then_inc(p_taken, 1)

        @block.vector
        def _(v):
            d = nc.vector
            st = Steps(v, dve)
            st(d.memset(sums[:, :, 0:PAD], 0.0))
            st(d.tensor_scalar(pos[:], G.iota[:, 0:PAD], 1.0, None, ALU.add))
            st.join()
            st(d.reciprocal(pos[:], pos[:]))
            st.join()
            for g in range(GR):
                st(d.tensor_scalar(inv[:, g, :], pos[:], 1.0 / (2 << g), None, ALU.max))
            for g in range(GR):
                v.wait_ge(u_ready, g + 1)
                if g:
                    st.join()
                    v.wait_ge(m_ready, g)
                st(d.tensor_copy(sums[:, 0, PAD:], u_ps[:, g % 2, :]))
                st.join()
                d.tensor_copy(u[:], sums[:, 0, PAD:]).then_inc(u_taken, 1)
                for n in range(g + 1):
                    src, dst = sums[:, n % 2], sums[:, (n + 1) % 2]
                    st(d.tensor_tensor(dst[:, PAD:], src[:, PAD:], src[:, PAD - (1 << n):PAD + S - (1 << n)], ALU.add))
                    st.join()
                total = sums[:, (g + 1) % 2]
                v.wait_ge(u_taken, g + 1)
                if g >= 2:
                    v.wait_ge(p_ready, g - 1)
                m = mean[:, g % 2]
                st(d.tensor_tensor(total[:, PAD:2 * PAD], total[:, PAD:2 * PAD], inv[:, g, :], ALU.mult))
                st.join()
                st(d.tensor_tensor(m[:, 0:PAD], total[:, PAD:2 * PAD], u[:, 0:PAD], ALU.subtract))
                d.scalar_tensor_tensor(out=m[:, PAD:], in0=total[:, 2 * PAD:], scalar=1.0 / (2 << g), in1=u[:, PAD:],
                                       op0=ALU.mult, op1=ALU.subtract).then_inc(m_ready, 1)


def mix_out(nc, A, G):
    ph = phase(nc)
    with ph.ctx:
        w_out = ph.sb("w_out", [P, C, D])
        ps = ph.ps("ps", [P, 2, D])
        w_in, ready, taken = ph.sems("w_in ready taken")
        block = ph.ctx.enter_context(nc.Block())

        @block.sync
        def _(sp):
            sp.dma_start(w_out[:], A["w_out_2"].rearrange("l (c p) n -> p (l c) n", p=P)).then_inc(w_in, 16)

        @block.tensor
        def _(pe):
            pe.wait_ge(w_in, 16)
            for t in range(T):
                if t >= 2:
                    pe.wait_ge(taken, t - 1)
                for h in range(HALF):
                    for kc in range(C):
                        last = nc.tensor.matmul(ps[:, t % 2, h * BANK:(h + 1) * BANK], G.mix[:, kc, t * P:(t + 1) * P],
                                                w_out[:, kc, h * BANK:(h + 1) * BANK], start=kc == 0, stop=kc == C - 1)
                last.then_inc(ready, 1)

        @block.vector
        def _(v):
            for t in range(T):
                v.wait_ge(ready, t + 1)
                nc.vector.scalar_tensor_tensor(out=G.h[:, t, :], in0=G.h[:, t, :], scalar=ALPHA, in1=ps[:, t % 2, :],
                                               op0=ALU.mult, op1=ALU.add).then_inc(taken, 1)


def layer_norm(nc, G, gain_d, bias_d, out_d):
    ph = phase(nc)
    with ph.ctx:
        gain = ph.sb("gain", [P, D])
        bias = ph.sb("bias", [P, D])
        junk = ph.sb("junk", [P, 2, D])
        total = ph.sb("total", [P, T])
        var = ph.sb("var", [P, T])
        shift = ph.sb("shift", [P, T])
        (vec_in, summed, mean, squared, var_ready, rooted, rstd_ready, dve, normed, rows_ready, stored) = ph.sems(
            "vec_in summed mean squared var_ready rooted rstd_ready dve normed rows_ready stored")
        block = ph.ctx.enter_context(nc.Block())

        @block.sync
        def _(sp):
            sp.dma_start(gain[:], gain_d.to_broadcast([P, D])).then_inc(vec_in, 16)
            sp.dma_start(bias[:], bias_d.to_broadcast([P, D])).then_inc(vec_in, 16)
            for t in range(T):
                sp.wait_ge(rows_ready, t + 1)
                sp.dma_start(out_d[t * P:(t + 1) * P, :], G.h[:, t, :]).then_inc(stored, 16)
            sp.wait_ge(stored, 16 * T)

        @block.scalar
        def _(a):
            s = nc.scalar

            def sums(t):
                if t:
                    a.wait_ge(summed, t)
                s.activation(junk[:, 0, :], G.h[:, t, :], ACT.Copy, accum_out=total[:, t:t + 1]).then_inc(summed, 1)

            sums(0)
            for t in range(T):
                if t + 1 < T:
                    sums(t + 1)
                a.wait_ge(mean, t + 1)
                if t:
                    a.wait_ge(squared, t)
                s.activation(junk[:, 1, :], G.h[:, t, :], ACT.Square, bias=total[:, t:t + 1],
                             accum_out=var[:, t:t + 1]).then_inc(squared, 1)
            a.wait_ge(var_ready, 1)
            s.activation(var[:], var[:], ACT.Sqrt).then_inc(rooted, 1)
            a.wait_ge(rstd_ready, 1)
            for t in range(T):
                s.activation(G.h[:, t, :], G.h[:, t, :], ACT.Identity, bias=shift[:, t:t + 1],
                             scale=var[:, t:t + 1]).then_inc(normed, 1)

        @block.vector
        def _(v):
            d = nc.vector
            st = Steps(v, dve)
            for t in range(T):
                v.wait_ge(summed, t + 1)
                d.tensor_scalar(total[:, t:t + 1], total[:, t:t + 1], -1.0 / D, None, ALU.mult).then_inc(mean, 1)
            v.wait_ge(squared, T)
            d.tensor_scalar(var[:], var[:], 1.0 / D, LN_EPS, ALU.mult, ALU.add).then_inc(var_ready, 1)
            v.wait_ge(rooted, 1)
            st(d.reciprocal(var[:], var[:]))
            st.join()
            v.wait_ge(mean, T)
            d.tensor_tensor(shift[:], total[:], var[:], ALU.mult).then_inc(rstd_ready, 1)
            v.wait_ge(vec_in, 32)
            for t in range(T):
                v.wait_ge(normed, t + 1)
                st(d.tensor_tensor(G.h[:, t, :], G.h[:, t, :], gain[:], ALU.mult))
                st.join()
                d.tensor_tensor(G.h[:, t, :], G.h[:, t, :], bias[:], ALU.add).then_inc(rows_ready, 1)


def route2(nc, A, G, scores):
    ph = phase(nc)
    PER = E2 // GROUPS2
    with ph.ctx:
        bias = ph.sb("bias", [P, E2])
        sel = ph.sb("sel", [P, T, E2])
        gtop = ph.sb("gtop", [P, T, GROUPS2, 8])
        gsum = ph.sb("gsum", [P, T, GROUPS2])
        best = ph.sb("best", [P, T, 8])
        bidx = ph.sb("bidx", [P, T, 8], U32)
        bnum = ph.sb("bnum", [P, T, TOPG2])
        hot = ph.sb("hot", [P, T, GROUPS2, TOPG2])
        pen = ph.sb("pen", [P, T, GROUPS2])
        etop = ph.sb("etop", [P, T, 8])
        eidx = ph.sb("eidx", [P, T, 8], U32)
        loaded, siged, dve = ph.sems("loaded siged dve")
        block = ph.ctx.enter_context(nc.Block())

        @block.sync
        def _(sp):
            sp.dma_start(bias[:], A["router_bias_2"].to_broadcast([P, E2])).then_inc(loaded, 16)

        @block.scalar
        def _(a):
            nc.scalar.activation(scores, scores, ACT.Sigmoid).then_inc(siged, 1)

        @block.vector
        def _(v):
            d = nc.vector
            st = Steps(v, dve)
            v.wait_ge(loaded, 16)
            v.wait_ge(siged, 1)
            st(d.tensor_tensor(sel[:], scores, bias[:, None, :].to_broadcast([P, T, E2]), ALU.add))
            st.join()
            for t in range(T):
                for g in range(GROUPS2):
                    st(d.max(gtop[:, t, g, :], sel[:, t, g * PER:(g + 1) * PER]))
            st.join()
            st(d.tensor_tensor(gsum[:], gtop[:, :, :, 0], gtop[:, :, :, 1], ALU.add))
            st.join()
            for t in range(T):
                st(d.max(best[:, t, :], gsum[:, t, :]))
            st.join()
            for t in range(T):
                st(d.max_index(bidx[:, t, :], best[:, t, :], gsum[:, t, :]))
            st.join()
            st(d.tensor_copy(bnum[:], bidx[:, :, 0:TOPG2]))
            st.join()
            st(d.tensor_tensor(hot[:], G.iota[:, None, 0:GROUPS2, None].to_broadcast([P, T, GROUPS2, TOPG2]),
                               bnum[:, :, None, :].to_broadcast([P, T, GROUPS2, TOPG2]), ALU.is_equal))
            st.join()
            st(d.tensor_reduce(pen[:], hot[:], AX, ALU.add))
            st.join()
            st(d.tensor_scalar(pen[:], pen[:], -1.0, -NEG, ALU.add, ALU.mult))
            st.join()
            st(d.tensor_tensor(sel[:].rearrange("p t (g e) -> p t g e", g=GROUPS2),
                               sel[:].rearrange("p t (g e) -> p t g e", g=GROUPS2),
                               pen[:, :, :, None].to_broadcast([P, T, GROUPS2, PER]), ALU.add))
            st.join()
            for t in range(T):
                st(d.max(etop[:, t, :], sel[:, t, :]))
            st.join()
            for t in range(T):
                st(d.max_index(eidx[:, t, :], etop[:, t, :], sel[:, t, :]))
            st.join()
            st(d.tensor_copy(G.e, eidx[:]))


def shared_and_combine(nc, A, G, cols, y_d):
    ph = phase(nc)
    K, R = K2, 4
    FC = F_EXP // P
    with ph.ctx:
        w_gu = ph.sb("w_gu", [P, 2, C, F_EXP])
        w_dn = ph.sb("w_dn", [P, FC, D])
        hid = ph.sb("hid", [P, FC, S])
        idx = ph.sb("idx", [P, T * K], I32)
        yr = ph.sb("yr", [P, R, D])
        gu_ps = ph.ps("gu_ps", [P, 2, 2, BANK])
        y_ps = ph.ps("y_ps", [P, 2, D])
        w_in, gu_ready, silu_done, hid_ready, y_ready, idx_ready, scaled, added = ph.sems(
            "w_in gu_ready silu_done hid_ready y_ready idx_ready scaled added")
        y_in = ph.sems(" ".join(f"y_in{r}" for r in range(R)))
        block = ph.ctx.enter_context(nc.Block())
        UNITS = [(f, half) for f in range(FC) for half in range(HALF)]
        order = []
        for t in range(T):
            order += [("row", t, k) for k in range(K)]
            if t < len(UNITS):
                order.append(("hid", t, 0))
            else:
                order.append(("out", t - len(UNITS), 0))
        order += [("out", t, 0) for t in range(T - len(UNITS), T)]
        adds = [x for x in order if x[0] != "hid"]
        add_no = {x: n for n, x in enumerate(adds)}

        @block.sync
        def _(sp):
            for i, name in enumerate(("ws_gate_2", "ws_up_2")):
                sp.dma_start(w_gu[:, i], A[name].rearrange("l (c p) n -> p (l c) n", p=P)).then_inc(w_in, 16)
            sp.dma_start(w_dn[:], A["ws_down_2"].rearrange("l (c p) n -> p (l c) n", p=P)).then_inc(w_in, 16)

        @block.gpsimd
        def _(pool):
            nc.gpsimd.tensor_copy(idx[:], G.slot.rearrange("p t k -> p (t k)")).then_inc(idx_ready, 1)
            pool.wait_ge(idx_ready, 1)
            for n in range(T * K):
                if n >= R:
                    pool.wait_ge(added, add_no["row", (n - R) // K, (n - R) % K] + 1)
                nc.gpsimd.indirect_dma_start(yr[:, n % R, :], None, y_d, bass.IndirectOffsetOnAxis(
                    ap=idx[:, n:n + 1], axis=0)).then_inc(y_in[n % R], 16)

        @block.tensor
        def _(pe):
            pe.wait_ge(w_in, 48)
            for n, (f, half) in enumerate(UNITS):
                if n >= 2:
                    pe.wait_ge(hid_ready, n - 1)
                for i in range(2):
                    for kc in range(C):
                        last = nc.tensor.matmul(gu_ps[:, n % 2, i, :], w_gu[:, i, kc, f * P:(f + 1) * P],
                                                cols[:, kc, half * BANK:(half + 1) * BANK],
                                                start=kc == 0, stop=kc == C - 1)
                last.then_inc(gu_ready, 1)
            pe.wait_ge(hid_ready, len(UNITS))
            for t in range(T):
                if t >= 2:
                    pe.wait_ge(added, add_no["out", t - 2, 0] + 1)
                for h in range(HALF):
                    for f in range(FC):
                        last = nc.tensor.matmul(y_ps[:, t % 2, h * BANK:(h + 1) * BANK], hid[:, f, t * P:(t + 1) * P],
                                                w_dn[:, f, h * BANK:(h + 1) * BANK], start=f == 0, stop=f == FC - 1)
                last.then_inc(y_ready, 1)

        @block.scalar
        def _(a):
            for t in range(T):
                nc.scalar.activation(G.h[:, t, :], G.h[:, t, :], ACT.Copy, scale=ALPHA).then_inc(scaled, 1)
            for n, (f, half) in enumerate(UNITS):
                a.wait_ge(gu_ready, n + 1)
                nc.scalar.activation(hid[:, f, half * BANK:(half + 1) * BANK], gu_ps[:, n % 2, 0, :], ACT.Silu
                                     ).then_inc(silu_done, 1)

        @block.vector
        def _(v):
            d = nc.vector
            for kind, n, k in order:
                if kind == "hid":
                    f, half = UNITS[n]
                    part = hid[:, f, half * BANK:(half + 1) * BANK]
                    v.wait_ge(silu_done, n + 1)
                    d.tensor_tensor(part, part, gu_ps[:, n % 2, 1, :], ALU.mult).then_inc(hid_ready, 1)
                    continue
                h = G.h[:, n, :]
                number = add_no[kind, n, k]
                if number:
                    v.wait_ge(added, number)
                if kind == "out":
                    v.wait_ge(y_ready, n + 1)
                    d.tensor_tensor(h, h, y_ps[:, n % 2, :], ALU.add).then_inc(added, 1)
                else:
                    if k == 0:
                        v.wait_ge(scaled, n + 1)
                    m = n * K + k
                    v.wait_ge(y_in[m % R], 16 * (m // R + 1))
                    d.scalar_tensor_tensor(out=h, in0=yr[:, m % R, :], scalar=G.w2[:, m:m + 1], in1=h,
                                           op0=ALU.mult, op1=ALU.add).then_inc(added, 1)


def program(nc, A, out):
    dram = lambda name, shape: nc.dram_tensor(name, shape, F32, kind="Internal").ap()
    qk_d = dram("qk_by_head", [2, HEADS, QK, S])
    v_d = dram("value_rows", [S, HEADS * VH])
    rows_d = dram("token_rows", [S, D])
    y_d = dram("expert_out", [(NB2 + 1) * P, D])
    with ExitStack() as ctx:
        G = persistent(nc, ctx)
        first = G.h
        second = ctx.enter_context(nc.sbuf_tensor("second", [P, T, D], F32))
        G.u, G.ya = second, first
        setup(nc, A, G)
        rms_to_cols(nc, G, vec(G, "norm_mix_g"), G.u)
        lru(nc, A, G, y_d)
        mla_project(nc, A, G, qk_d, v_d)
        with nc.sbuf_tensor("yb", [P, C, S], F32) as yb:
            G.yb = yb
            G.x2 = second[:]
            attention(nc, A, G, qk_d, v_d)
            merge(nc, A, G)
        G.h, G.u = second, first
        with ExitStack() as moe:
            moe_state(nc, moe, G, K1, E1)
            with (nc.sbuf_tensor("rows", [P, T, D], F32) as rows,
                  nc.sbuf_tensor("logits_1", [P, T, GROUPS1 + E1], F32) as logits):
                norm_rows(nc, A, G, rows, rows_d)
                rows_to_cols(nc, G, rows, G.u, logits[:], [(A["router_group_w"], GROUPS1),
                                                           (A["router_expert_w"], E1)])
                route1(nc, A, G, logits[:])
                dispatch(nc, G, K1, E1, NB1)
            experts(nc, G, E1, NB1, rows_d, A["w_gate"], A["w_up"], A["w_down"], y_d[0:(NB1 + 1) * P, :])
            combine(nc, G, K1, y_d[0:NB1 * P, :])
        rows_to_cols(nc, G, G.h, G.u)
        with nc.sbuf_tensor("mix", [P, C, S], F32) as mix:
            G.mix = mix
            hgrn(nc, A, G)
            pooling(nc, A, G)
            mix_out(nc, A, G)
        layer_norm(nc, G, A["ln1_g_2"], A["ln1_b_2"], rows_d)
        with ExitStack() as moe:
            moe_state(nc, moe, G, K2, E2)
            with nc.sbuf_tensor("logits_2", [P, T, E2], F32) as scores:
                rows_to_cols(nc, G, G.h, G.u, scores[:], [(A["w_router_2"], E2)])
                route2(nc, A, G, scores[:])
                dispatch(nc, G, K2, E2, NB2, scores[:])
            experts(nc, G, E2, NB2, rows_d, A["w_gate_2"], A["w_up_2"], A["w_down_2"], y_d)
            shared_and_combine(nc, A, G, G.u, y_d[0:NB2 * P, :])
        layer_norm(nc, G, A["ln2_g_2"], A["ln2_b_2"], out.rearrange("b s d -> (b s) d"))


def kernel(**inputs):
    import concourse.bacc as bacc
    from concourse.bass_utils import run_bass_kernel_spmd

    nc = bacc.Bacc("TRN2", target_bir_lowering=False, num_devices=1)
    arrays, aps = {}, {}
    for name, value in inputs.items():
        a = np.ascontiguousarray(value)
        arrays[f"in_{name}_dram"] = a
        aps[name] = nc.dram_tensor(f"in_{name}_dram", a.shape, mybir.dt.from_np(a.dtype), kind="ExternalInput").ap()
    out = nc.dram_tensor("out_dram", (1, S, D), F32, kind="ExternalOutput").ap()
    program(nc, aps, out)
    return run_bass_kernel_spmd(nc, [arrays], core_ids=[0]).results[0]["out_dram"]
```

```python
from contextlib import ExitStack

import numpy as np

import concourse.bass as bass
from concourse import mybir

F32 = mybir.dt.float32
I32 = mybir.dt.int32
U32 = mybir.dt.uint32
ALU = mybir.AluOpType
ACT = mybir.ActivationFunctionType
AX = mybir.AxisListType.X

P = 128
S = 1024
D = 1024
T = S // P
C = D // P
BANK = 512
HALF = S // BANK
EPS = 1e-6
LN_EPS = 1e-5
NEG = -1.0e30

LRU_W = 256
HEADS, NOPE, ROPE, VH = 16, 64, 32, 64
QK = NOPE + ROPE
Q_LORA, KV_LORA = 768, 256
ROPE_THETA = 10000.0
E1, GROUPS1, K1 = 32, 4, 2
E2, GROUPS2, K2, TOPG2 = 64, 8, 8, 4
F_EXP = 256
NB1 = (S * K1 + E1 * (P - 1)) // P
NB2 = (S * K2 + E2 * (P - 1)) // P
HG_HEADS = 4
HG_W = 512
POOL_W = 512
ALPHA = 2.0 ** 0.25
ROUTED_SCALE = 2.5


class Names:
    pass


def start_at_one(eng, *sems):
    for sem in sems:
        eng.sem_inc(sem, 1)


class Steps:

    def __init__(self, eng, sem, base=0):
        self.eng, self.sem, self.base, self.n = eng, sem, base, 0

    def __call__(self, ins):
        ins.then_inc(self.sem, 1)
        self.n += 1
        return self.n

    def join(self, n=None):
        self.eng.wait_ge(self.sem, self.base + (self.n if n is None else n))


def phase(nc):
    ctx = ExitStack()
    ns = Names()
    ns.ctx = ctx
    allocated = []

    def sems(names):
        allocated.extend(nc.alloc_semaphore(f"{name}_{n}") for name in names.split())
        return allocated[-len(names.split()):]

    def clear():
        nc.clear_and_free_semaphores(allocated)
        nc.all_engine_barrier()

    ctx.callback(clear)
    ns.sems = sems
    ns.n = n = nc.next_id()
    ns.sb = lambda name, shape, dt=F32: ctx.enter_context(nc.sbuf_tensor(f"{name}_{n}", shape, dt))
    ns.ps = lambda name, shape: ctx.enter_context(nc.psum_tensor(f"{name}_{n}", shape, F32))
    return ns


VECTORS = ("norm_mix_g:8 conv_w:32 conv_b:8 lru_ba:8 lru_bx:8 lru_lambda:8 q_a_g:6 kv_a_g:2 "
           "norm_ffn_g:8 hg_lb_logits_2:8 pool_scale_2:4")
VROW = {}
for _item in VECTORS.split():
    _name, _rows = _item.split(":")
    VROW[_name] = (sum(n for _, n in VROW.values()), int(_rows))
VROWS = sum(n for _, n in VROW.values())


def setup(nc, A, G):
    ph = phase(nc)
    with ph.ctx:
        vrow = ph.sb("vrow", [VROWS, P])
        posi = ph.sb("posi", [P, T], I32)
        posf = ph.sb("posf", [P, T])
        freq = ph.sb("freq", [P, ROPE // 2])
        ang = ph.sb("ang", [P, T, ROPE // 2])
        red = ph.sb("red", [P, T, ROPE // 2])
        turns = ph.sb("turns", [P, T, ROPE // 2])
        t1 = ph.sb("t1", [P, C])
        t2 = ph.sb("t2", [P, C])
        t3 = ph.sb("t3", [P, C])
        t4 = ph.sb("t4", [P, C])
        vps = ph.ps("vps", [P, P])
        (loaded, zeroed, made, vec_t, vec_ready, dve, act) = ph.sems(
            "loaded zeroed made vec_t vec_ready dve act")
        block = ph.ctx.enter_context(nc.Block())

        rowvecs = [(G.qg, A["q_norm_g"]), (G.kg, A["k_norm_g"])]
        N_LOADS = len(VROW) + 1 + len(rowvecs)

        @block.sync
        def _(sp):
            for name, (first, n) in VROW.items():
                src = A[name]
                if name == "conv_w":
                    src = src.rearrange("l w (c p) -> (l w c) p", p=P)
                else:
                    src = src.rearrange("l (c p) -> (l c) p", p=P)
                sp.dma_start(vrow[first:first + n, :], src).then_inc(loaded, 16)
            with nc.allow_non_contiguous_dma("1024 positions, once"):
                sp.dma_start(posi[:], A["positions"].rearrange("b (t p) -> p (b t)", p=P)).then_inc(loaded, 16)
            for dst, src in rowvecs:
                sp.dma_start(dst[:], src.to_broadcast([P, src.shape[1]])).then_inc(loaded, 16)
            for t in range(T):
                sp.dma_start(G.h[:, t, :], A["x"][0, t * P:(t + 1) * P, :]).then_inc(G.x_in[t], 16)

        @block.gpsimd
        def _(pool):
            g = nc.gpsimd
            st = Steps(pool, zeroed)
            st(g.memset(G.ident[:], 0.0))
            st(g.memset(G.ones[:], 1.0))
            st(g.memset(G.tri[:], 1.0))
            st.join()
            g.affine_select(out=G.ident[:], in_=G.ident[:], compare_op=ALU.not_equal, fill=1.0,
                            base=0, pattern=[[-1, P]], channel_multiplier=1).then_inc(made, 1)
            g.affine_select(out=G.tri[:], in_=G.tri[:], compare_op=ALU.is_gt, fill=0.0,
                            base=0, pattern=[[1, P]], channel_multiplier=-1).then_inc(made, 1)
            g.iota(G.iota[:], [[1, P]], base=0, channel_multiplier=0,
                   allow_small_or_imprecise_dtypes=True).then_inc(made, 1)
            g.iota(G.tok[:], [[P, T]], base=0, channel_multiplier=1,
                   allow_small_or_imprecise_dtypes=True).then_inc(made, 1)
            pool.wait_ge(made, 4)

        @block.tensor
        def _(pe):
            pe.wait_ge(loaded, 16 * N_LOADS)
            pe.wait_ge(made, 4)
            nc.tensor.transpose(vps[:, 0:VROWS], vrow[:], G.ident[0:VROWS, 0:VROWS]).then_inc(vec_t, 1)

        @block.vector
        def _(v):
            d = nc.vector
            st = Steps(v, dve)
            for i in range(ROPE // 2):
                st(d.memset(freq[:, i:i + 1], float(np.float32(ROPE_THETA ** (-i / (ROPE // 2))))))
            v.wait_ge(loaded, 16 * N_LOADS)
            st(d.tensor_scalar(G.qg[:], G.qg[:], -float(QK) ** -0.5, None, ALU.mult))
            st(d.tensor_copy(posf[:], posi[:]))
            st.join()
            st(d.tensor_tensor(ang[:], posf[:, :, None].to_broadcast([P, T, ROPE // 2]),
                               freq[:, None, :].to_broadcast([P, T, ROPE // 2]), ALU.mult))
            st.join()
            MAGIC = 1.5 * 2.0 ** 23
            PI2 = 2.0 * np.pi
            A1 = 6.28125
            A2 = float(np.float32(np.round((PI2 - A1) * 2.0 ** 22) / 2.0 ** 22))
            A3 = float(np.float32(PI2 - A1 - A2))
            for out, quarter in ((G.sin, 0.0), (G.cos, 0.25)):
                st(d.tensor_scalar(turns[:], ang[:], float(np.float32(1.0 / PI2)), quarter, ALU.mult, ALU.add))
                st.join()
                st(d.tensor_scalar(turns[:], turns[:], MAGIC, None, ALU.add))
                st.join()
                st(d.tensor_scalar(turns[:], turns[:], MAGIC, None, ALU.subtract))
                st.join()
                st(d.scalar_tensor_tensor(out=red[:], in0=turns[:], scalar=-A1, in1=ang[:],
                                          op0=ALU.mult, op1=ALU.add))
                st.join()
                st(d.scalar_tensor_tensor(out=red[:], in0=turns[:], scalar=-A2, in1=red[:],
                                          op0=ALU.mult, op1=ALU.add))
                st.join()
                st(d.scalar_tensor_tensor(out=red[:], in0=turns[:], scalar=-A3, in1=red[:],
                                          op0=ALU.mult, op1=ALU.add))
                st.join()
                st(d.tensor_scalar(red[:], red[:], quarter * PI2, 3.1415925, ALU.add, ALU.min))
                st.join()
                st(d.tensor_scalar(out[:], red[:], -3.1415925, None, ALU.max))
                st.join()
            v.wait_ge(vec_t, 1)
            d.tensor_copy(G.vec[:], vps[:, 0:VROWS]).then_inc(vec_ready, 1)
            v.wait_ge(act, 3)
            y, z, z2, acc = t1, t2, t3, t4
            st(d.tensor_scalar(z[:], y[:], 2.0, None, ALU.add))
            st.join()
            st(d.reciprocal(z[:], z[:]))
            st.join()
            st(d.tensor_tensor(z[:], z[:], y[:], ALU.mult))
            st.join()
            st(d.tensor_tensor(z2[:], z[:], z[:], ALU.mult))
            st(d.memset(acc[:], 1.0 / 17.0))
            st.join()
            for k in range(15, 0, -2):
                st(d.tensor_tensor(acc[:], acc[:], z2[:], ALU.mult))
                st.join()
                st(d.tensor_scalar(acc[:], acc[:], 1.0 / k, None, ALU.add))
                st.join()
            st(d.tensor_tensor(acc[:], acc[:], z[:], ALU.mult))
            first, n = VROW["lru_lambda"]
            st(d.tensor_scalar(z2[:], G.vec[:, first:first + n], -1.0, 0.0, ALU.mult, ALU.max))
            st.join()
            st(d.scalar_tensor_tensor(out=acc[:], in0=acc[:], scalar=2.0, in1=z2[:], op0=ALU.mult, op1=ALU.add))
            st.join()
            st(d.tensor_scalar(G.decay[:], acc[:], -8.0, None, ALU.mult))

        @block.scalar
        def _(a):
            a.wait_ge(vec_ready, 1)
            first, n = VROW["lru_lambda"]
            nc.scalar.activation(t1[:], G.vec[:, first:first + n], ACT.Abs).then_inc(act, 1)
            a.wait_ge(act, 1)
            nc.scalar.activation(t1[:], t1[:], ACT.Exp, scale=-1.0).then_inc(act, 1)
            nc.scalar.activation(G.sin[:], G.sin[:], ACT.Sin)
            nc.scalar.activation(G.cos[:], G.cos[:], ACT.Sin).then_inc(act, 1)


def vec(G, name):
    first, n = VROW[name]
    return G.vec[:, first:first + n]


def rms_to_cols(nc, G, gain, dst):
    ph = phase(nc)
    with ph.ctx:
        junk = ph.sb("junk", [P, D])
        ssq = ph.sb("ssq", [P, T])
        rstd = ph.sb("rstd", [P, T])
        xn = ph.sb("xn", [P, 2, D])
        tp = ph.ps("tp", [P, 2, C, P])
        squared, rooted, scaled, turned, taken, dve = ph.sems("squared rooted scaled turned taken dve")
        block = ph.ctx.enter_context(nc.Block())

        @block.scalar
        def _(a):
            for t in range(T):
                a.wait_ge(G.x_in[t], 16)
                if t:
                    a.wait_ge(squared, t)
                nc.scalar.activation(junk[:], G.h[:, t, :], ACT.Square,
                                     accum_out=ssq[:, t:t + 1]).then_inc(squared, 1)
            a.wait_ge(dve, 1)
            nc.scalar.activation(rstd[:], ssq[:], ACT.Sqrt).then_inc(rooted, 1)
            a.wait_ge(dve, 2)
            for t in range(T):
                if t >= 2:
                    a.wait_ge(turned, t - 1)
                nc.scalar.activation(xn[:, t % 2, :], G.h[:, t, :], ACT.Copy,
                                     scale=rstd[:, t:t + 1]).then_inc(scaled, 1)

        @block.tensor
        def _(pe):
            for t in range(T):
                pe.wait_ge(scaled, t + 1)
                if t >= 2:
                    pe.wait_ge(taken, t - 1)
                for c in range(C):
                    last = nc.tensor.transpose(tp[:, t % 2, c, :], xn[:, t % 2, c * P:(c + 1) * P], G.ident[:])
                last.then_inc(turned, 1)

        @block.vector
        def _(v):
            d = nc.vector
            v.wait_ge(squared, T)
            d.tensor_scalar(ssq[:], ssq[:], 1.0 / D, EPS, ALU.mult, ALU.add).then_inc(dve, 1)
            v.wait_ge(rooted, 1)
            d.reciprocal(rstd[:], rstd[:]).then_inc(dve, 1)
            for t in range(T):
                v.wait_ge(turned, t + 1)
                d.tensor_tensor(dst[:, :, t * P:(t + 1) * P], tp[:, t % 2, :, :],
                                gain[:, :, None].to_broadcast([P, C, P]), ALU.mult).then_inc(taken, 1)


def lru(nc, A, G, y_d):
    ph = phase(nc)
    B = LRU_W // P
    NBLK = D // LRU_W
    CONV = 4
    w_in = A["w_in"].rearrange("l (c p) n -> p (l c) n", p=P)
    wa_d = A["lru_wa"].rearrange("l b (c p) n -> (l b) p c n", p=P)
    wx_d = A["lru_wx"].rearrange("l b (c p) n -> (l b) p c n", p=P)
    with ph.ctx:
        wcol = ph.sb("wcol", [P, 3, C, LRU_W])
        wgate = ph.sb("wgate", [P, 2, B, LRU_W])
        xp = ph.sb("xp", [P, B, CONV - 1 + S])
        xa = ph.sb("xa", [P, B, S])
        rr = ph.sb("rr", [P, B, S])
        aa = ph.sb("aa", [P, B, S])
        pp = ph.sb("pp", [P, B, S])
        ii = ph.sb("ii", [P, B, S])
        hh = ph.sb("hh", [P, B, S])
        gelu = ph.sb("gelu", [P, B, S])
        gate = ph.sb("gate", [P, B, S])
        zero = ph.sb("zero", [P, D])
        ps = ph.ps("ps", [P, 2, B, S])
        (w0, w1, w2, wg_in, group_ready, group_taken, pad_ready, xa_ready, log_ready, p_ready,
         q_ready, root_ready, dve, act, block_done, cleared, zero_out) = ph.sems(
            "w0 w1 w2 wg_in group_ready group_taken pad_ready xa_ready log_ready p_ready "
            "q_ready root_ready dve act block_done cleared zero_out")
        w_in_sem = [w0, w1, w2]
        COL = [0, D, 2 * D + Q_LORA + KV_LORA + ROPE]
        GROUPS = 5
        block = ph.ctx.enter_context(nc.Block())

        @block.sync
        def _(sp):
            for k in range(3):
                sp.dma_start(wcol[:, k], w_in[:, :, COL[k]:COL[k] + LRU_W]).then_inc(w_in_sem[k], 16)
            sp.dma_start(wgate[:, 0], wa_d[0]).then_inc(wg_in, 16)
            sp.dma_start(wgate[:, 1], wx_d[0]).then_inc(wg_in, 16)
            with sp.Fori(0, NBLK - 1) as b:
                for k in range(3):
                    sp.wait_ge(group_ready, b * GROUPS + k + 1)
                    sp.dma_start(wcol[:, k], w_in[:, :, bass.ds((b + 1) * LRU_W + COL[k], LRU_W)]).then_inc(w_in_sem[k], 16)
                sp.wait_ge(group_ready, b * GROUPS + GROUPS)
                for k, src in enumerate((wa_d, wx_d)):
                    sp.dma_start(wgate[:, k], src[bass.ds(b + 1, 1)].rearrange("o p c n -> p (o c) n")).then_inc(wg_in, 16)

        @block.gpsimd
        def _(pool):
            nc.gpsimd.memset(zero[:], 0.0).then_inc(cleared, 1)
            pool.wait_ge(cleared, 1)
            spans = ((S * K1 // P, NB1), (S * K2 // P, NB2))
            for b0, b1 in spans:
                with pool.Fori(b0, b1) as b:
                    pool.dma_start(y_d[bass.ds(b * P, P), :], zero[:]).then_inc(zero_out, 16)
            pool.wait_ge(zero_out, 16 * sum(b1 - b0 for b0, b1 in spans))

        @block.tensor
        def _(pe):
            def in_group(b, m, k):
                slot = m % 2
                pe.wait_ge(w_in_sem[k], b * 16 + 16)
                for c in range(B):
                    for h in range(HALF):
                        for kc in range(C):
                            last = nc.tensor.matmul(ps[:, slot, c, h * BANK:(h + 1) * BANK],
                                                    wcol[:, k, kc, c * P:(c + 1) * P],
                                                    G.u[:, kc, h * BANK:(h + 1) * BANK],
                                                    start=kc == 0, stop=kc == C - 1)
                last.then_inc(group_ready, 1)

            def gate_group(b, m, k):
                slot = m % 2
                if k == 0:
                    pe.wait_ge(wg_in, b * 32 + 32)
                    pe.wait_ge(xa_ready, b + 1)
                for c in range(B):
                    for h in range(HALF):
                        for kc in range(B):
                            last = nc.tensor.matmul(ps[:, slot, c, h * BANK:(h + 1) * BANK],
                                                    wgate[:, k, kc, c * P:(c + 1) * P],
                                                    xa[:, kc, h * BANK:(h + 1) * BANK],
                                                    start=kc == 0, stop=kc == B - 1)
                last.then_inc(group_ready, 1)

            with pe.Fori(0, NBLK // 2) as j:
                for u in range(2):
                    b = j * 2 + u
                    for k in range(GROUPS):
                        m = u * GROUPS + k
                        pe.wait_ge(group_taken, 1 + j * (2 * GROUPS) + max(m - 1, 0))
                        if k < 3:
                            in_group(b, m, k)
                        else:
                            gate_group(b, m, k - 3)

        @block.scalar
        def _(a):
            s = nc.scalar
            start_at_one(a, group_taken)
            with a.Fori(0, NBLK // 2) as j:
                for u in range(2):
                    b = j * 2 + u
                    st = Steps(a, act, b * 3)
                    m = u * GROUPS
                    first = j * (2 * GROUPS) + m
                    a.wait_ge(group_ready, first + 1)
                    a.wait_ge(pad_ready, b + 1)
                    s.activation(xp[:, :, CONV - 1:], ps[:, m % 2], ACT.Copy).then_inc(group_taken, 1)
                    a.wait_ge(group_ready, first + 2)
                    a.wait_ge(block_done, 1 + b)
                    s.activation(gelu[:], ps[:, (m + 1) % 2], ACT.Gelu_apprx_tanh).then_inc(group_taken, 1)
                    a.wait_ge(group_ready, first + 3)
                    s.activation(gate[:], ps[:, (m + 2) % 2], ACT.Sigmoid).then_inc(group_taken, 1)
                    for k, (out, bias) in enumerate(((rr, vec(G, "lru_ba")), (ii, vec(G, "lru_bx")))):
                        a.wait_ge(group_ready, first + 4 + k)
                        for c in range(B):
                            last = s.activation(out[:, c, :], ps[:, (m + 3 + k) % 2, c, :], ACT.Sigmoid,
                                                bias=bias[:, bass.ds(b * B + c, 1)])
                            if c == B - 1:
                                last.then_inc(group_taken, 1)
                            else:
                                last.then_inc(act, 1)
                    a.wait_ge(log_ready, b + 1)
                    s.activation(pp[:], rr[:], ACT.Tanh, scale=-1.0).then_inc(p_ready, 1)
                    s.activation(aa[:], rr[:], ACT.Exp).then_inc(act, 1)
                    a.wait_ge(q_ready, b + 1)
                    s.activation(pp[:], pp[:], ACT.Sqrt).then_inc(root_ready, 1)

        @block.vector
        def _(v):
            d = nc.vector
            start_at_one(v, block_done)
            d.memset(xp[:, :, 0:CONV - 1], 0.0).then_inc(pad_ready, 1)
            N_STEPS = B * CONV - 1 + 1 + 1 + 2 + B + 1
            with v.Fori(0, NBLK) as b:
                st = Steps(v, dve, b * N_STEPS)
                v.wait_ge(group_taken, 1 + b * GROUPS + 1)
                v.wait_ge(pad_ready, b + 1)
                for k in range(CONV):
                    for c in range(B):
                        wk = vec(G, "conv_w")[:, bass.ds(b * B + (k * C + c), 1)]
                        if k == 0:
                            ins = d.tensor_scalar(xa[:, c, :], xp[:, c, 0:S], wk,
                                                  vec(G, "conv_b")[:, bass.ds(b * B + c, 1)], ALU.mult, ALU.add)
                        else:
                            st.join(st.n - 1)
                            ins = d.scalar_tensor_tensor(out=xa[:, c, :], in0=xp[:, c, k:k + S], scalar=wk,
                                                         in1=xa[:, c, :], op0=ALU.mult, op1=ALU.add)
                        if k == CONV - 1 and c == B - 1:
                            ins.then_inc(xa_ready, 1)
                        else:
                            st(ins)
                v.wait_ge(xa_ready, b + 1)
                d.memset(xp[:, :, 0:CONV - 1], 0.0).then_inc(pad_ready, 1)
                v.wait_ge(group_taken, 1 + b * GROUPS + 4)
                v.wait_ge(act, b * 3 + 1)
                st(d.tensor_scalar(rr[:, 0, :], rr[:, 0, :], G.decay[:, bass.ds(b * B, 1)], None, ALU.mult))
                d.tensor_scalar(rr[:, 1, :], rr[:, 1, :], G.decay[:, bass.ds(b * B + 1, 1)], None,
                                ALU.mult).then_inc(log_ready, 1)
                v.wait_ge(act, b * 3 + 3)
                st(d.tensor_tensor(hh[:], aa[:], aa[:], ALU.mult))
                st.join()
                v.wait_ge(p_ready, b + 1)
                d.scalar_tensor_tensor(out=pp[:], in0=hh[:], scalar=1.0, in1=pp[:], op0=ALU.add,
                                       op1=ALU.mult).then_inc(q_ready, 1)
                v.wait_ge(group_taken, 1 + b * GROUPS + 5)
                st(d.tensor_tensor(ii[:], ii[:], xa[:], ALU.mult))
                st.join()
                v.wait_ge(root_ready, b + 1)
                st(d.tensor_tensor(ii[:], ii[:], pp[:], ALU.mult))
                st.join()
                for c in range(B):
                    st(d.tensor_tensor_scan(hh[:, c, :], aa[:, c, :], ii[:, c, :], 0.0, ALU.mult, ALU.add))
                st.join()
                st(d.tensor_tensor(hh[:], hh[:], gelu[:], ALU.mult))
                st.join()
                d.tensor_tensor(G.ya[:, bass.ds(b * B, B), :], hh[:], gate[:], ALU.mult).then_inc(block_done, 1)
                assert st.n == N_STEPS, st.n


def persistent(nc, ctx):
    G = Names()
    sb = lambda name, shape, dt=F32: ctx.enter_context(nc.sbuf_tensor(name, shape, dt))
    G.h = sb("h", [P, T, D])
    G.vec = sb("vec", [P, VROWS])
    G.ident = sb("ident", [P, P])
    G.ones = sb("ones", [P, P])
    G.tri = sb("tri", [P, P])
    G.iota = sb("iota", [P, P])
    G.tok = sb("tok", [P, T])
    G.qg = sb("qg", [P, QK])
    G.kg = sb("kg", [P, QK])
    G.sin = sb("sin", [P, T, ROPE // 2])
    G.cos = sb("cos", [P, T, ROPE // 2])
    G.decay = sb("decay", [P, C])
    return G


def mla_project(nc, A, G, qk_d, v_d):
    ph = phase(nc)
    QC = Q_LORA // P
    KC = KV_LORA // P
    IN_W = Q_LORA + KV_LORA + ROPE
    HALF_Q = Q_LORA // 2
    KV_W = KV_LORA + ROPE
    H2 = ROPE // 2
    GROUP_HEADS = BANK // (NOPE + VH)
    NQ, NKV = HEADS * QK // BANK, HEADS * (NOPE + VH) // BANK
    TURN = 4
    with ph.ctx:
        w_low = ph.sb("w_low", [P, C, IN_W])
        w_uq = ph.sb("w_uq", [P, QC, HEADS * QK])
        w_ukv = ph.sb("w_ukv", [P, KC, HEADS * (NOPE + VH)])
        low = ph.sb("low", [P, Q_LORA + KV_LORA])
        kpe = ph.sb("kpe", [P, 2, ROPE])
        low_t = ph.sb("low_t", [P, QC + KC, P])
        gains = ph.sb("gains", [P, QC + KC])
        qk = ph.sb("qk", [P, 2, HEADS, QK])
        sq = ph.sb("sq", [P, 2, HEADS, QK])
        vv = ph.sb("vv", [P, HEADS, VH])
        stage = ph.sb("stage", [QK, 2, 2 * TURN, P])
        ss = ph.sb("ss", [P, 2])
        hs = ph.sb("hs", [P, 2, HEADS])
        qk_flat = qk[:].rearrange("p s h d -> p (s h d)")
        sq_low = ph.sb("sq_low", [P, Q_LORA + KV_LORA])
        rot_all = ph.sb("rot_all", [P, 4, HEADS, H2])
        rot = [rot_all[:, i] for i in range(4)]
        acc = ph.ps("acc", [P, 4, BANK])
        tr = ph.ps("tr", [P, QC + KC, P])
        ht = ph.ps("ht", [P, 2, TURN, P])
        (w_in0, w_in1, w_in2, acc_ready, acc_taken, row_sq, row_ms, row_rt, row_ok, tr_ready,
         tr_taken, q_sq, qk_sq, qk_ms, qk_rt, qk_ok, ht_ready, ht_taken, v_out, st_out0,
         st_out1, dve, act) = ph.sems(
            "w_in0 w_in1 w_in2 acc_ready acc_taken row_sq row_ms row_rt row_ok tr_ready tr_taken "
            "q_sq qk_sq qk_ms qk_rt qk_ok ht_ready ht_taken v_out st_out0 st_out1 dve act")
        st_out = [st_out0, st_out1]
        block = ph.ctx.enter_context(nc.Block())
        PER = 3 + NQ + NKV
        TURNS = 2 * HEADS // TURN

        order = [("low", 0, k) for k in range(3)]
        for t in range(T):
            if t + 1 < T:
                order += [("low", t + 1, k) for k in range(3)]
            order += [("up", t, k) for k in range(NQ + NKV)]
        number = {key: n for n, key in enumerate(order)}

        @block.sync
        def _(sp):
            w = A["w_in"].rearrange("l (c p) n -> p (l c) n", p=P)
            sp.dma_start(w_low[:], w[:, :, 2 * D:2 * D + IN_W]).then_inc(w_in0, 16)
            sp.dma_start(w_uq[:], A["w_uq"].rearrange("l (c p) n -> p (l c) n", p=P)).then_inc(w_in1, 16)
            sp.dma_start(w_ukv[:], A["w_ukv"].rearrange("l (c p) n -> p (l c) n", p=P)).then_inc(w_in2, 16)
            for t in range(T):
                sp.wait_ge(acc_taken, number["up", t, NQ + NKV - 1] + 1)
                sp.dma_start(v_d[t * P:(t + 1) * P, :], vv[:].rearrange("p h d -> p (h d)")).then_inc(v_out, 16)
                for n in range(TURNS // 2):
                    sp.wait_ge(ht_taken, t * TURNS + 2 * n + 2)
                    s, first = divmod(n * 2 * TURN, HEADS)
                    sp.dma_start(qk_d[s, first:first + 2 * TURN, :, t * P:(t + 1) * P].rearrange("h p t -> p h t"),
                                 stage[:, n % 2]).then_inc(st_out[n % 2], 16)
            sp.wait_ge(v_out, 16 * T)
            for q in st_out:
                sp.wait_ge(q, 16 * T * TURNS // 4)

        @block.tensor
        def _(pe):
            def low_groups(t):
                if t == 0:
                    pe.wait_ge(w_in0, 16)
                for k in range(3):
                    n = number["low", t, k]
                    if n >= 4:
                        pe.wait_ge(acc_taken, n - 3)
                    c0 = k * HALF_Q
                    width = HALF_Q if k < 2 else KV_W
                    for kc in range(C):
                        last = nc.tensor.matmul(acc[:, n % 4, 0:width], G.u[:, kc, t * P:(t + 1) * P],
                                                w_low[:, kc, c0:c0 + width], start=kc == 0, stop=kc == C - 1)
                    last.then_inc(acc_ready, 1)

            def turn_low(t):
                pe.wait_ge(row_ok, t + 1)
                if t:
                    pe.wait_ge(tr_taken, t)
                for c in range(QC + KC):
                    last = nc.tensor.transpose(tr[:, c, :], low[:, c * P:(c + 1) * P], G.ident[:])
                last.then_inc(tr_ready, 1)

            def up_groups(t):
                if t == 0:
                    pe.wait_ge(w_in1, 16)
                    pe.wait_ge(w_in2, 16)
                pe.wait_ge(tr_taken, t + 1)
                for k in range(NQ + NKV):
                    if k == NQ and t:
                        turn_heads(t - 1)
                    n = number["up", t, k]
                    pe.wait_ge(acc_taken, n - 3)
                    chunks = range(QC) if k < NQ else range(QC, QC + KC)
                    for kc in chunks:
                        rhs = (w_uq[:, kc, k * BANK:(k + 1) * BANK] if k < NQ else
                               w_ukv[:, kc - QC, (k - NQ) * BANK:(k - NQ + 1) * BANK])
                        last = nc.tensor.matmul(acc[:, n % 4, :], low_t[:, kc, :], rhs,
                                                start=kc == chunks[0], stop=kc == chunks[-1])
                    last.then_inc(acc_ready, 1)

            def turn_heads(t):
                for n in range(TURNS):
                    if n % (TURNS // 2) == 0:
                        pe.wait_ge(qk_ok, 2 * t + n // (TURNS // 2) + 1)
                    m = t * TURNS + n
                    if m >= 2:
                        pe.wait_ge(ht_taken, m - 1)
                    for i in range(TURN):
                        s, head = divmod(n * TURN + i, HEADS)
                        last = nc.tensor.transpose(ht[0:QK, n % 2, i, :], qk[:, s, head, :], G.ident[:])
                    last.then_inc(ht_ready, 1)

            low_groups(0)
            for t in range(T):
                turn_low(t)
                if t + 1 < T:
                    low_groups(t + 1)
                up_groups(t)
            turn_heads(T - 1)

        @block.scalar
        def _(a):
            s = nc.scalar
            st = Steps(a, act)

            def take_low(t):
                if t:
                    a.wait_ge(tr_ready, t)
                for k in range(3):
                    n = number["low", t, k]
                    a.wait_ge(acc_ready, n + 1)
                    c0 = k * HALF_Q
                    if k == 2:
                        if t >= 2:
                            a.wait_ge(qk_sq, t - 1)
                        st(s.activation(kpe[:, t % 2, :], acc[:, n % 4, KV_LORA:KV_W], ACT.Copy))
                    width = HALF_Q if k < 2 else KV_LORA
                    s.activation(low[:, c0:c0 + width], acc[:, n % 4, 0:width], ACT.Copy).then_inc(acc_taken, 1)
                a.wait_ge(acc_taken, number["low", t, 2] + 1)
                st(s.activation(sq_low[:, 0:Q_LORA], low[:, 0:Q_LORA], ACT.Square, accum_out=ss[:, 0:1]))
                s.activation(sq_low[:, Q_LORA:], low[:, Q_LORA:], ACT.Square,
                             accum_out=ss[:, 1:2]).then_inc(row_sq, 1)
                a.wait_ge(row_ms, t + 1)
                s.activation(ss[:], ss[:], ACT.Sqrt).then_inc(row_rt, 1)

            def take_up(t):
                if t:
                    a.wait_ge(ht_ready, t * TURNS)
                    a.wait_ge(v_out, 16 * t)
                for k in range(NQ + NKV):
                    n = number["up", t, k]
                    a.wait_ge(acc_ready, n + 1)
                    if k < NQ:
                        s.activation(qk_flat[:, k * BANK:(k + 1) * BANK], acc[:, n % 4, :],
                                     ACT.Copy).then_inc(acc_taken, 1)
                        continue
                    head = (k - NQ) * GROUP_HEADS
                    src = acc[:, n % 4, :].rearrange("p (h d) -> p h d", d=NOPE + VH)
                    st(s.activation(qk[:, 1, head:head + GROUP_HEADS, 0:NOPE], src[:, :, 0:NOPE], ACT.Copy))
                    s.activation(vv[:, head:head + GROUP_HEADS, :], src[:, :, NOPE:],
                                 ACT.Copy).then_inc(acc_taken, 1)
                    if k == NQ:
                        a.wait_ge(acc_taken, number["up", t, NQ - 1] + 1)
                        s.activation(sq[:, 0], qk[:, 0], ACT.Square).then_inc(q_sq, 1)
                st(s.activation(qk[:, 1, :, NOPE:], kpe[:, t % 2, None, :].to_broadcast([P, HEADS, ROPE]), ACT.Copy))
                a.wait_ge(acc_taken, number["up", t, NQ + NKV - 1] + 1)
                st.join()
                s.activation(sq[:, 1], qk[:, 1], ACT.Square).then_inc(qk_sq, 1)

            def take_heads(t):
                for n in range(TURNS):
                    m = t * TURNS + n
                    a.wait_ge(ht_ready, m + 1)
                    d = (m // 2)
                    if n % 2 == 0 and d >= 2:
                        a.wait_ge(st_out[(n // 2) % 2], 16 * (d // 2))
                    s.activation(stage[:, (n // 2) % 2, (n % 2) * TURN:(n % 2 + 1) * TURN, :],
                                 ht[0:QK, n % 2], ACT.Copy).then_inc(ht_taken, 1)

            def root_heads(t):
                for i in range(2):
                    a.wait_ge(qk_ms, 2 * t + i + 1)
                    s.activation(hs[:, i], hs[:, i], ACT.Sqrt).then_inc(qk_rt, 1)

            take_low(0)
            for t in range(T):
                if t:
                    root_heads(t - 1)
                if t + 1 < T:
                    take_low(t + 1)
                if t:
                    take_heads(t - 1)
                take_up(t)
            root_heads(T - 1)
            take_heads(T - 1)

        @block.vector
        def _(v):
            d = nc.vector
            st = Steps(v, dve)
            st(d.tensor_copy(gains[:, 0:QC], vec(G, "q_a_g")))
            st(d.tensor_copy(gains[:, QC:], vec(G, "kv_a_g")))
            st.join()

            def scale_rows(t):
                v.wait_ge(row_sq, t + 1)
                st(d.tensor_scalar(ss[:, 0:1], ss[:, 0:1], 1.0 / Q_LORA, EPS, ALU.mult, ALU.add))
                d.tensor_scalar(ss[:, 1:2], ss[:, 1:2], 1.0 / KV_LORA, EPS, ALU.mult, ALU.add).then_inc(row_ms, 1)
                v.wait_ge(row_rt, t + 1)
                st(d.reciprocal(ss[:], ss[:]))
                st.join()
                st(d.tensor_scalar(low[:, 0:Q_LORA], low[:, 0:Q_LORA], ss[:, 0:1], None, ALU.mult))
                d.tensor_scalar(low[:, Q_LORA:], low[:, Q_LORA:], ss[:, 1:2], None, ALU.mult).then_inc(row_ok, 1)

            def take_turned(t):
                v.wait_ge(tr_ready, t + 1)
                if t:
                    v.wait_ge(acc_ready, number["up", t - 1, NQ + NKV - 1] + 1)
                d.tensor_tensor(low_t[:], tr[:], gains[:, :, None].to_broadcast([P, QC + KC, P]),
                                ALU.mult).then_inc(tr_taken, 1)

            def norm_heads(t):
                for i, squares in enumerate((q_sq, qk_sq)):
                    v.wait_ge(squares, t + 1)
                    st(d.tensor_reduce(hs[:, i], sq[:, i], AX, ALU.add))
                    st.join()
                    d.tensor_scalar(hs[:, i], hs[:, i], 1.0 / QK, EPS, ALU.mult, ALU.add).then_inc(qk_ms, 1)
                for i, g in enumerate((G.qg, G.kg)):
                    x = qk[:, i]
                    v.wait_ge(qk_rt, 2 * t + i + 1)
                    st(d.reciprocal(hs[:, i], hs[:, i]))
                    st.join()
                    st(d.tensor_tensor(x, x, hs[:, i, :, None].to_broadcast([P, HEADS, QK]), ALU.mult))
                    st.join()
                    st(d.tensor_tensor(x, x, g[:, None, :].to_broadcast([P, HEADS, QK]), ALU.mult))
                    st.join()
                    x1, x2 = x[:, :, NOPE:NOPE + H2], x[:, :, NOPE + H2:]
                    cos = G.cos[:, t, None, :].to_broadcast([P, HEADS, H2])
                    sin = G.sin[:, t, None, :].to_broadcast([P, HEADS, H2])
                    st(d.tensor_tensor(rot[0], x1, cos, ALU.mult))
                    st(d.tensor_tensor(rot[1], x2, sin, ALU.mult))
                    st(d.tensor_tensor(rot[2], x1, sin, ALU.mult))
                    st(d.tensor_tensor(rot[3], x2, cos, ALU.mult))
                    st.join()
                    st(d.tensor_tensor(x1, rot[0], rot[1], ALU.subtract))
                    d.tensor_tensor(x2, rot[2], rot[3], ALU.add).then_inc(qk_ok, 1)

            scale_rows(0)
            for t in range(T):
                take_turned(t)
                if t:
                    norm_heads(t - 1)
                if t + 1 < T:
                    scale_rows(t + 1)
            norm_heads(T - 1)


def attention(nc, A, G, qk_d, v_d):
    ph = phase(nc)
    ROUND = 8
    ROUNDS = HEADS // ROUND
    CHUNK = 64
    ORDER = [7, 0, 6, 1, 5, 2, 4, 3]
    N = ROUND * T
    turns = []
    for i in range(N):
        turns.append(("probs", i))
        if i >= 2 * T and (i - 1) % (2 * T) == 0:
            turns.append(("out", (i - 1) // (2 * T) - 1))
    turns.append(("out", ROUND // 2 - 1))
    a_turns = [x for x in turns if x[0] == "out" or x[1] % 2 == 0]
    a_no = {x: n for n, x in enumerate(a_turns)}
    b_no = {x: n for n, x in enumerate(turns)}
    A_ALL, B_ALL = len(a_turns), len(turns)
    with ph.ctx:
        qk = ph.sb("qk", [QK, 2, 2, S])
        vv = ph.sb("vv", [P, 2, T, VH])
        prob = ph.sb("prob", [P, 2, S])
        prob_t = ph.sb("prob_t", [P, 2, T, P])
        o_rows = ph.sb("o_rows", [P, T, 2 * VH])
        shift = ph.sb("shift", [P, 4])
        total = ph.sb("total", [P, 16])
        inv = ph.sb("inv", [P, T])
        early = ph.sb("early", [1, P])
        hide = ph.sb("hide", [1, CHUNK])
        wide = ph.ps("wide", [P, 2, S])
        narrow = ph.ps("narrow", [P, BANK])
        turn_a = ph.ps("turn_a", [P, 4, P])
        turn_b = ph.ps("turn_b", [P, 4, P])
        o_ps = ph.ps("o_ps", [P, T, VH])
        (qk_in0, qk_in1, v_in0, v_in1, sc_ready, max_ready, exp_done, a_ready, a_taken, b_ready,
         b_taken, o_ready, o_taken, inv_ready, cleared) = ph.sems(
            "qk_in0 qk_in1 v_in0 v_in1 sc_ready max_ready exp_done a_ready a_taken b_ready b_taken "
            "o_ready o_taken inv_ready cleared")
        qk_in, v_in = [qk_in0, qk_in1], [v_in0, v_in1]
        block = ph.ctx.enter_context(nc.Block())
        v_rows = v_d.rearrange("(t p) (h d) -> h p t d", p=P, d=VH)
        qk_h = qk_d.rearrange("s h p t -> h p s t")

        def scores_of(s):
            n = (ORDER[s % T] + 1) * P
            return wide[:, s // 2 % 2, 0:n] if s % 2 == 0 else narrow[:, 0:n]

        def total_of(s):
            c = s // T % 2 * T + ORDER[s % T]
            return total[:, c:c + 1]

        @block.sync
        def _(sp):
            def load(head, u):
                sp.dma_start(qk[:, u], qk_h[bass.ds(head, 1)].rearrange("o p s t -> p (o s) t")).then_inc(qk_in[u], 16)

            def load_values(head, u):
                sp.dma_start(vv[:, u], v_rows[bass.ds(head, 1)].rearrange("o p t d -> p (o t) d")).then_inc(v_in[u], 16)

            def reload(j, u):
                sp.wait_ge(sc_ready, j * N + (u + 1) * T)
                load(j * ROUND + (u + 2), u % 2)
                sp.wait_ge(o_ready, j * N + (u + 1) * T)
                load_values(j * ROUND + (u + 2), u % 2)

            for u in range(2):
                load(u, u)
                load_values(u, u)
            with sp.Fori(0, ROUNDS - 1) as j:
                for u in range(ROUND):
                    reload(j, u)
            for u in range(ROUND - 2):
                reload(ROUNDS - 1, u)

        @block.gpsimd
        def _(pool):
            nc.gpsimd.memset(early[:, 0:CHUNK], 1.0).then_inc(cleared, 1)
            nc.gpsimd.memset(early[:, CHUNK:], 0.0).then_inc(cleared, 1)
            nc.gpsimd.memset(hide[:], -NEG).then_inc(cleared, 1)

        @block.tensor
        def _(pe):
            pe.wait_ge(cleared, 3)
            with pe.Fori(0, ROUNDS) as j:
                def scores(s):
                    u, t = s // T, ORDER[s % T]
                    if s % T == 0:
                        pe.wait_ge(qk_in[u % 2], j * (ROUND // 2 * 16) + (u // 2 * 16 + 16))
                    out, n = scores_of(s), (t + 1) * P
                    for c0 in range(0, n, BANK):
                        w = min(BANK, n - c0)
                        nc.tensor.matmul(out[:, c0:c0 + w], qk[:, u % 2, 0, t * P:(t + 1) * P],
                                         qk[:, u % 2, 1, c0:c0 + w], start=True, stop=c0 + w < n)
                    nc.tensor.matmul(out[:, n - CHUNK:n], early[:], hide[:], start=False, stop=True
                                     ).then_inc(sc_ready, 1)

                def turn_probs(s):
                    t, what = ORDER[s % T], ("probs", s)
                    pe.wait_ge(exp_done, j * N + (s + 1))
                    blocks = [prob[:, s % 2, b * P:(b + 1) * P] for b in range(t + 1)]
                    if s % 2 == 0:
                        pe.wait_ge(a_taken, 1 + j * A_ALL + a_no[what])
                        for b in range(4):
                            last = nc.tensor.transpose(turn_a[:, b, :], blocks[b], G.ident[:])
                        last.then_inc(a_ready, 1)
                        blocks = blocks[4:]
                    pe.wait_ge(b_taken, 1 + j * B_ALL + b_no[what])
                    for b, src in enumerate(blocks):
                        last = nc.tensor.transpose(turn_b[:, b, :], src, G.ident[:])
                    last.then_inc(b_ready, 1)

                def values(s):
                    u, t, what = s // T, ORDER[s % T], ("probs", s)
                    if s % T == 0:
                        pe.wait_ge(v_in[u % 2], j * (ROUND // 2 * 16) + (u // 2 * 16 + 16))
                    if s % T == 0:
                        pe.wait_ge(o_taken, 1 + j * ROUND + u)
                    if s % 2 == 0:
                        pe.wait_ge(a_taken, 1 + j * A_ALL + (a_no[what] + 1))
                    pe.wait_ge(b_taken, 1 + j * B_ALL + (b_no[what] + 1))
                    for b in range(t + 1):
                        last = nc.tensor.matmul(o_ps[:, t, :], prob_t[:, s % 2, b, :],
                                                vv[:, u % 2, b, :], start=b == 0, stop=b == t)
                    last.then_inc(o_ready, 1)

                def turn_out(p):
                    what = ("out", p)
                    pe.wait_ge(o_taken, 1 + j * ROUND + (p + 1) * 2)
                    pe.wait_ge(a_taken, 1 + j * A_ALL + a_no[what])
                    for b in range(4):
                        last = nc.tensor.transpose(turn_a[:, b, :], o_rows[:, b, :], G.ident[:])
                    last.then_inc(a_ready, 1)
                    pe.wait_ge(b_taken, 1 + j * B_ALL + b_no[what])
                    for b in range(4):
                        last = nc.tensor.transpose(turn_b[:, b, :], o_rows[:, 4 + b, :], G.ident[:])
                    last.then_inc(b_ready, 1)

                scores(0)
                scores(1)
                for i in range(N):
                    turn_probs(i)
                    if i + 2 < N:
                        scores(i + 2)
                    if i:
                        values(i - 1)
                    for kind, p in turns[b_no["probs", i] + 1:][:1]:
                        if kind == "out" and i + 1 < N:
                            turn_out(p)
                values(N - 1)
                turn_out(ROUND // 2 - 1)

        @block.scalar
        def _(a):
            start_at_one(a, a_taken)
            with a.Fori(0, ROUNDS) as j:
                def exps(s):
                    n = (ORDER[s % T] + 1) * P
                    a.wait_ge(max_ready, j * N + (s + 1))
                    nc.scalar.activation(prob[:, s % 2, 0:n], scores_of(s), ACT.Exp, bias=shift[:, s % 4:s % 4 + 1],
                                         scale=-1.0, accum_out=total_of(s)).then_inc(exp_done, 1)

                exps(0)
                exps(1)
                for kind, n in turns:
                    if (kind, n) in a_no:
                        a.wait_ge(a_ready, j * A_ALL + (a_no[kind, n] + 1))
                    if kind == "out":
                        nc.scalar.activation(
                            G.yb[:, bass.ds(j * (ROUND // 2) + n, 1), 0:4 * P].rearrange("p o (b t) -> p (o b) t", t=P),
                            turn_a[:], ACT.Copy).then_inc(a_taken, 1)
                        continue
                    if n % 2 == 0:
                        if n >= 2:
                            a.wait_ge(o_ready, j * N + (n - 1))
                        nc.scalar.activation(prob_t[:, n % 2, 0:4, :], turn_a[:], ACT.Copy).then_inc(a_taken, 1)
                    if n + 2 < N:
                        a.wait_ge(b_ready, j * B_ALL + (b_no[kind, n] + 1))
                        exps(n + 2)

        @block.vector
        def _(v):
            d = nc.vector
            start_at_one(v, b_taken, o_taken)
            with v.Fori(0, ROUNDS) as j:
                def tops(s):
                    v.wait_ge(sc_ready, j * N + (s + 1))
                    d.tensor_reduce(shift[:, s % 4:s % 4 + 1], scores_of(s), AX, ALU.min).then_inc(max_ready, 1)

                def scale_out(u):
                    v.wait_ge(o_ready, j * N + (u + 1) * T)
                    d.reciprocal(inv[:], total[:, u % 2 * T:(u % 2 + 1) * T]).then_inc(inv_ready, 1)
                    v.wait_ge(inv_ready, j * ROUND + (u + 1))
                    d.tensor_tensor(o_rows[:, :, u % 2 * VH:(u % 2 + 1) * VH], o_ps[:],
                                    inv[:, :, None].to_broadcast([P, T, VH]), ALU.mult).then_inc(o_taken, 1)

                tops(0)
                tops(1)
                for kind, n in turns[:-1]:
                    if kind == "probs" and n > T and n % T == 1:
                        scale_out(n // T - 1)
                    v.wait_ge(b_ready, j * B_ALL + (b_no[kind, n] + 1))
                    if kind == "out":
                        d.tensor_copy(G.yb[:, bass.ds(j * (ROUND // 2) + n, 1), 4 * P:]
                                      .rearrange("p o (b t) -> p (o b) t", t=P), turn_b[:]).then_inc(b_taken, 1)
                        continue
                    t = ORDER[n % T]
                    if n >= 2:
                        v.wait_ge(o_ready, j * N + (n - 1))
                    if n % 2 == 0:
                        d.tensor_copy(prob_t[:, n % 2, 4:t + 1, :], turn_b[:, 0:t - 3, :]).then_inc(b_taken, 1)
                    else:
                        d.tensor_copy(prob_t[:, n % 2, 0:t + 1, :], turn_b[:, 0:t + 1, :]).then_inc(b_taken, 1)
                    if n + 2 < N:
                        tops(n + 2)
                scale_out(ROUND - 1)
                v.wait_ge(b_ready, j * B_ALL + B_ALL)
                d.tensor_copy(G.yb[:, bass.ds(j * (ROUND // 2) + (ROUND // 2 - 1), 1), 4 * P:]
                              .rearrange("p o (b t) -> p (o b) t", t=P), turn_b[:]).then_inc(b_taken, 1)


def merge(nc, A, G, rows_d, logits):
    ph = phase(nc)
    COL = 2 * D + Q_LORA + KV_LORA + ROPE + D
    HC = C // 2
    with ph.ctx:
        w_gate = ph.sb("w_gate", [P, 2, C, D // 4])
        w_out = ph.sb("w_out", [P, C, D])
        gate = ph.sb("gate", [P, 2, S])
        ps = ph.ps("ps", [P, 2, S])
        ps_o = ph.ps("ps_o", [P, 2, D])
        W_ROUTE = GROUPS1 + E1
        w_route = ph.sb("w_route", [P, C, W_ROUTE])
        gain = ph.sb("gain", [P, D])
        junk = ph.sb("junk", [P, D])
        rows = ph.sb("rows", [P, 2, D])
        rstd = ph.sb("rstd", [P, T])
        tp = ps[:, 0, :].rearrange("p (c t) -> p c t", t=P)
        lps = ps[:, 1, 0:T * W_ROUTE].rearrange("p (t n) -> p t n", n=W_ROUTE)
        (wr_in, gain_in, squared, mean, rooted, rows_ready, turned, cols_ready, routed, row_out0, row_out1) = ph.sems(
            "wr_in gain_in squared mean rooted rows_ready turned cols_ready routed row_out0 row_out1")
        row_out = [row_out0, row_out1]
        (wg0, wg1, wo_in, x_in, g_ready, g_taken, m_ready, o_ready, o_taken, dve) = ph.sems(
            "wg0 wg1 wo_in x_in g_ready g_taken m_ready o_ready o_taken dve")
        wg = [wg0, wg1]
        block = ph.ctx.enter_context(nc.Block())
        Q = 4
        PERQ = C // Q

        @block.sync
        def _(sp):
            w = A["w_in"].rearrange("l (c p) n -> p (l c) n", p=P)
            for q in range(Q):
                if q >= 2:
                    sp.wait_ge(g_ready, (q - 1) * PERQ)
                c0 = COL + q * (D // Q)
                sp.dma_start(w_gate[:, q % 2], w[:, :, c0:c0 + D // Q]).then_inc(wg[q % 2], 16)
                if q == 1:
                    sp.dma_start(w_out[:], A["w_out"].rearrange("l (c p) n -> p (l c) n", p=P)).then_inc(wo_in, 16)
            sp.wait_ge(g_ready, C)
            sp.dma_start(G.x2, A["x"].rearrange("b (t p) d -> p (b t) d", p=P)).then_inc(x_in, 16)
            sp.dma_start(gain[:], A["norm_ffn_g"].to_broadcast([P, D])).then_inc(gain_in, 16)
            c0 = 0
            with nc.allow_non_contiguous_dma("small router matrices"):
                for name, n in (("router_group_w", GROUPS1), ("router_expert_w", E1)):
                    sp.dma_start(w_route[:, :, c0:c0 + n], A[name].rearrange("l (c p) n -> p (l c) n", p=P)
                                 ).then_inc(wr_in, 16)
                    c0 += n
            for t in range(T):
                sp.wait_ge(rows_ready, t + 1)
                sp.dma_start(rows_d[t * P:(t + 1) * P, :], rows[:, t % 2, :]).then_inc(row_out[t % 2], 16)
            for q in row_out:
                sp.wait_ge(q, 16 * T // 2)

        @block.tensor
        def _(pe):
            for c in range(C):
                q, i = divmod(c, PERQ)
                if i == 0:
                    pe.wait_ge(wg[q % 2], 16 * (q // 2 + 1))
                if c >= 2:
                    pe.wait_ge(g_taken, c - 1)
                for h in range(HALF):
                    for kc in range(C):
                        last = nc.tensor.matmul(ps[:, c % 2, h * BANK:(h + 1) * BANK],
                                                w_gate[:, q % 2, kc, i * P:(i + 1) * P],
                                                G.u[:, kc, h * BANK:(h + 1) * BANK],
                                                start=kc == 0, stop=kc == C - 1)
                last.then_inc(g_ready, 1)
            def turn(t):
                pe.wait_ge(rows_ready, t + 1)
                if t:
                    pe.wait_ge(cols_ready, t)
                for c in range(C):
                    last = nc.tensor.transpose(tp[:, c, :], rows[:, t % 2, c * P:(c + 1) * P], G.ident[:])
                last.then_inc(turned, 1)

            def route(t):
                if t == 0:
                    pe.wait_ge(wr_in, 32)
                pe.wait_ge(cols_ready, t + 1)
                for kc in range(C):
                    last = nc.tensor.matmul(lps[:, t, :], G.ya[:, kc, t * P:(t + 1) * P], w_route[:, kc, :],
                                            start=kc == 0, stop=kc == C - 1)
                last.then_inc(routed, 1)

            pe.wait_ge(wo_in, 16)
            pe.wait_ge(m_ready, C)
            for t in range(T):
                if t >= 2:
                    pe.wait_ge(o_taken, t - 1)
                for h in range(HALF):
                    for kc in range(C):
                        last = nc.tensor.matmul(ps_o[:, t % 2, h * BANK:(h + 1) * BANK],
                                                G.ya[:, kc, t * P:(t + 1) * P],
                                                w_out[:, kc, h * BANK:(h + 1) * BANK],
                                                start=kc == 0, stop=kc == C - 1)
                last.then_inc(o_ready, 1)
                if t >= 1:
                    turn(t - 1)
                if t >= 2:
                    route(t - 2)
            route(T - 2)
            turn(T - 1)
            route(T - 1)

        @block.scalar
        def _(a):
            for c in range(C):
                a.wait_ge(g_ready, c + 1)
                if c >= 2:
                    a.wait_ge(m_ready, c - 1)
                nc.scalar.activation(gate[:, c % 2, :], ps[:, c % 2, :], ACT.Sigmoid).then_inc(g_taken, 1)
            for t in range(T):
                a.wait_ge(o_taken, t + 1)
                if t:
                    a.wait_ge(squared, t)
                nc.scalar.activation(junk[:], G.x2[:, t, :], ACT.Square, accum_out=rstd[:, t:t + 1]).then_inc(squared, 1)
                a.wait_ge(mean, t + 1)
                nc.scalar.activation(rstd[:, t:t + 1], rstd[:, t:t + 1], ACT.Sqrt).then_inc(rooted, 1)

        @block.vector
        def _(v):
            d = nc.vector
            st = Steps(v, dve)
            for c in range(C):
                v.wait_ge(g_taken, c + 1)
                st(d.tensor_tensor(G.yb[:, c, :], G.yb[:, c, :], gate[:, c % 2, :], ALU.mult))
                st.join()
                d.tensor_tensor(G.ya[:, c, :], G.ya[:, c, :], G.yb[:, c, :], ALU.add).then_inc(m_ready, 1)

            def take(t):
                v.wait_ge(turned, t + 1)
                d.tensor_copy(G.ya[:, :, t * P:(t + 1) * P], tp).then_inc(cols_ready, 1)

            v.wait_ge(x_in, 16)
            v.wait_ge(gain_in, 16)
            for t in range(T):
                v.wait_ge(o_ready, t + 1)
                d.tensor_tensor(G.x2[:, t, :], G.x2[:, t, :], ps_o[:, t % 2, :], ALU.add).then_inc(o_taken, 1)
                one = slice(t, t + 1)
                v.wait_ge(squared, t + 1)
                d.tensor_scalar(rstd[:, one], rstd[:, one], 1.0 / D, EPS, ALU.mult, ALU.add).then_inc(mean, 1)
                v.wait_ge(rooted, t + 1)
                st(d.reciprocal(rstd[:, one], rstd[:, one]))
                st.join()
                if t >= 2:
                    v.wait_ge(turned, t - 1)
                    v.wait_ge(row_out[t % 2], 16 * (t // 2))
                d.scalar_tensor_tensor(out=rows[:, t % 2, :], in0=G.x2[:, t, :], scalar=rstd[:, one], in1=gain[:],
                                       op0=ALU.mult, op1=ALU.mult).then_inc(rows_ready, 1)
                if t:
                    take(t - 1)
            take(T - 1)
            v.wait_ge(routed, T)
            d.tensor_copy(logits, lps)


def rows_to_cols(nc, G, rows, cols):
    ph = phase(nc)
    with ph.ctx:
        tp = ph.ps("tp", [P, 2, C, P])
        turned, taken = ph.sems("turned taken")
        block = ph.ctx.enter_context(nc.Block())

        @block.tensor
        def _(pe):
            for t in range(T):
                if t >= 2:
                    pe.wait_ge(taken, t - 1)
                for c in range(C):
                    last = nc.tensor.transpose(tp[:, t % 2, c, :], rows[:, t, c * P:(c + 1) * P], G.ident[:])
                last.then_inc(turned, 1)

        @block.vector
        def _(v):
            for t in range(T):
                v.wait_ge(turned, t + 1)
                nc.vector.tensor_copy(cols[:, :, t * P:(t + 1) * P], tp[:, t % 2]).then_inc(taken, 1)


def route1(nc, A, G, lg):
    ph = phase(nc)
    PER = E1 // GROUPS1
    with ph.ctx:
        bias = ph.sb("bias", [P, GROUPS1 + E1])
        pad = ph.sb("pad", [P, T, 8])
        gtop = ph.sb("gtop", [P, T, 8])
        gidx = ph.sb("gidx", [P, T, 8], U32)
        gnum = ph.sb("gnum", [P, T, 1])
        pen = ph.sb("pen", [P, T, GROUPS1])
        ex = ph.sb("ex", [P, T, GROUPS1])
        pgrp = ph.sb("pgrp", [P, T])
        em = ph.sb("em", [P, T, GROUPS1, PER])
        etop = ph.sb("etop", [P, T, 8])
        eidx = ph.sb("eidx", [P, T, 8], U32)
        gap = ph.sb("gap", [P, T])
        loaded, dve, to_exp, exped, to_sig, siged = ph.sems("loaded dve to_exp exped to_sig siged")
        block = ph.ctx.enter_context(nc.Block())

        @block.sync
        def _(sp):
            sp.dma_start(bias[:, 0:GROUPS1], A["router_group_b"].to_broadcast([P, GROUPS1])).then_inc(loaded, 16)
            sp.dma_start(bias[:, GROUPS1:], A["router_expert_b"].to_broadcast([P, E1])).then_inc(loaded, 16)

        @block.scalar
        def _(a):
            a.wait_ge(to_exp, 1)
            nc.scalar.activation(ex[:], ex[:], ACT.Exp).then_inc(exped, 1)
            a.wait_ge(to_sig, 1)
            nc.scalar.activation(G.w[:, :, 0], gap[:], ACT.Sigmoid).then_inc(siged, 1)
            nc.scalar.activation(G.w[:, :, 1], gap[:], ACT.Sigmoid, scale=-1.0).then_inc(siged, 1)

        @block.vector
        def _(v):
            d = nc.vector
            st = Steps(v, dve)
            W = GROUPS1 + E1
            v.wait_ge(loaded, 32)
            st(d.tensor_tensor(lg, lg, bias[:, None, :].to_broadcast([P, T, W]), ALU.add))
            st(d.memset(pad[:], NEG))
            st.join()
            st(d.tensor_copy(pad[:, :, 0:GROUPS1], lg[:, :, 0:GROUPS1]))
            st.join()
            for t in range(T):
                st(d.max(gtop[:, t, :], pad[:, t, :]))
            st.join()
            for t in range(T):
                st(d.max_index(gidx[:, t, :], gtop[:, t, :], pad[:, t, :]))
            d.tensor_tensor(ex[:], lg[:, :, 0:GROUPS1], gtop[:, :, 0:1].to_broadcast([P, T, GROUPS1]),
                            ALU.subtract).then_inc(to_exp, 1)
            st.join()
            st(d.tensor_copy(gnum[:], gidx[:, :, 0:1]))
            st.join()
            st(d.tensor_tensor(pen[:], G.iota[:, None, 0:GROUPS1].to_broadcast([P, T, GROUPS1]),
                               gnum[:].to_broadcast([P, T, GROUPS1]), ALU.is_equal))
            st.join()
            st(d.tensor_scalar(pen[:], pen[:], -1.0, -NEG, ALU.add, ALU.mult))
            st.join()
            st(d.tensor_tensor(em[:], lg[:, :, GROUPS1:].rearrange("p t (g e) -> p t g e", g=GROUPS1),
                               pen[:, :, :, None].to_broadcast([P, T, GROUPS1, PER]), ALU.add))
            st.join()
            for t in range(T):
                st(d.max(etop[:, t, :], em[:, t]))
            st.join()
            for t in range(T):
                st(d.max_index(eidx[:, t, :], etop[:, t, :], em[:, t].rearrange("p g e -> p (g e)")))
            st(d.tensor_tensor(gap[:], etop[:, :, 0], etop[:, :, 1], ALU.subtract))
            st.join()
            d.tensor_copy(G.e, eidx[:, :, 0:K1]).then_inc(to_sig, 1)
            v.wait_ge(exped, 1)
            st(d.tensor_reduce(pgrp[:], ex[:], AX, ALU.add))
            st.join()
            st(d.reciprocal(pgrp[:], pgrp[:]))
            st.join()
            v.wait_ge(siged, 2)
            st(d.tensor_tensor(G.w, G.w, pgrp[:, :, None].to_broadcast([P, T, K1]), ALU.mult))


def dispatch(nc, G, K, E, NB, scores=None):
    ph = phase(nc)
    with ph.ctx:
        oh = ph.sb("oh", [P, T, K, E])
        prod = ph.sb("prod", [P, T, K, E])
        m = ph.sb("m", [P, T, E])
        before = ph.sb("before", [P, T + 1, E])
        cnt = ph.sb("cnt", [P, E])
        cnt_i = ph.sb("cnt_i", [P, E], I32)
        last_b = ph.sb("last_b", [P, E])
        first_b = ph.sb("first_b", [P, E])
        dest = ph.sb("dest", [P, T, E])
        destk = ph.sb("destk", [P, T, K])
        half_i = ph.sb("half_i", [P, 2, T, K], I32)
        half_f = ph.sb("half_f", [P, 2, T, K])
        lo = ph.sb("lo", [P, 2, K, P])
        hi = ph.sb("hi", [P, 2, K, P])
        cmp = ph.sb("cmp", [P, E])
        be = ph.sb("be", [P, 1])
        wsum = ph.sb("wsum", [P, T])
        rank = ph.ps("rank", [P, BANK])[:, 0:T * E].rearrange("p (t e) -> p t e", e=E)
        cps = ph.ps("cps", [P, BANK])[:, 0:E]
        tok_ps = ph.ps("tok_ps", [P, BANK])[:, 0:P]
        row_ps = ph.ps("row_ps", [1, BANK])[:, 0:P]
        (dve, sums_ready, ranked, be_ready, be_row, hot, scaled, used, toks) = ph.sems(
            "dve sums_ready ranked be_ready be_row hot scaled used toks")
        block = ph.ctx.enter_context(nc.Block())

        @block.tensor
        def _(pe):
            pe.wait_ge(sums_ready, 1)
            for t in range(T):
                nc.tensor.matmul(rank[:, t, :], G.tri[:], m[:, t, :], start=True, stop=False)
                nc.tensor.matmul(rank[:, t, :], G.ones[:], before[:, t, :], start=False, stop=True)
            nc.tensor.matmul(cps, G.ones[:], before[:, T, :], start=True, stop=True).then_inc(ranked, 1)
            pe.wait_ge(be_ready, 1)
            nc.tensor.matmul(row_ps, be[:], G.ident[:], start=True, stop=True).then_inc(be_row, 1)
            for t in range(T):
                pe.wait_ge(hot, t + 1)
                pe.wait_ge(scaled, t + 1)
                for k in range(K):
                    last = nc.tensor.matmul(tok_ps, lo[:, t % 2, k, :], hi[:, t % 2, k, :],
                                            start=t == 0 and k == 0, stop=t == T - 1 and k == K - 1)
                last.then_inc(used, 1)

        @block.scalar
        def _(a):
            for t in range(T):
                a.wait_ge(hot, t + 1)
                nc.scalar.activation(hi[:, t % 2], hi[:, t % 2], ACT.Copy, scale=G.tok[:, t:t + 1]).then_inc(scaled, 1)

        @block.vector
        def _(v):
            d = nc.vector
            st = Steps(v, dve)
            iota_e = G.iota[:, 0:E]
            for t in range(T):
                st(d.tensor_tensor(oh[:, t], G.e[:, t, :, None].to_broadcast([P, K, E]),
                                   iota_e[:, None, :].to_broadcast([P, K, E]), ALU.is_equal))
            st(d.memset(before[:, 0, :], 0.0))
            st.join()
            st(d.tensor_reduce(m[:], oh[:].rearrange("p t k e -> p t e k"), AX, ALU.add))
            st.join()
            for t in range(T):
                ins = d.tensor_tensor(before[:, t + 1, :], before[:, t, :], m[:, t, :], ALU.add)
                if t + 1 < T:
                    st(ins)
                    st.join()
                else:
                    ins.then_inc(sums_ready, 1)
            v.wait_ge(ranked, 1)
            st(d.tensor_scalar(cnt[:], cps, float(P - 1), None, ALU.add))
            st.join()
            st(d.tensor_copy(cnt_i[:], cnt[:]))
            st.join()
            st(d.tensor_scalar(cnt_i[:], cnt_i[:], 7, None, ALU.logical_shift_right))
            st.join()
            st(d.tensor_copy(cnt[:], cnt_i[:]))
            st.join()
            st(d.tensor_tensor_scan(last_b[:], G.ones[:, 0:E], cnt[:], 0.0, ALU.mult, ALU.add))
            st.join()
            st(d.tensor_tensor(first_b[:], last_b[:], cnt[:], ALU.subtract))
            st(d.tensor_copy(G.used, last_b[0:1, E - 1:E]))
            st(d.tensor_scalar(cmp[:], last_b[:], G.tok[:, 0:1], None, ALU.is_le))
            st.join()
            st(d.tensor_copy(G.first, first_b[0:1, :]))
            st(d.tensor_reduce(be[:], cmp[:], AX, ALU.add))
            st.join()
            d.tensor_scalar(be[:], be[:], float(E - 1), None, ALU.min).then_inc(be_ready, 1)
            st(d.scalar_tensor_tensor(out=dest[:], in0=first_b[:, None, :].to_broadcast([P, T, E]),
                                      scalar=float(P), in1=rank, op0=ALU.mult, op1=ALU.add))
            st.join()
            for t in range(T):
                st(d.tensor_tensor(prod[:, t], oh[:, t], dest[:, t, None, :].to_broadcast([P, K, E]), ALU.mult))
            st.join()
            st(d.tensor_reduce(destk[:], prod[:], AX, ALU.add))
            st.join()
            st(d.tensor_copy(G.slot, destk[:]))
            st.join()
            st(d.tensor_scalar(half_i[:, 0], G.slot, 7, None, ALU.logical_shift_right))
            st(d.tensor_scalar(half_i[:, 1], G.slot, P - 1, None, ALU.bitwise_and))
            st.join()
            st(d.tensor_copy(half_f[:], half_i[:]))
            st.join()
            iota_b = G.iota[:, None, :].to_broadcast([P, K, P])
            for t in range(T):
                if t >= 2:
                    v.wait_ge(used, t - 1)
                st(d.tensor_tensor(lo[:, t % 2], half_f[:, 1, t, :, None].to_broadcast([P, K, P]), iota_b, ALU.is_equal))
                d.tensor_tensor(hi[:, t % 2], half_f[:, 0, t, :, None].to_broadcast([P, K, P]), iota_b,
                                ALU.is_equal).then_inc(hot, 1)
            v.wait_ge(be_row, 1)
            st(d.tensor_copy(G.blk_e[:, 0:P], row_ps))
            st(d.memset(G.blk_e[:, P:], E - 1))
            if scores is not None:
                for t in range(T):
                    st(d.tensor_tensor(prod[:, t], oh[:, t], scores[:, t, None, :].to_broadcast([P, K, E]), ALU.mult))
                st.join()
                st(d.tensor_reduce(G.w, prod[:], AX, ALU.add))
                st.join()
                st(d.tensor_reduce(wsum[:], G.w, AX, ALU.add))
                st.join()
                st(d.reciprocal(wsum[:], wsum[:]))
                st.join()
                st(d.tensor_scalar(wsum[:], wsum[:], ROUTED_SCALE, None, ALU.mult))
                st.join()
                st(d.tensor_tensor(G.w, G.w, wsum[:, :, None].to_broadcast([P, T, K]), ALU.mult))
            st(d.memset(G.slot_tok, 0))
            v.wait_ge(used, T)
            st.join()
            st(d.tensor_copy(G.slot_tok[:, 0:P], tok_ps))


def experts(nc, G, E, NB, rows_d, wg_d, wu_d, wd_d, y_d):
    ph = phase(nc)
    W = 4
    FC = F_EXP // P
    with ph.ctx:
        w_gu = ph.sb("w_gu", [P, W, 2, C, F_EXP])
        w_dn = ph.sb("w_dn", [P, W, FC, D])
        idx = ph.sb("idx", [P, 2], I32)
        mark = ph.sb("mark", [P, 2])
        xb = ph.sb("xb", [P, 2, D])
        x_t = ph.sb("x_t", [P, 2, C, P])
        act_g = ph.sb("act_g", [P, 2, F_EXP])
        hid = ph.sb("hid", [P, 2, F_EXP])
        hid_t = ph.sb("hid_t", [P, 2, FC, P])
        y = ph.sb("y", [P, 2, D])
        x_ps = ph.ps("x_ps", [P, C, P])
        gu_ps = ph.ps("gu_ps", [P, 2, 2, F_EXP])
        h_ps = ph.ps("h_ps", [P, BANK // P, P])[:, 0:FC, :]
        y_ps = ph.ps("y_ps", [P, D])
        (w_in0, w_in1, w_in2, w_in3, w_ready, idx_ready, x_in0, x_in1, x_turned, x_ready, gu_ready,
         silu_done, hid_ready, h_turned, h_ready, y_ready, y_taken, y_out0, y_out1) = ph.sems(
            "w_in0 w_in1 w_in2 w_in3 w_ready idx_ready x_in0 x_in1 x_turned x_ready gu_ready "
            "silu_done hid_ready h_turned h_ready y_ready y_taken y_out0 y_out1")
        w_in, x_in, y_out = [w_in0, w_in1, w_in2, w_in3], [x_in0, x_in1], [y_out0, y_out1]
        wg_v = wg_d.rearrange("l e (p c) n -> (l e) p (c n)", c=C)
        wu_v = wu_d.rearrange("l e (p c) n -> (l e) p (c n)", c=C)
        wd_v = wd_d.rearrange("l e (p c) n -> (l e) p (c n)", c=FC)
        PAIRS = (NB + 1) // 2
        FAR = W - 2
        block = ph.ctx.enter_context(nc.Block())

        def steps(eng, step):
            n = eng.value_load(G.used, min_val=0, max_val=NB)
            for i in range(3):
                step(i, i % 2, 0)
            with eng.Fori(1, PAIRS) as j:
                for u in range(2):
                    i = j * 2 + (1 + u)
                    with eng.If(i <= n):
                        step(i, (1 + u) % 2, j * 16)
            return n

        @block.sync
        def _(sp):
            def load(e, slot):
                for dst, src in ((w_gu[:, slot, 0].rearrange("p c n -> p (c n)"), wg_v),
                                 (w_gu[:, slot, 1].rearrange("p c n -> p (c n)"), wu_v),
                                 (w_dn[:, slot].rearrange("p c n -> p (c n)"), wd_v)):
                    sp.dma_start(dst, src[bass.ds(e, 1)].rearrange("o p n -> p (o n)")).then_inc(w_in[slot], 16)

            for e in range(W):
                load(e, e)
            for e in range(W - 1):
                sp.wait_ge(w_in[e], 48)
                sp.sem_inc(w_ready, 1)
            with sp.Fori(0, E // W - 1) as j:
                for u in range(W):
                    e = j * W + (W + u)
                    done = sp.value_load(G.first[0:1, bass.ds(j * W + (u + 1), 1)], min_val=0, max_val=NB)
                    sp.wait_ge(y_ready, 1 + done)
                    load(e, u)
                    sp.wait_ge(w_in[(u - 1) % W], j * 48 + (48 if u == 0 else 96))
                    sp.sem_inc(w_ready, 1)
            sp.wait_ge(w_in[W - 1], (E // W) * 48)
            sp.sem_inc(w_ready, 1)

        @block.gpsimd
        def _(pool):
            g = nc.gpsimd

            def gather(b, slot, landed):
                if landed is not None:
                    pool.wait_ge(x_in[slot], landed)
                g.tensor_copy(idx[:, slot:slot + 1], G.slot_tok[:, bass.ds(b, 1)]).then_inc(idx_ready, 1)
                pool.wait_ge(idx_ready, 2 * b + 1)
                g.tensor_tensor(mark[:, slot:slot + 1], G.tok[:, 0:1], G.tok[:, 0:1], ALU.add).then_inc(idx_ready, 1)
                g.indirect_dma_start(xb[:, slot, :], None, rows_d, bass.IndirectOffsetOnAxis(
                    ap=idx[:, slot:slot + 1], axis=0)).then_inc(x_in[slot], 16)

            gather(0, 0, None)
            gather(1, 1, None)
            n = pool.value_load(G.used, min_val=0, max_val=NB)
            with pool.Fori(0, PAIRS) as j:
                for u in range(2):
                    i = j * 2 + (1 + u)
                    with pool.If(i <= n):
                        pool.wait_ge(x_turned, i)
                        gather(i + 1, u, j * 16 + 16)
            pool.wait_ge(y_out[0], (n + 1) // 2 * 16)
            pool.wait_ge(y_out[1], n // 2 * 16)

        @block.tensor
        def _(pe):
            def turn_rows(b, slot, landed):
                pe.wait_ge(x_in[slot], landed)
                for c in range(C):
                    last = nc.tensor.transpose(x_ps[:, c, :], xb[:, slot, c::C], G.ident[:])
                last.then_inc(x_turned, 1)

            def step(i, slot, rounds):
                first = isinstance(i, int) and i == 0
                e = pe.value_load(G.blk_e[0:1, bass.ds(i, 1)], min_val=0, max_val=E - 1)
                if not first:
                    e_before = pe.value_load(G.blk_e[0:1, bass.ds(i - 1, 1)], min_val=0, max_val=E - 1)
                    with pe.If(e > e_before + FAR):
                        finish(i, 1 - slot, e_before)
                pe.wait_ge(w_ready, e + 1)
                pe.wait_ge(x_ready, i + 1)
                ws = e % W
                for c in range(C):
                    last = nc.tensor.matmul(gu_ps[:, slot], x_t[:, slot, c, :],
                                            w_gu[:, bass.ds(ws, 1), :, c, :].rearrange("p o g n -> p (o g) n"),
                                            start=c == 0, stop=c == C - 1)
                last.then_inc(gu_ready, 1)
                turn_rows(i + 1, 1 - slot, 16 if first else rounds + 32)
                if not first:
                    with pe.If(e <= e_before + FAR):
                        finish(i, 1 - slot, e_before)
                pe.wait_ge(hid_ready, i + 1)
                for c in range(FC):
                    last = nc.tensor.transpose(h_ps[:, c, :], hid[:, slot, c::FC], G.ident[:])
                last.then_inc(h_turned, 1)

            def finish(i, slot, e):
                pe.wait_ge(h_ready, i)
                pe.wait_ge(y_taken, 1 + i - 1)
                ws = e % W
                for h in range(D // BANK):
                    for c in range(FC):
                        last = nc.tensor.matmul(y_ps[:, h * BANK:(h + 1) * BANK], hid_t[:, slot, c, :],
                                                w_dn[:, bass.ds(ws, 1), c, h * BANK:(h + 1) * BANK]
                                                .rearrange("p o n -> p (o n)"),
                                                start=c == 0, stop=c == FC - 1)
                last.then_inc(y_ready, 1)

            start_at_one(pe, y_ready)
            turn_rows(0, 0, 16)
            steps(pe, step)

        @block.scalar
        def _(a):
            s = nc.scalar

            def step(i, slot, rounds):
                a.wait_ge(gu_ready, i + 1)
                s.activation(act_g[:, slot, :], gu_ps[:, slot, 0, :], ACT.Silu).then_inc(silu_done, 1)
                if not (isinstance(i, int) and i == 0):
                    a.wait_ge(y_ready, 1 + i)
                    if not (isinstance(i, int) and i <= 2):
                        a.wait_ge(y_out[1 - slot], rounds)
                    s.activation(y[:, 1 - slot, :], y_ps[:], ACT.Copy).then_inc(y_taken, 1)
                    a.wait_ge(y_taken, 1 + i)
                    a.dma_start(y_d[bass.ds((i - 1) * P, P), :], y[:, 1 - slot, :]).then_inc(y_out[1 - slot], 16)

            start_at_one(a, y_taken)
            steps(a, step)

        @block.vector
        def _(v):
            d = nc.vector

            def step(i, slot, rounds):
                v.wait_ge(silu_done, i + 1)
                d.tensor_tensor(hid[:, slot, :], act_g[:, slot, :], gu_ps[:, slot, 1, :], ALU.mult).then_inc(hid_ready, 1)
                v.wait_ge(x_turned, i + 2)
                d.tensor_copy(x_t[:, 1 - slot], x_ps[:]).then_inc(x_ready, 1)
                v.wait_ge(h_turned, i + 1)
                d.tensor_copy(hid_t[:, slot], h_ps).then_inc(h_ready, 1)

            v.wait_ge(x_turned, 1)
            d.tensor_copy(x_t[:, 0], x_ps[:]).then_inc(x_ready, 1)
            steps(v, step)


def combine(nc, G, K, y_d):
    ph = phase(nc)
    R = 4
    with ph.ctx:
        idx = ph.sb("idx", [P, T * K], I32)
        yr = ph.sb("yr", [P, R, D])
        idx_ready, added = ph.sems("idx_ready added")
        y_in = ph.sems(" ".join(f"y_in{r}" for r in range(R)))
        block = ph.ctx.enter_context(nc.Block())

        @block.gpsimd
        def _(pool):
            nc.gpsimd.tensor_copy(idx[:], G.slot.rearrange("p t k -> p (t k)")).then_inc(idx_ready, 1)
            pool.wait_ge(idx_ready, 1)
            for n in range(T * K):
                if n >= R:
                    pool.wait_ge(added, n - R + 1)
                nc.gpsimd.indirect_dma_start(yr[:, n % R, :], None, y_d, bass.IndirectOffsetOnAxis(
                    ap=idx[:, n:n + 1], axis=0)).then_inc(y_in[n % R], 16)

        @block.vector
        def _(v):
            for n in range(T * K):
                v.wait_ge(y_in[n % R], 16 * (n // R + 1))
                if n % K:
                    v.wait_ge(added, n)
                h = G.h[:, n // K, :]
                nc.vector.scalar_tensor_tensor(out=h, in0=yr[:, n % R, :], scalar=G.w2[:, n:n + 1], in1=h,
                                               op0=ALU.mult, op1=ALU.add).then_inc(added, 1)


def moe_state(nc, ctx, G, K, E):
    sb = lambda name, shape, dt=F32: ctx.enter_context(nc.sbuf_tensor(name, shape, dt))
    G.e = sb(f"moe_e{E}", [P, T, K])[:]
    w = sb(f"moe_w{E}", [P, T * K])
    G.w2 = w[:]
    G.w = w[:].rearrange("p (t k) -> p t k", k=K)
    G.slot = sb(f"moe_slot{E}", [P, T, K], I32)[:]
    G.slot_tok = sb(f"moe_slot_tok{E}", [P, P + 2], I32)[:]
    G.blk_e = sb(f"moe_blk_e{E}", [1, P + 1], I32)[:]
    G.first = sb(f"moe_first{E}", [1, E], I32)[:]
    G.used = sb(f"moe_used{E}", [1, 1], I32)[:]


def hgrn(nc, A, G):
    ph = phase(nc)
    LEVELS = P.bit_length() - 1
    N = LEVELS + 1
    MASKED = 4 + 3 * LEVELS
    N_STEPS = 6 + 3 * LEVELS
    TO_EXP = LEVELS + 2
    EXPED = LEVELS + 4
    EARLY = 4
    H = HG_HEADS
    HT = T // 2
    w_in = A["w_in_2"].rearrange("l (c p) (k h n) -> (l h) p c k n", p=P, h=HG_HEADS, n=P)
    COLS = [1, 0, 2, 3]
    with ph.ctx:
        w = ph.sb("w", [P, 4, C, P])
        lb_col = ph.sb("lb_col", [P, HG_HEADS])
        lb1_col = ph.sb("lb1_col", [P, HG_HEADS])
        gain = ph.sb("gain", [P, HG_W])
        mask = ph.sb("mask", [P, N, P])
        keep = ph.sb("keep", [P, S])
        q = ph.sb("q", [P, S])
        k = ph.sb("k", [P, S])
        b = ph.sb("b", [P, S])
        e = ph.sb("e", [P, S])
        qk = ph.sb("qk", [P, LEVELS, S])
        qb = ph.sb("qb", [P, S])
        kd = ph.sb("kd", [P, S])
        eb = ph.sb("eb", [P, T])
        val = ph.sb("val", [P, T, P])
        gate = ph.sb("gate", [P, T, P])
        osq = e[:].rearrange("p (t n) -> p t n", n=P)
        kd_t = ph.sb("kd_t", [P, T, P])
        sm = ph.sb("sm", [P, N, P])
        sc = ph.sb("sc", [P, 2, P])
        state = ph.sb("state", [P, T, P])
        o = ph.sb("o", [P, T, P])
        rs = ph.sb("rs", [P, T])
        big = ph.ps("big", [P, 2, S])
        ko_ps = ph.ps("ko_ps", [P, T, P])
        u_ps = ph.ps("u_ps", [P, T, P])
        (w0, w1, w2, w3, gain_in, masked, proj, proj_taken, dve, act, to_exp, exped, kd_ready, lev_ready,
         sc_ps, sc_taken, sc_ready, kt_ready, kt_taken, o_ready, o_taken, u_ready, st_ready, root_in,
         rooted, o_done, turned, turn_taken, lb_ready) = ph.sems(
            "w0 w1 w2 w3 gain_in masked proj proj_taken dve act to_exp exped kd_ready lev_ready "
            "sc_ps sc_taken sc_ready kt_ready kt_taken o_ready o_taken u_ready st_ready root_in "
            "rooted o_done turned turn_taken lb_ready")
        w_in_sem = [w0, w1, w2, w3]
        block = ph.ctx.enter_context(nc.Block())

        @block.sync
        def _(sp):
            def load(h, n):
                sp.dma_start(w[:, n], w_in[bass.ds(h, 1), :, :, COLS[n], :].rearrange("o p c n -> p (o c) n")
                             ).then_inc(w_in_sem[n], 16)

            for n in range(4):
                load(0, n)
            sp.dma_start(gain[:], A["hg_norm_g_2"].to_broadcast([P, HG_W])).then_inc(gain_in, 16)
            with sp.Fori(0, H - 1) as h:
                for n in (1, 3):
                    sp.wait_ge(proj, h * 4 + (n + 1))
                    load(h + 1, n - 1)
                    load(h + 1, n)

        @block.gpsimd
        def _(pool):
            g = nc.gpsimd
            st = Steps(pool, masked)
            st(g.memset(mask[:], 1.0))
            st(g.memset(keep[:], 1.0))
            st.join()
            st(g.memset(keep[:, 0::P], 0.0))
            for lev in range(LEVELS):
                half = 1 << lev
                pieces = P // (2 * half)
                m = mask[:, lev, :].rearrange("s (n r) -> s n r", r=2 * half)
                st(g.affine_select(out=m, in_=m, compare_op=ALU.is_ge, fill=0.0, base=0,
                                   pattern=[[-2 * half, pieces], [0, 2 * half]], channel_multiplier=1))
                st.join()
                st(g.affine_select(out=m, in_=m, compare_op=ALU.is_gt, fill=0.0, base=half,
                                   pattern=[[2 * half, pieces], [0, 2 * half]], channel_multiplier=-1))
                st.join()
                st(g.memset(m[:, :, 0:half], 0.0))
            st(g.affine_select(out=mask[:, LEVELS, :], in_=mask[:, LEVELS, :], compare_op=ALU.is_equal, fill=0.0,
                               base=0, pattern=[[-1, P]], channel_multiplier=1))
            assert st.n == MASKED, st.n

        @block.tensor
        def _(pe):
            def turn_out(done):
                pe.wait_ge(o_done, done)
                for t in range(T):
                    last = nc.tensor.transpose(u_ps[:, t, :], o[:, t, :], G.ident[:])
                last.then_inc(turned, 1)

            with pe.Fori(0, H) as h:
                def project(n):
                    pe.wait_ge(w_in_sem[n], h * 16 + 16)
                    if n >= 2:
                        pe.wait_ge(proj_taken, 1 + h * 4 + (n - 1))
                    slot = n % 2
                    if n < 2:
                        for half in range(HALF):
                            for kc in range(C):
                                last = nc.tensor.matmul(big[:, slot, half * BANK:(half + 1) * BANK], w[:, n, kc, :],
                                                        G.u[:, kc, half * BANK:(half + 1) * BANK],
                                                        start=kc == 0, stop=kc == C - 1)
                    else:
                        for t in range(T):
                            for kc in range(C):
                                last = nc.tensor.matmul(big[:, slot, t * P:(t + 1) * P],
                                                        G.u[:, kc, t * P:(t + 1) * P], w[:, n, kc, :],
                                                        start=kc == 0, stop=kc == C - 1)
                    last.then_inc(proj, 1)

                project(0)
                with pe.If(h > 0):
                    turn_out(h)
                for n in range(1, 4):
                    project(n)
                pe.wait_ge(kd_ready, h + 1)
                for g in range(2):
                    pe.wait_ge(o_taken, 1 + h * 2)
                    for t in range(g * HT, min((g + 1) * HT, T - 1)):
                        last = nc.tensor.transpose(ko_ps[:, t, :], kd[:, t * P:(t + 1) * P], G.ident[:])
                    last.then_inc(kt_ready, 1)

                def scores(t):
                    cs = slice(t * P, (t + 1) * P)
                    if t < 2:
                        pe.wait_ge(proj_taken, 1 + h * 4 + (t + 3))
                    else:
                        pe.wait_ge(sc_taken, h * T + (t - 1))
                    for lev in range(N):
                        kk, qq = (qk[:, lev, cs], qk[:, lev, cs]) if lev < LEVELS else (k[:, cs], q[:, cs])
                        last = nc.tensor.matmul(big[:, t % 2, lev * P:(lev + 1) * P], kk, qq, start=True, stop=True)
                    last.then_inc(sc_ps, 1)

                pe.wait_ge(lev_ready, h + 1)
                scores(0)
                scores(1)
                pe.wait_ge(turn_taken, 1 + h)
                pe.wait_ge(kt_taken, h * 2 + 2)
                for t in range(T - 1):
                    last = nc.tensor.matmul(u_ps[:, t, :], kd_t[:, t, :], val[:, t, :], start=True, stop=True)
                last.then_inc(u_ready, 1)
                for t in range(T):
                    if t + 2 < T:
                        scores(t + 2)
                    pe.wait_ge(sc_ready, h * T + (t + 1))
                    last = nc.tensor.matmul(ko_ps[:, t, :], sc[:, t % 2, :], val[:, t, :], start=True, stop=t == 0)
                    if t:
                        pe.wait_ge(st_ready, h * (T - 1) + t)
                        last = nc.tensor.matmul(ko_ps[:, t, :], qb[:, t * P:(t + 1) * P], state[:, t, :],
                                                start=False, stop=True)
                    last.then_inc(o_ready, 1)
            turn_out(H)

        @block.scalar
        def _(a):
            s = nc.scalar
            start_at_one(a, proj_taken, o_taken)
            a.wait_ge(lb_ready, 1)
            s.activation(lb_col[:], lb_col[:], ACT.Sigmoid).then_inc(act, 1)
            with a.Fori(0, H) as h:
                a.wait_ge(proj, h * 4 + 1)
                s.activation(k[:], big[:, 0], ACT.Sigmoid).then_inc(proj_taken, 1)
                a.wait_ge(to_exp, h * TO_EXP + 1)
                s.activation(b[:], e[:], ACT.Ln).then_inc(exped, 1)

                def level(lev):
                    a.wait_ge(to_exp, h * TO_EXP + (lev + 2))
                    s.activation(qk[:, lev, :], qk[:, lev, :], ACT.Exp).then_inc(exped, 1)

                for lev in range(EARLY):
                    level(lev)
                a.wait_ge(proj, h * 4 + 2)
                s.activation(q[:], big[:, 1], ACT.Silu).then_inc(proj_taken, 1)
                for lev in range(EARLY, LEVELS):
                    level(lev)
                a.wait_ge(to_exp, h * TO_EXP + TO_EXP)
                s.activation(kd[:], kd[:], ACT.Exp).then_inc(exped, 1)
                s.activation(eb[:], e[:, P - 1::P], ACT.Exp).then_inc(exped, 1)
                s.activation(qb[:], e[:], ACT.Exp).then_inc(exped, 1)
                a.wait_ge(proj, h * 4 + 3)
                s.activation(val[:].rearrange("p t n -> p (t n)"), big[:, 0], ACT.Copy).then_inc(proj_taken, 1)
                a.wait_ge(proj, h * 4 + 4)
                s.activation(gate[:].rearrange("p t n -> p (t n)"), big[:, 1], ACT.Silu).then_inc(proj_taken, 1)
                for g in range(2):
                    a.wait_ge(kt_ready, h * 2 + (g + 1))
                    ts = slice(g * HT, min((g + 1) * HT, T - 1))
                    s.activation(kd_t[:, ts, :], ko_ps[:, ts, :], ACT.Copy).then_inc(kt_taken, 1)
                for g in range(2):
                    a.wait_ge(o_ready, h * T + (g + 1) * HT)
                    ts = slice(g * HT, (g + 1) * HT)
                    s.activation(o[:, ts, :], ko_ps[:, ts, :], ACT.Copy).then_inc(o_taken, 1)
                a.wait_ge(o_taken, 1 + h * 2 + 2)
                s.activation(osq, o[:], ACT.Square).then_inc(act, 1)
                a.wait_ge(root_in, h + 1)
                s.activation(rs[:], rs[:], ACT.Sqrt).then_inc(rooted, 1)

        @block.vector
        def _(v):
            d = nc.vector
            start_at_one(v, turn_taken)
            first, _ = VROW["hg_lb_logits_2"]
            d.tensor_tensor(lb_col[:], G.vec[:, first:first + H], G.vec[:, first + H:first + 2 * H],
                            ALU.subtract).then_inc(lb_ready, 1)
            v.wait_ge(act, 1)
            d.tensor_scalar(lb1_col[:], lb_col[:], -1.0, 1.0, ALU.mult, ALU.add).then_inc(lb_ready, 1)
            v.wait_ge(lb_ready, 2)
            v.wait_ge(masked, MASKED)
            v.wait_ge(gain_in, 16)

            def take_out(head, done):
                v.wait_ge(turned, done)
                d.tensor_copy(G.mix[:, bass.ds(head, 1), :].rearrange("p o t -> p (o t)"),
                              u_ps[:].rearrange("p t n -> p (t n)")).then_inc(turn_taken, 1)

            with v.Fori(0, H) as h:
                st = Steps(v, dve, h * N_STEPS)
                EXD = h * EXPED
                v.wait_ge(proj_taken, 1 + h * 4 + 1)
                d.tensor_scalar(e[:], k[:], lb1_col[:, bass.ds(h, 1)], lb_col[:, bass.ds(h, 1)], ALU.mult,
                                ALU.add).then_inc(to_exp, 1)
                v.wait_ge(to_exp, h * TO_EXP + 1)
                st(d.tensor_scalar(k[:], e[:], -1.0, 1.0, ALU.mult, ALU.add))
                v.wait_ge(exped, EXD + 1)
                st.join()
                st(d.tensor_tensor_scan(e[:], keep[:], b[:], 0.0, ALU.mult, ALU.add))
                st.join()
                piece = "p (n r) -> p n r"
                for lev in range(LEVELS):
                    half = 1 << lev
                    bb = e[:].rearrange(piece, r=2 * half)
                    out = qk[:, lev, :].rearrange(piece, r=2 * half)
                    mid = bb[:, :, half - 1:half].to_broadcast([P, S // (2 * half), half])
                    st(d.tensor_tensor(out[:, :, 0:half], mid, bb[:, :, 0:half], ALU.subtract))
                    d.tensor_tensor(out[:, :, half:], bb[:, :, half:], mid, ALU.subtract).then_inc(to_exp, 1)
                bb = e[:].rearrange(piece, r=P)
                d.tensor_tensor(kd[:].rearrange(piece, r=P), bb[:, :, P - 1:P].to_broadcast([P, T, P]),
                                bb, ALU.subtract).then_inc(to_exp, 1)
                with v.If(h > 0):
                    take_out((h + (H - 1)) % H, h)
                v.wait_ge(proj_taken, 1 + h * 4 + 2)
                for lev in range(LEVELS):
                    half = 1 << lev
                    out = qk[:, lev, :].rearrange(piece, r=2 * half)
                    v.wait_ge(exped, EXD + (2 + lev))
                    for by, sl in ((k, slice(0, half)), (q, slice(half, 2 * half))):
                        st(d.tensor_tensor(out[:, :, sl], out[:, :, sl],
                                           by[:].rearrange(piece, r=2 * half)[:, :, sl], ALU.mult))
                v.wait_ge(exped, EXD + EXPED)
                d.tensor_tensor(kd[:], kd[:], k[:], ALU.mult).then_inc(kd_ready, 1)
                d.tensor_tensor(qb[:], qb[:], q[:], ALU.mult).then_inc(lev_ready, 1)
                for t in range(T):
                    if t == 2:
                        v.wait_ge(u_ready, h + 1)
                        d.tensor_copy(state[:, 1, :], u_ps[:, 0, :]).then_inc(st_ready, 1)
                        for n in range(2, T):
                            v.wait_ge(st_ready, h * (T - 1) + (n - 1))
                            d.scalar_tensor_tensor(out=state[:, n, :], in0=state[:, n - 1, :], scalar=eb[:, n - 1:n],
                                                   in1=u_ps[:, n - 1, :], op0=ALU.mult, op1=ALU.add
                                                   ).then_inc(st_ready, 1)
                    v.wait_ge(sc_ps, h * T + (t + 1))
                    if t:
                        v.wait_ge(sc_ready, h * T + t)
                    d.tensor_tensor(sm[:].rearrange("p n t -> p (n t)"), big[:, t % 2],
                                    mask[:].rearrange("p n t -> p (n t)"), ALU.mult).then_inc(sc_taken, 1)
                    v.wait_ge(sc_taken, h * T + (t + 1))
                    if t >= 2:
                        v.wait_ge(o_ready, h * T + (t - 1))
                    d.tensor_reduce(sc[:, t % 2, :], sm[:].rearrange("p n t -> p t n"), AX, ALU.add).then_inc(sc_ready, 1)
                v.wait_ge(proj_taken, 1 + h * 4 + 4)
                st(d.tensor_tensor(gate[:], gate[:], gain[:, bass.ds(h * P, P)].unsqueeze(1).to_broadcast([P, T, P]), ALU.mult))
                v.wait_ge(act, h + 2)
                st(d.tensor_reduce(rs[:], osq, AX, ALU.add))
                st.join()
                d.tensor_scalar(rs[:], rs[:], 1.0 / P, EPS, ALU.mult, ALU.add).then_inc(root_in, 1)
                v.wait_ge(rooted, h + 1)
                st(d.reciprocal(rs[:], rs[:]))
                st.join()
                st(d.tensor_tensor(o[:], o[:], rs[:, :, None].to_broadcast([P, T, P]), ALU.mult))
                st.join()
                d.tensor_tensor(o[:], o[:], gate[:], ALU.mult).then_inc(o_done, 1)
                assert st.n == N_STEPS, st.n
            take_out(H - 1, H)


def pooling(nc, A, G):
    ph = phase(nc)
    GR = POOL_W // P
    PAD = 1 << GR
    scale = vec(G, "pool_scale_2")
    with ph.ctx:
        w = ph.sb("w", [P, C, POOL_W])
        w_pool = ph.sb("w_pool", [P, GR, P])
        sums = ph.sb("sums", [P, 2, PAD + S])
        u = ph.sb("u", [P, S])
        inv = ph.sb("inv", [P, GR, PAD])
        pos = ph.sb("pos", [P, PAD])
        mean = ph.sb("mean", [P, 2, S])
        u_ps = ph.ps("u_ps", [P, 2, S])
        p_ps = ph.ps("p_ps", [P, 2, S])
        w_in, wp_in, u_ready, u_taken, m_ready, p_ready, p_taken, dve = ph.sems(
            "w_in wp_in u_ready u_taken m_ready p_ready p_taken dve")
        block = ph.ctx.enter_context(nc.Block())

        @block.sync
        def _(sp):
            sp.dma_start(w[:], A["w_in_2"].rearrange("l (c p) n -> p (l c) n", p=P)[:, :, 4 * HG_W:]).then_inc(w_in, 16)
            sp.dma_start(w_pool[:], A["w_pool_2"].rearrange("l g c d -> c (l g) d")).then_inc(wp_in, 16)

        @block.tensor
        def _(pe):
            def mix(g):
                pe.wait_ge(m_ready, g + 1)
                if g >= 2:
                    pe.wait_ge(p_taken, g - 1)
                for half in range(HALF):
                    hs = slice(half * BANK, (half + 1) * BANK)
                    last = nc.tensor.matmul(p_ps[:, g % 2, hs], w_pool[:, g, :], mean[:, g % 2, hs], start=True, stop=True)
                last.then_inc(p_ready, 1)

            pe.wait_ge(w_in, 16)
            pe.wait_ge(wp_in, 16)
            for g in range(GR):
                if g >= 2:
                    pe.wait_ge(u_taken, g - 1)
                for half in range(HALF):
                    hs = slice(half * BANK, (half + 1) * BANK)
                    for kc in range(C):
                        last = nc.tensor.matmul(u_ps[:, g % 2, hs], w[:, kc, g * P:(g + 1) * P], G.u[:, kc, hs],
                                                start=kc == 0, stop=kc == C - 1)
                last.then_inc(u_ready, 1)
                if g:
                    mix(g - 1)
            mix(GR - 1)

        @block.scalar
        def _(a):
            for g in range(GR):
                a.wait_ge(p_ready, g + 1)
                nc.scalar.activation(G.mix[:, HG_HEADS + g, :], p_ps[:, g % 2, :], ACT.Copy,
                                     scale=scale[:, g:g + 1]).then_inc(p_taken, 1)

        @block.vector
        def _(v):
            d = nc.vector
            st = Steps(v, dve)
            st(d.memset(sums[:, :, 0:PAD], 0.0))
            st(d.tensor_scalar(pos[:], G.iota[:, 0:PAD], 1.0, None, ALU.add))
            st.join()
            st(d.reciprocal(pos[:], pos[:]))
            st.join()
            for g in range(GR):
                st(d.tensor_scalar(inv[:, g, :], pos[:], 1.0 / (2 << g), None, ALU.max))
            for g in range(GR):
                v.wait_ge(u_ready, g + 1)
                if g:
                    st.join()
                    v.wait_ge(m_ready, g)
                st(d.tensor_copy(sums[:, 0, PAD:], u_ps[:, g % 2, :]))
                st.join()
                d.tensor_copy(u[:], sums[:, 0, PAD:]).then_inc(u_taken, 1)
                for n in range(g + 1):
                    src, dst = sums[:, n % 2], sums[:, (n + 1) % 2]
                    st(d.tensor_tensor(dst[:, PAD:], src[:, PAD:], src[:, PAD - (1 << n):PAD + S - (1 << n)], ALU.add))
                    st.join()
                total = sums[:, (g + 1) % 2]
                v.wait_ge(u_taken, g + 1)
                if g >= 2:
                    v.wait_ge(p_ready, g - 1)
                m = mean[:, g % 2]
                st(d.tensor_tensor(total[:, PAD:2 * PAD], total[:, PAD:2 * PAD], inv[:, g, :], ALU.mult))
                st.join()
                st(d.tensor_tensor(m[:, 0:PAD], total[:, PAD:2 * PAD], u[:, 0:PAD], ALU.subtract))
                d.scalar_tensor_tensor(out=m[:, PAD:], in0=total[:, 2 * PAD:], scalar=1.0 / (2 << g), in1=u[:, PAD:],
                                       op0=ALU.mult, op1=ALU.subtract).then_inc(m_ready, 1)


def mix_out(nc, A, G, rows_d, logits):
    ph = phase(nc)
    with ph.ctx:
        w_out = ph.sb("w_out", [P, C, D])
        w_route = ph.sb("w_route", [P, C, E2])
        gain = ph.sb("gain", [P, D])
        bias = ph.sb("bias", [P, D])
        junk = ph.sb("junk", [P, 2, D])
        total = ph.sb("total", [P, T])
        var = ph.sb("var", [P, T])
        shift = ph.sb("shift", [P, T])
        ps = ph.ps("ps", [P, 2, D])
        tp = ph.ps("tp", [P, C, P])
        lps = ph.ps("lps", [P, T, E2])
        (w_in, wr_in, vec_in, ready, summed_in, summed, mean, squared, var_ready, rooted, rstd_ready, dve, normed,
         rows_ready, stored, turned, cols_ready, routed) = ph.sems(
            "w_in wr_in vec_in ready summed_in summed mean squared var_ready rooted rstd_ready dve normed "
            "rows_ready stored turned cols_ready routed")
        block = ph.ctx.enter_context(nc.Block())

        @block.sync
        def _(sp):
            sp.dma_start(w_out[:], A["w_out_2"].rearrange("l (c p) n -> p (l c) n", p=P)).then_inc(w_in, 16)
            sp.dma_start(gain[:], A["ln1_g_2"].to_broadcast([P, D])).then_inc(vec_in, 16)
            sp.dma_start(bias[:], A["ln1_b_2"].to_broadcast([P, D])).then_inc(vec_in, 16)
            sp.dma_start(w_route[:], A["w_router_2"].rearrange("l (c p) n -> p (l c) n", p=P)).then_inc(wr_in, 16)
            for t in range(T):
                sp.wait_ge(rows_ready, t + 1)
                sp.dma_start(rows_d[t * P:(t + 1) * P, :], G.h[:, t, :]).then_inc(stored, 16)
            sp.wait_ge(stored, 16 * T)

        @block.tensor
        def _(pe):
            def turn(t):
                pe.wait_ge(rows_ready, t + 1)
                if t:
                    pe.wait_ge(cols_ready, t)
                for c in range(C):
                    last = nc.tensor.transpose(tp[:, c, :], G.h[:, t, c * P:(c + 1) * P], G.ident[:])
                last.then_inc(turned, 1)

            def route(t):
                if t == 0:
                    pe.wait_ge(wr_in, 16)
                pe.wait_ge(cols_ready, t + 1)
                for kc in range(C):
                    last = nc.tensor.matmul(lps[:, t, :], G.u[:, kc, t * P:(t + 1) * P], w_route[:, kc, :],
                                            start=kc == 0, stop=kc == C - 1)
                last.then_inc(routed, 1)

            pe.wait_ge(w_in, 16)
            for t in range(T):
                if t >= 2:
                    pe.wait_ge(summed_in, t - 1)
                for h in range(HALF):
                    for kc in range(C):
                        last = nc.tensor.matmul(ps[:, t % 2, h * BANK:(h + 1) * BANK], G.mix[:, kc, t * P:(t + 1) * P],
                                                w_out[:, kc, h * BANK:(h + 1) * BANK], start=kc == 0, stop=kc == C - 1)
                last.then_inc(ready, 1)
                if t >= 1:
                    turn(t - 1)
                if t >= 2:
                    route(t - 2)
            route(T - 2)
            turn(T - 1)
            route(T - 1)

        @block.scalar
        def _(a):
            s = nc.scalar
            for t in range(T):
                x = G.h[:, t, :]
                a.wait_ge(summed_in, t + 1)
                s.activation(junk[:, 0, :], x, ACT.Copy, accum_out=total[:, t:t + 1]).then_inc(summed, 1)
                a.wait_ge(mean, t + 1)
                s.activation(junk[:, 1, :], x, ACT.Square, bias=total[:, t:t + 1],
                             accum_out=var[:, t:t + 1]).then_inc(squared, 1)
                a.wait_ge(var_ready, t + 1)
                s.activation(var[:, t:t + 1], var[:, t:t + 1], ACT.Sqrt).then_inc(rooted, 1)
                a.wait_ge(rstd_ready, t + 1)
                s.activation(x, x, ACT.Identity, bias=shift[:, t:t + 1], scale=var[:, t:t + 1]).then_inc(normed, 1)

        @block.vector
        def _(v):
            d = nc.vector
            st = Steps(v, dve)

            def take(t):
                v.wait_ge(turned, t + 1)
                d.tensor_copy(G.u[:, :, t * P:(t + 1) * P], tp[:]).then_inc(cols_ready, 1)

            v.wait_ge(vec_in, 32)
            for t in range(T):
                x, one = G.h[:, t, :], slice(t, t + 1)
                v.wait_ge(ready, t + 1)
                d.scalar_tensor_tensor(out=x, in0=x, scalar=ALPHA, in1=ps[:, t % 2, :],
                                       op0=ALU.mult, op1=ALU.add).then_inc(summed_in, 1)
                v.wait_ge(summed, t + 1)
                d.tensor_scalar(total[:, one], total[:, one], -1.0 / D, None, ALU.mult).then_inc(mean, 1)
                v.wait_ge(squared, t + 1)
                d.tensor_scalar(var[:, one], var[:, one], 1.0 / D, LN_EPS, ALU.mult, ALU.add).then_inc(var_ready, 1)
                v.wait_ge(rooted, t + 1)
                st(d.reciprocal(var[:, one], var[:, one]))
                st.join()
                d.tensor_tensor(shift[:, one], total[:, one], var[:, one], ALU.mult).then_inc(rstd_ready, 1)
                v.wait_ge(normed, t + 1)
                st(d.tensor_tensor(x, x, gain[:], ALU.mult))
                st.join()
                d.tensor_tensor(x, x, bias[:], ALU.add).then_inc(rows_ready, 1)
                if t:
                    take(t - 1)
            take(T - 1)
            v.wait_ge(routed, T)
            d.tensor_copy(logits, lps[:])


def layer_norm(nc, G, gain_d, bias_d, out_d):
    ph = phase(nc)
    with ph.ctx:
        gain = ph.sb("gain", [P, D])
        bias = ph.sb("bias", [P, D])
        junk = ph.sb("junk", [P, 2, D])
        total = ph.sb("total", [P, T])
        var = ph.sb("var", [P, T])
        shift = ph.sb("shift", [P, T])
        (vec_in, summed, mean, squared, var_ready, rooted, rstd_ready, dve, normed, rows_ready, stored) = ph.sems(
            "vec_in summed mean squared var_ready rooted rstd_ready dve normed rows_ready stored")
        block = ph.ctx.enter_context(nc.Block())

        @block.sync
        def _(sp):
            sp.dma_start(gain[:], gain_d.to_broadcast([P, D])).then_inc(vec_in, 16)
            sp.dma_start(bias[:], bias_d.to_broadcast([P, D])).then_inc(vec_in, 16)
            for t in range(T):
                sp.wait_ge(rows_ready, t + 1)
                sp.dma_start(out_d[t * P:(t + 1) * P, :], G.h[:, t, :]).then_inc(stored, 16)
            sp.wait_ge(stored, 16 * T)

        @block.scalar
        def _(a):
            s = nc.scalar

            def sums(t):
                if t:
                    a.wait_ge(summed, t)
                s.activation(junk[:, 0, :], G.h[:, t, :], ACT.Copy, accum_out=total[:, t:t + 1]).then_inc(summed, 1)

            def squares(t):
                a.wait_ge(mean, t + 1)
                if t:
                    a.wait_ge(squared, t)
                s.activation(junk[:, 1, :], G.h[:, t, :], ACT.Square, bias=total[:, t:t + 1],
                             accum_out=var[:, t:t + 1]).then_inc(squared, 1)

            sums(0)
            for t in range(T):
                if t + 1 < T:
                    sums(t + 1)
                squares(t)
                if t % 2 == 0:
                    continue
                a.wait_ge(var_ready, t // 2 + 1)
                s.activation(var[:, t - 1:t + 1], var[:, t - 1:t + 1], ACT.Sqrt).then_inc(rooted, 1)
                a.wait_ge(rstd_ready, t // 2 + 1)
                for n in (t - 1, t):
                    s.activation(G.h[:, n, :], G.h[:, n, :], ACT.Identity, bias=shift[:, n:n + 1],
                                 scale=var[:, n:n + 1]).then_inc(normed, 1)

        @block.vector
        def _(v):
            d = nc.vector
            st = Steps(v, dve)

            def finish(n):
                v.wait_ge(normed, n + 1)
                st(d.tensor_tensor(G.h[:, n, :], G.h[:, n, :], gain[:], ALU.mult))
                st.join()
                d.tensor_tensor(G.h[:, n, :], G.h[:, n, :], bias[:], ALU.add).then_inc(rows_ready, 1)

            v.wait_ge(vec_in, 32)
            for t in range(T):
                v.wait_ge(summed, t + 1)
                d.tensor_scalar(total[:, t:t + 1], total[:, t:t + 1], -1.0 / D, None, ALU.mult).then_inc(mean, 1)
                if t % 2 == 0:
                    if t:
                        finish(t - 2)
                    continue
                if t >= 3:
                    finish(t - 2)
                two = slice(t - 1, t + 1)
                v.wait_ge(squared, t + 1)
                d.tensor_scalar(var[:, two], var[:, two], 1.0 / D, LN_EPS, ALU.mult, ALU.add).then_inc(var_ready, 1)
                v.wait_ge(rooted, t // 2 + 1)
                st(d.reciprocal(var[:, two], var[:, two]))
                st.join()
                v.wait_ge(mean, t + 1)
                d.tensor_tensor(shift[:, two], total[:, two], var[:, two], ALU.mult).then_inc(rstd_ready, 1)
            finish(T - 2)
            finish(T - 1)


def route2(nc, A, G, scores):
    ph = phase(nc)
    PER = E2 // GROUPS2
    with ph.ctx:
        bias = ph.sb("bias", [P, E2])
        sel = ph.sb("sel", [P, T, E2])
        gtop = ph.sb("gtop", [P, T, GROUPS2, 8])
        gsum = ph.sb("gsum", [P, T, GROUPS2])
        best = ph.sb("best", [P, T, 8])
        bidx = ph.sb("bidx", [P, T, 8], U32)
        bnum = ph.sb("bnum", [P, T, TOPG2])
        hot = ph.sb("hot", [P, T, GROUPS2, TOPG2])
        pen = ph.sb("pen", [P, T, GROUPS2])
        etop = ph.sb("etop", [P, T, 8])
        eidx = ph.sb("eidx", [P, T, 8], U32)
        loaded, siged, dve = ph.sems("loaded siged dve")
        block = ph.ctx.enter_context(nc.Block())

        @block.sync
        def _(sp):
            sp.dma_start(bias[:], A["router_bias_2"].to_broadcast([P, E2])).then_inc(loaded, 16)

        @block.scalar
        def _(a):
            nc.scalar.activation(scores, scores, ACT.Sigmoid).then_inc(siged, 1)

        @block.vector
        def _(v):
            d = nc.vector
            st = Steps(v, dve)
            v.wait_ge(loaded, 16)
            v.wait_ge(siged, 1)
            st(d.tensor_tensor(sel[:], scores, bias[:, None, :].to_broadcast([P, T, E2]), ALU.add))
            st.join()
            for t in range(T):
                for g in range(GROUPS2):
                    st(d.max(gtop[:, t, g, :], sel[:, t, g * PER:(g + 1) * PER]))
            st.join()
            st(d.tensor_tensor(gsum[:], gtop[:, :, :, 0], gtop[:, :, :, 1], ALU.add))
            st.join()
            for t in range(T):
                st(d.max(best[:, t, :], gsum[:, t, :]))
            st.join()
            for t in range(T):
                st(d.max_index(bidx[:, t, :], best[:, t, :], gsum[:, t, :]))
            st.join()
            st(d.tensor_copy(bnum[:], bidx[:, :, 0:TOPG2]))
            st.join()
            st(d.tensor_tensor(hot[:], G.iota[:, None, 0:GROUPS2, None].to_broadcast([P, T, GROUPS2, TOPG2]),
                               bnum[:, :, None, :].to_broadcast([P, T, GROUPS2, TOPG2]), ALU.is_equal))
            st.join()
            st(d.tensor_reduce(pen[:], hot[:], AX, ALU.add))
            st.join()
            st(d.tensor_scalar(pen[:], pen[:], -1.0, -NEG, ALU.add, ALU.mult))
            st.join()
            st(d.tensor_tensor(sel[:].rearrange("p t (g e) -> p t g e", g=GROUPS2),
                               sel[:].rearrange("p t (g e) -> p t g e", g=GROUPS2),
                               pen[:, :, :, None].to_broadcast([P, T, GROUPS2, PER]), ALU.add))
            st.join()
            for t in range(T):
                st(d.max(etop[:, t, :], sel[:, t, :]))
            st.join()
            for t in range(T):
                st(d.max_index(eidx[:, t, :], etop[:, t, :], sel[:, t, :]))
            st.join()
            st(d.tensor_copy(G.e, eidx[:]))


def shared_and_combine(nc, A, G, cols, y_d):
    ph = phase(nc)
    K, R = K2, 4
    FC = F_EXP // P
    with ph.ctx:
        w_gu = ph.sb("w_gu", [P, 2, C, F_EXP])
        w_dn = ph.sb("w_dn", [P, FC, D])
        hid = ph.sb("hid", [P, FC, S])
        idx = ph.sb("idx", [P, T * K], I32)
        yr = ph.sb("yr", [P, R, D])
        gu_ps = ph.ps("gu_ps", [P, 2, 2, BANK])
        y_ps = ph.ps("y_ps", [P, 2, D])
        w_in, gu_ready, silu_done, hid_ready, y_ready, idx_ready, scaled, added = ph.sems(
            "w_in gu_ready silu_done hid_ready y_ready idx_ready scaled added")
        y_in = ph.sems(" ".join(f"y_in{r}" for r in range(R)))
        block = ph.ctx.enter_context(nc.Block())
        UNITS = [(f, half) for f in range(FC) for half in range(HALF)]
        order = []
        for t in range(T):
            order += [("row", t, k) for k in range(K)]
            if t < len(UNITS):
                order.append(("hid", t, 0))
            else:
                order.append(("out", t - len(UNITS), 0))
        order += [("out", t, 0) for t in range(T - len(UNITS), T)]
        adds = [x for x in order if x[0] != "hid"]
        add_no = {x: n for n, x in enumerate(adds)}

        @block.sync
        def _(sp):
            for i, name in enumerate(("ws_gate_2", "ws_up_2")):
                sp.dma_start(w_gu[:, i], A[name].rearrange("l (c p) n -> p (l c) n", p=P)).then_inc(w_in, 16)
            sp.dma_start(w_dn[:], A["ws_down_2"].rearrange("l (c p) n -> p (l c) n", p=P)).then_inc(w_in, 16)

        @block.gpsimd
        def _(pool):
            nc.gpsimd.tensor_copy(idx[:], G.slot.rearrange("p t k -> p (t k)")).then_inc(idx_ready, 1)
            pool.wait_ge(idx_ready, 1)
            for n in range(T * K):
                if n >= R:
                    pool.wait_ge(added, add_no["row", (n - R) // K, (n - R) % K] + 1)
                nc.gpsimd.indirect_dma_start(yr[:, n % R, :], None, y_d, bass.IndirectOffsetOnAxis(
                    ap=idx[:, n:n + 1], axis=0)).then_inc(y_in[n % R], 16)

        @block.tensor
        def _(pe):
            pe.wait_ge(w_in, 48)
            for n, (f, half) in enumerate(UNITS):
                if n >= 2:
                    pe.wait_ge(hid_ready, n - 1)
                for i in range(2):
                    for kc in range(C):
                        last = nc.tensor.matmul(gu_ps[:, n % 2, i, :], w_gu[:, i, kc, f * P:(f + 1) * P],
                                                cols[:, kc, half * BANK:(half + 1) * BANK],
                                                start=kc == 0, stop=kc == C - 1)
                last.then_inc(gu_ready, 1)
            pe.wait_ge(hid_ready, len(UNITS))
            for t in range(T):
                if t >= 2:
                    pe.wait_ge(added, add_no["out", t - 2, 0] + 1)
                for h in range(HALF):
                    for f in range(FC):
                        last = nc.tensor.matmul(y_ps[:, t % 2, h * BANK:(h + 1) * BANK], hid[:, f, t * P:(t + 1) * P],
                                                w_dn[:, f, h * BANK:(h + 1) * BANK], start=f == 0, stop=f == FC - 1)
                last.then_inc(y_ready, 1)

        @block.scalar
        def _(a):
            for t in range(T):
                nc.scalar.activation(G.h[:, t, :], G.h[:, t, :], ACT.Copy, scale=ALPHA).then_inc(scaled, 1)
            for n, (f, half) in enumerate(UNITS):
                a.wait_ge(gu_ready, n + 1)
                nc.scalar.activation(hid[:, f, half * BANK:(half + 1) * BANK], gu_ps[:, n % 2, 0, :], ACT.Silu
                                     ).then_inc(silu_done, 1)

        @block.vector
        def _(v):
            d = nc.vector
            for kind, n, k in order:
                if kind == "hid":
                    f, half = UNITS[n]
                    part = hid[:, f, half * BANK:(half + 1) * BANK]
                    v.wait_ge(silu_done, n + 1)
                    d.tensor_tensor(part, part, gu_ps[:, n % 2, 1, :], ALU.mult).then_inc(hid_ready, 1)
                    continue
                h = G.h[:, n, :]
                number = add_no[kind, n, k]
                if number:
                    v.wait_ge(added, number)
                if kind == "out":
                    v.wait_ge(y_ready, n + 1)
                    d.tensor_tensor(h, h, y_ps[:, n % 2, :], ALU.add).then_inc(added, 1)
                else:
                    if k == 0:
                        v.wait_ge(scaled, n + 1)
                    m = n * K + k
                    v.wait_ge(y_in[m % R], 16 * (m // R + 1))
                    d.scalar_tensor_tensor(out=h, in0=yr[:, m % R, :], scalar=G.w2[:, m:m + 1], in1=h,
                                           op0=ALU.mult, op1=ALU.add).then_inc(added, 1)


def program(nc, A, out):
    dram = lambda name, shape: nc.dram_tensor(name, shape, F32, kind="Internal").ap()
    qk_d = dram("qk_by_head", [2, HEADS, QK, S])
    v_d = dram("value_rows", [S, HEADS * VH])
    rows_d = dram("token_rows", [S, D])
    y_d = dram("expert_out", [(NB2 + 1) * P, D])
    with ExitStack() as ctx:
        G = persistent(nc, ctx)
        first = G.h
        second = ctx.enter_context(nc.sbuf_tensor("second", [P, T, D], F32))
        G.u, G.ya = second, first
        G.x_in = [nc.alloc_semaphore(f"x_in{t}") for t in range(T)]
        setup(nc, A, G)
        rms_to_cols(nc, G, vec(G, "norm_mix_g"), G.u)
        lru(nc, A, G, y_d)
        mla_project(nc, A, G, qk_d, v_d)
        with ExitStack() as moe:
            moe_state(nc, moe, G, K1, E1)
            with nc.sbuf_tensor("logits_1", [P, T, GROUPS1 + E1], F32) as logits:
                with nc.sbuf_tensor("yb", [P, C, S], F32) as yb:
                    G.yb = yb
                    G.x2 = second[:]
                    attention(nc, A, G, qk_d, v_d)
                    merge(nc, A, G, rows_d, logits[:])
                G.h, G.u = second, first
                route1(nc, A, G, logits[:])
                dispatch(nc, G, K1, E1, NB1)
            experts(nc, G, E1, NB1, rows_d, A["w_gate"], A["w_up"], A["w_down"], y_d[0:(NB1 + 1) * P, :])
            combine(nc, G, K1, y_d[0:NB1 * P, :])
        rows_to_cols(nc, G, G.h, G.u)
        with ExitStack() as moe:
            moe_state(nc, moe, G, K2, E2)
            with nc.sbuf_tensor("logits_2", [P, T, E2], F32) as scores:
                with nc.sbuf_tensor("mix", [P, C, S], F32) as mix:
                    G.mix = mix
                    hgrn(nc, A, G)
                    pooling(nc, A, G)
                    mix_out(nc, A, G, rows_d, scores[:])
                route2(nc, A, G, scores[:])
                dispatch(nc, G, K2, E2, NB2, scores[:])
            experts(nc, G, E2, NB2, rows_d, A["w_gate_2"], A["w_up_2"], A["w_down_2"], y_d)
            shared_and_combine(nc, A, G, G.u, y_d[0:NB2 * P, :])
        layer_norm(nc, G, A["ln2_g_2"], A["ln2_b_2"], out.rearrange("b s d -> (b s) d"))


def kernel(**inputs):
    import concourse.bacc as bacc
    from concourse.bass_utils import run_bass_kernel_spmd

    nc = bacc.Bacc("TRN2", target_bir_lowering=False, num_devices=1)
    arrays, aps = {}, {}
    for name, value in inputs.items():
        a = np.ascontiguousarray(value)
        arrays[f"in_{name}_dram"] = a
        aps[name] = nc.dram_tensor(f"in_{name}_dram", a.shape, mybir.dt.from_np(a.dtype), kind="ExternalInput").ap()
    out = nc.dram_tensor("out_dram", (1, S, D), F32, kind="ExternalOutput").ap()
    program(nc, aps, out)
    return run_bass_kernel_spmd(nc, [arrays], core_ids=[0]).results[0]["out_dram"]
```
